# Optimizing a Trainium2 kernel written in Bass

```python
import math
import jax, jax.numpy as jnp
from jax import lax
import numpy as np

D_MODEL = 1024
BATCH = 1
SEQ = 512
DEPTH = 2

GRID_W = 64
CTX_LEN = 256
Q_BLOCK = 128
EPS = 1e-6
ROPE_BASE = 10000.0

H_A = 8
Q_LORA = 384
KV_LORA = 256
NOPE_A = 64
ROPE_A = 32
V_A = 64

H_B = 4
DH_B = 64
V_B = 2 * DH_B

D_FF = 2816
CONV_W = 3

QKV_B = H_B * 2 * DH_B
IN_W = Q_LORA + KV_LORA + ROPE_A + 3 * QKV_B + 2 * D_MODEL


def rms_norm(x, g):
    xf = x.astype(jnp.float32)
    y = xf * lax.rsqrt(jnp.mean(xf * xf, axis=-1, keepdims=True) + EPS)
    return (y * g.astype(jnp.float32)).astype(x.dtype)

def modulate(h, shift, scale):
    return h * (1.0 + scale) + shift

def axial_rope_tables(rows, cols, dr, dtype):
    q = dr // 4
    freqs = ROPE_BASE ** (-jnp.arange(q, dtype=jnp.float32) / q)
    ang = jnp.concatenate([rows[:, None] * freqs, cols[:, None] * freqs], axis=-1)
    return jnp.cos(ang)[:, None, :].astype(dtype), jnp.sin(ang)[:, None, :].astype(dtype)

def apply_axial_rope(x, cos, sin):
    q = x.shape[-1] // 4
    xr1, xr2, xc1, xc2 = jnp.split(x, 4, axis=-1)
    cr, cc = cos[..., :q], cos[..., q:]
    sr, sc = sin[..., :q], sin[..., q:]
    return jnp.concatenate([xr1 * cr - xr2 * sr, xr1 * sr + xr2 * cr,
                            xc1 * cc - xc2 * sc, xc1 * sc + xc2 * cc], axis=-1)

def map_query_blocks(fn, qs):
    B, S = qs[0].shape[:2]
    nb = S // Q_BLOCK
    blk = tuple(q.reshape(B, nb, Q_BLOCK, *q.shape[2:]).swapaxes(0, 1) for q in qs)
    out = lax.map(lambda qb: fn(*qb), blk)
    return out.swapaxes(0, 1).reshape(B, S, *out.shape[3:])

def mla_attend(qn, qr, kn, kr, v):
    scale = (NOPE_A + ROPE_A) ** -0.5

    def one(qnb, qrb):
        s = (jnp.einsum('bqhd,bkhd->bhqk', qnb, kn) + jnp.einsum('bqhr,bkr->bhqk', qrb, kr)).astype(jnp.float32)
        p = jax.nn.softmax(s * scale, axis=-1).astype(v.dtype)
        return jnp.einsum('bhqk,bkhe->bqhe', p, v)

    return map_query_blocks(one, (qn, qr))

def diff_attend(q1, q2, k1, k2, v, lam):
    scale = DH_B ** -0.5

    def one(q1b, q2b):
        s1 = jnp.einsum('bqhd,bkhd->bhqk', q1b, k1).astype(jnp.float32) * scale
        s2 = jnp.einsum('bqhd,bkhd->bhqk', q2b, k2).astype(jnp.float32) * scale
        p = jax.nn.softmax(s1, axis=-1) - lam * jax.nn.softmax(s2, axis=-1)
        return jnp.einsum('bhqk,bkhe->bqhe', p.astype(v.dtype), v)

    return map_query_blocks(one, (q1, q2))

def mixer_inputs(h, p, rope_a, rope_b):
    B, S, _ = h.shape
    z = h @ p['w_in']
    cuts = np.cumsum([Q_LORA, KV_LORA, ROPE_A, QKV_B, QKV_B, QKV_B, D_MODEL]).tolist()
    c_q, c_kv, k_r, dq, dk, dv, ga, gb = jnp.split(z, cuts, axis=-1)
    q = (rms_norm(c_q, p['g_q']) @ p['w_uq']).reshape(B, S, H_A, NOPE_A + ROPE_A)
    qn, qr = q[..., :NOPE_A], q[..., NOPE_A:]
    kv = (rms_norm(c_kv, p['g_kv']) @ p['w_ukv']).reshape(B, S, H_A, NOPE_A + V_A)
    kn, va = kv[..., :NOPE_A], kv[..., NOPE_A:]
    kr = k_r[:, :, None, :]
    dq = dq.reshape(B, S, H_B, 2, DH_B)
    dk = dk.reshape(B, S, H_B, 2, DH_B)
    q1, q2 = dq[..., 0, :], dq[..., 1, :]
    k1, k2 = dk[..., 0, :], dk[..., 1, :]
    vb = dv.reshape(B, S, H_B, V_B)
    if rope_a is not None:
        qr = apply_axial_rope(qr, *rope_a)
        kr = apply_axial_rope(kr, *rope_a)
        q1, q2, k1, k2 = (apply_axial_rope(t, *rope_b) for t in (q1, q2, k1, k2))
    return {'qn': qn, 'qr': qr, 'kn': kn, 'kr': kr[:, :, 0, :], 'va': va,
            'q1': q1, 'q2': q2, 'k1': k1, 'k2': k2, 'vb': vb, 'ga': ga, 'gb': gb}

def mixer_outputs(o_a, o_b, ga, gb, p, lam_init):
    B, S = o_a.shape[:2]
    y_a = o_a.reshape(B, S, H_A * V_A) @ p['w_br_a']
    o_b = rms_norm(o_b, p['g_sub']) * (1.0 - lam_init)
    y_b = o_b.reshape(B, S, H_B * V_B) @ p['w_br_b']
    merged = jax.nn.sigmoid(ga) * y_a + jax.nn.sigmoid(gb) * y_b
    return merged @ p['w_out']

def conv_ffn(h, p):
    u = h @ p['w_up']
    C = u.shape[-1]
    u = lax.conv_general_dilated(u, p['conv_w'][:, None, :], window_strides=(1,),
                                 padding=((CONV_W // 2, CONV_W // 2),),
                                 dimension_numbers=('NWC', 'WIO', 'NWC'),
                                 feature_group_count=C) + p['conv_b']
    a, b = jnp.split(u, 2, axis=-1)
    return (jax.nn.silu(a) * b) @ p['w_down']

def first_inputs(seed: int = 0) -> dict:
    key = jax.random.key(seed)
    ks = jax.random.split(key, 32)
    L, D, F = DEPTH, D_MODEL, D_FF

    def nrm(k, shape, scale):
        return jax.random.normal(k, shape, jnp.float32) * scale

    def gain(k, shape):
        return 1.0 + 0.02 * jax.random.normal(k, shape, jnp.float32)

    return {
        'x': nrm(ks[0], (BATCH, SEQ, D), 1.0),
        'c': nrm(ks[1], (BATCH, D), 1.0),
        'ctx': nrm(ks[2], (BATCH, CTX_LEN, D), 1.0),
        'c_ctx': nrm(ks[3], (D,), 1.0),
        'w_ada': nrm(ks[4], (L, D, 6 * D), 0.5 * D ** -0.5),
        'b_ada': nrm(ks[5], (L, 6 * D), 0.01),
        'g_mix': gain(ks[6], (L, D)),
        'g_ffn': gain(ks[7], (L, D)),
        'w_in': nrm(ks[8], (L, D, IN_W), D ** -0.5),
        'g_q': gain(ks[9], (L, Q_LORA)),
        'w_uq': nrm(ks[10], (L, Q_LORA, H_A * (NOPE_A + ROPE_A)), Q_LORA ** -0.5),
        'g_kv': gain(ks[11], (L, KV_LORA)),
        'w_ukv': nrm(ks[12], (L, KV_LORA, H_A * (NOPE_A + V_A)), KV_LORA ** -0.5),
        'lam_q1': nrm(ks[13], (L, DH_B), 0.1),
        'lam_k1': nrm(ks[14], (L, DH_B), 0.1),
        'lam_q2': nrm(ks[15], (L, DH_B), 0.1),
        'lam_k2': nrm(ks[16], (L, DH_B), 0.1),
        'g_sub': gain(ks[17], (L, V_B)),
        'w_br_a': nrm(ks[18], (L, H_A * V_A, D), (H_A * V_A) ** -0.5),
        'w_br_b': nrm(ks[19], (L, H_B * V_B, D), (H_B * V_B) ** -0.5),
        'w_out': nrm(ks[20], (L, D, D), D ** -0.5),
        'w_up': nrm(ks[21], (L, D, 2 * F), D ** -0.5),
        'conv_w': nrm(ks[22], (L, CONV_W, 2 * F), CONV_W ** -0.5),
        'conv_b': nrm(ks[23], (L, 2 * F), 0.01),
        'w_down': nrm(ks[24], (L, F, D), F ** -0.5),
        'g_final': gain(ks[25], (D,)),
    }

def first_block(x, c, ctx, c_ctx, w_ada, b_ada, g_mix, g_ffn, w_in, g_q, w_uq, g_kv, w_ukv,
              lam_q1, lam_k1, lam_q2, lam_k2, g_sub, w_br_a, w_br_b, w_out,
              w_up, conv_w, conv_b, w_down, g_final):
    B, S, D = x.shape
    ROWS = S // GRID_W
    rows = jnp.repeat(jnp.arange(ROWS), GRID_W).astype(jnp.float32)
    cols = jnp.tile(jnp.arange(GRID_W), ROWS).astype(jnp.float32)
    rope_a = axial_rope_tables(rows, cols, ROPE_A, x.dtype)
    rope_b = axial_rope_tables(rows, cols, DH_B, x.dtype)

    x_lat, x_ctx = x, ctx
    for l in range(DEPTH):
        last = l == DEPTH - 1
        p = {'w_in': w_in[l], 'g_q': g_q[l], 'w_uq': w_uq[l], 'g_kv': g_kv[l], 'w_ukv': w_ukv[l],
             'g_sub': g_sub[l], 'w_br_a': w_br_a[l], 'w_br_b': w_br_b[l], 'w_out': w_out[l],
             'w_up': w_up[l], 'conv_w': conv_w[l], 'conv_b': conv_b[l], 'w_down': w_down[l]}
        lam_init = 0.8 - 0.6 * math.exp(-0.3 * l)
        lam = (jnp.exp(jnp.sum(lam_q1[l].astype(jnp.float32) * lam_k1[l].astype(jnp.float32)))
               - jnp.exp(jnp.sum(lam_q2[l].astype(jnp.float32) * lam_k2[l].astype(jnp.float32)))
               + lam_init)

        mod_lat = (jax.nn.silu(c) @ w_ada[l] + b_ada[l])[:, None, :]
        mod_ctx = jax.nn.silu(c_ctx) @ w_ada[l] + b_ada[l]
        sh1, sc1, gt1, sh2, sc2, gt2 = jnp.split(mod_lat, 6, axis=-1)
        csh1, csc1, cgt1, csh2, csc2, cgt2 = jnp.split(mod_ctx, 6, axis=-1)

        h_lat = modulate(rms_norm(x_lat, g_mix[l]), sh1, sc1)
        h_ctx = modulate(rms_norm(x_ctx, g_mix[l]), csh1, csc1)
        pl = mixer_inputs(h_lat, p, rope_a, rope_b)
        pc = mixer_inputs(h_ctx, p, None, None)
        cat = lambda name: jnp.concatenate([pc[name], pl[name]], axis=1)
        o_a = mla_attend(pl['qn'], pl['qr'], cat('kn'), cat('kr'), cat('va'))
        o_b = diff_attend(pl['q1'], pl['q2'], cat('k1'), cat('k2'), cat('vb'), lam)
        o_lat = mixer_outputs(o_a, o_b, pl['ga'], pl['gb'], p, lam_init)
        if not last:
            oc_a = mla_attend(pc['qn'], pc['qr'], pc['kn'], pc['kr'], pc['va'])
            oc_b = diff_attend(pc['q1'], pc['q2'], pc['k1'], pc['k2'], pc['vb'], lam)
            o_ctx = mixer_outputs(oc_a, oc_b, pc['ga'], pc['gb'], p, lam_init)
            x_ctx = x_ctx + cgt1 * o_ctx
        x_lat = x_lat + gt1 * o_lat

        h_lat = modulate(rms_norm(x_lat, g_ffn[l]), sh2, sc2)
        x_lat = x_lat + gt2 * conv_ffn(h_lat, p)
        if not last:
            h_ctx = modulate(rms_norm(x_ctx, g_ffn[l]), csh2, csc2)
            x_ctx = x_ctx + cgt2 * conv_ffn(h_ctx, p)

    return rms_norm(x_lat, g_final)


A_HEADS = 8
HEAD_DIM = 64
A_WIDTH = A_HEADS * HEAD_DIM
IDX_HEADS = 4
IDX_DIM = 64
TOPK_MAX = 256
ATTN_SCALE = HEAD_DIM ** -0.5
IDX_SCALE = (IDX_DIM ** -0.5) * (IDX_HEADS ** -0.5)

ROPE_THETA = 500000.0
ROT_DIM = HEAD_DIM // 4

B_HEADS = 4
B_DK = 32
B_DV = 64
B_KWIDTH = B_HEADS * B_DK
B_VWIDTH = B_HEADS * B_DV
GATE_RANK = 16
GATE_TAU = 16.0
CHUNK = 64

POOL_WINDOWS = (2, 4, 8, 16)
C_GROUPS = 4
C_GROUP_DIM = 64
C_WIDTH = C_GROUPS * C_GROUP_DIM

MIX_WIDTH = A_WIDTH + B_VWIDTH + C_WIDTH

SPLIT_SIZES = (
    A_WIDTH, A_WIDTH, A_WIDTH,
    IDX_HEADS * IDX_DIM, IDX_DIM, IDX_HEADS,
    B_KWIDTH, B_KWIDTH, B_VWIDTH, B_VWIDTH,
    GATE_RANK,
    C_WIDTH,
)
IN_WIDTH = sum(SPLIT_SIZES)

CONV_WIDTH = 3


def rms_norm_2(x, g):
    xf = x.astype(jnp.float32)
    y = xf * lax.rsqrt(jnp.mean(xf * xf, axis=-1, keepdims=True) + EPS)
    return (y * g.astype(jnp.float32)).astype(x.dtype)

def rope_tables(positions):
    inv = ROPE_THETA ** (-jnp.arange(0, ROT_DIM, 2, dtype=jnp.float32) / ROT_DIM)
    ang = positions.astype(jnp.float32)[..., None] * inv
    return jnp.cos(ang), jnp.sin(ang)

def partial_rope(x, cos, sin):
    half = ROT_DIM // 2
    x1 = x[..., :half].astype(jnp.float32)
    x2 = x[..., half:ROT_DIM].astype(jnp.float32)
    c = cos[:, :, None, :]
    s = sin[:, :, None, :]
    rot = jnp.concatenate([x1 * c - x2 * s, x2 * c + x1 * s], axis=-1).astype(x.dtype)
    return jnp.concatenate([rot, x[..., ROT_DIM:]], axis=-1)

def split_cols(p):
    outs = []
    off = 0
    for n in SPLIT_SIZES:
        outs.append(p[..., off:off + n])
        off += n
    return outs

def dsa_attention(q, k, v, qi, ki, wi):
    nbat, S, H, Dh = q.shape
    n_keep = min(TOPK_MAX, S // 4)
    nb = S // Q_BLOCK
    key_pos = jnp.arange(S)
    ki_f = ki.astype(jnp.float32)

    def to_blocks(a):
        return a.reshape(nbat, nb, Q_BLOCK, *a.shape[2:]).swapaxes(0, 1)

    def block(args):
        qb, qib, wib, qpos = args
        logits = jnp.einsum('bqhd,bsd->bqhs', qib.astype(jnp.float32), ki_f)
        score = jnp.einsum('bqh,bqhs->bqs', wib.astype(jnp.float32), jax.nn.relu(logits)) * IDX_SCALE
        causal = key_pos[None, :] <= qpos[:, None]
        score = jnp.where(causal[None], score, -jnp.inf)
        _, idx = lax.top_k(score, n_keep)
        valid = idx <= qpos[None, :, None]
        kg = jax.vmap(lambda kk, ii: kk[ii])(k, idx)
        vg = jax.vmap(lambda vv, ii: vv[ii])(v, idx)
        s = jnp.einsum('bqhd,bqkhd->bhqk', qb.astype(jnp.float32), kg.astype(jnp.float32)) * ATTN_SCALE
        s = jnp.where(valid[:, None], s, -jnp.inf)
        p = jax.nn.softmax(s, axis=-1)
        o = jnp.einsum('bhqk,bqkhd->bqhd', p, vg.astype(jnp.float32))
        return o.astype(q.dtype)

    qpos_blocks = jnp.arange(S).reshape(nb, Q_BLOCK)
    out = lax.map(block, (to_blocks(q), to_blocks(qi), to_blocks(wi), qpos_blocks))
    return out.swapaxes(0, 1).reshape(nbat, S, H, Dh)

def gla_chunked(q, k, v, log_a):
    nbat, S, H, DK = q.shape
    DV = v.shape[-1]
    nc = S // CHUNK

    def chunks(a):
        return a.astype(jnp.float32).reshape(nbat, nc, CHUNK, H, a.shape[-1]).transpose(1, 0, 3, 2, 4)

    qc = chunks(q * (DK ** -0.5))
    kc, vc, gc = chunks(k), chunks(v), chunks(log_a)
    tri = jnp.tril(jnp.ones((CHUNK, CHUNK), dtype=bool))

    def step(state, inp):
        qq, kk, vv, gg = inp
        b = jnp.cumsum(gg, axis=2)
        o_inter = jnp.einsum('bhcd,bhde->bhce', qq * jnp.exp(b), state)
        diff = b[:, :, :, None, :] - b[:, :, None, :, :]
        decay = jnp.exp(jnp.where(tri[:, :, None], diff, -jnp.inf))
        att = jnp.einsum('bhid,bhjd,bhijd->bhij', qq, kk, decay)
        o_intra = jnp.einsum('bhij,bhje->bhie', att, vv)
        b_last = b[:, :, -1:, :]
        new_state = state * jnp.exp(b_last[:, :, 0, :, None]) + jnp.einsum(
            'bhcd,bhce->bhde', kk * jnp.exp(b_last - b), vv)
        return new_state, o_inter + o_intra

    state0 = jnp.zeros((nbat, H, DK, DV), jnp.float32)
    _, o = lax.scan(step, state0, (qc, kc, vc, gc))
    return o.transpose(1, 0, 3, 2, 4).reshape(nbat, S, H, DV)

def multiscale_pool(u, w_pool, pool_scale):
    nbat, S, _ = u.shape
    uf = u.astype(jnp.float32).reshape(nbat, S, C_GROUPS, C_GROUP_DIM)
    cs = jnp.concatenate([jnp.zeros((nbat, 1, C_GROUPS, C_GROUP_DIM), jnp.float32),
                          jnp.cumsum(uf, axis=1)], axis=1)
    pos = jnp.arange(S)
    win = jnp.array(POOL_WINDOWS, dtype=jnp.int32)
    lo_idx = jnp.maximum(pos[:, None] + 1 - win[None, :], 0)
    lo = cs[:, lo_idx, jnp.arange(C_GROUPS)[None, :]]
    cnt = jnp.minimum(pos[:, None] + 1, win[None, :]).astype(jnp.float32)
    pooled = (cs[:, 1:] - lo) / cnt[None, :, :, None] - uf
    y = jnp.einsum('bsgd,gde->bsge', pooled, w_pool.astype(jnp.float32))
    y = y * pool_scale.astype(jnp.float32).reshape(C_GROUPS, C_GROUP_DIM)
    return y.reshape(nbat, S, C_WIDTH).astype(u.dtype)

def conv_glu_ffn(x, w_up, conv_w, conv_b, w_down):
    S = x.shape[1]
    h = x @ w_up
    a, b = h[..., :D_FF], h[..., D_FF:]
    ap = jnp.pad(a, ((0, 0), (CONV_WIDTH - 1, 0), (0, 0)))
    conv = conv_b + ap[:, 0:S] * conv_w[0]
    for j in range(1, CONV_WIDTH):
        conv = conv + ap[:, j:j + S] * conv_w[j]
    return (jax.nn.silu(conv) * b) @ w_down

def hybrid_layer(x, cos, sin, norm1_g, w_in, w_gate_up, b_gate, gla_norm_g, w_pool, pool_scale,
                 w_out, norm2_g, w_up, conv_w, conv_b, w_down):
    nbat, S, _ = x.shape
    h = rms_norm_2(x, norm1_g)
    proj = h @ w_in
    (qa, ka, va, qi, ki, wi, qb, kb, vb, rb, gl, uc) = split_cols(proj)

    qa = partial_rope(qa.reshape(nbat, S, A_HEADS, HEAD_DIM), cos, sin)
    ka = partial_rope(ka.reshape(nbat, S, A_HEADS, HEAD_DIM), cos, sin)
    va = va.reshape(nbat, S, A_HEADS, HEAD_DIM)
    qi = partial_rope(qi.reshape(nbat, S, IDX_HEADS, IDX_DIM), cos, sin)
    ki = partial_rope(ki[:, :, None, :], cos, sin)[:, :, 0, :]
    o_a = dsa_attention(qa, ka, va, qi, ki, wi).reshape(nbat, S, A_WIDTH)

    z = (gl @ w_gate_up + b_gate).astype(jnp.float32)
    log_a = (jax.nn.log_sigmoid(z) / GATE_TAU).reshape(nbat, S, B_HEADS, B_DK)
    o_b = gla_chunked(qb.reshape(nbat, S, B_HEADS, B_DK), kb.reshape(nbat, S, B_HEADS, B_DK),
                      vb.reshape(nbat, S, B_HEADS, B_DV), log_a)
    o_b = rms_norm_2(o_b, gla_norm_g).reshape(nbat, S, B_VWIDTH)
    o_b = (o_b * jax.nn.silu(rb.astype(jnp.float32))).astype(x.dtype)

    o_c = multiscale_pool(uc, w_pool, pool_scale)

    mix = jnp.concatenate([o_a.astype(x.dtype), o_b, o_c], axis=-1) @ w_out
    x = x + mix
    x = x + conv_glu_ffn(rms_norm_2(x, norm2_g), w_up, conv_w, conv_b, w_down)
    return x

def second_inputs(seed: int = 0) -> dict:
    key = jax.random.key(seed)
    ks = jax.random.split(key, 16)
    f32 = jnp.float32
    nrm = lambda k, shape, s: jax.random.normal(k, shape, f32) * s
    return {
        "x": jax.random.normal(ks[0], (BATCH, SEQ, D_MODEL), f32),
        "positions": jnp.broadcast_to(jnp.arange(SEQ, dtype=jnp.int32)[None, :], (BATCH, SEQ)),
        "norm1_g": 1.0 + nrm(ks[1], (DEPTH, D_MODEL), 0.02),
        "w_in": nrm(ks[2], (DEPTH, D_MODEL, IN_WIDTH), D_MODEL ** -0.5),
        "w_gate_up": nrm(ks[3], (DEPTH, GATE_RANK, B_KWIDTH), GATE_RANK ** -0.5),
        "b_gate": nrm(ks[4], (DEPTH, B_KWIDTH), 0.01),
        "gla_norm_g": 1.0 + nrm(ks[5], (DEPTH, B_HEADS, B_DV), 0.02),
        "w_pool": nrm(ks[6], (DEPTH, C_GROUPS, C_GROUP_DIM, C_GROUP_DIM), C_GROUP_DIM ** -0.5),
        "pool_scale": 1.0 + nrm(ks[7], (DEPTH, C_WIDTH), 0.1),
        "w_out": nrm(ks[8], (DEPTH, MIX_WIDTH, D_MODEL), MIX_WIDTH ** -0.5),
        "norm2_g": 1.0 + nrm(ks[9], (DEPTH, D_MODEL), 0.02),
        "w_up": nrm(ks[10], (DEPTH, D_MODEL, 2 * D_FF), D_MODEL ** -0.5),
        "conv_w": nrm(ks[11], (DEPTH, CONV_WIDTH, D_FF), CONV_WIDTH ** -0.5),
        "conv_b": nrm(ks[12], (DEPTH, D_FF), 0.01),
        "w_down": nrm(ks[13], (DEPTH, D_FF, D_MODEL), D_FF ** -0.5),
        "final_norm_g": 1.0 + nrm(ks[14], (D_MODEL,), 0.02),
    }

def second_block(x, positions, norm1_g, w_in, w_gate_up, b_gate, gla_norm_g, w_pool, pool_scale,
              w_out, norm2_g, w_up, conv_w, conv_b, w_down, final_norm_g):
    cos, sin = rope_tables(positions)
    for l in range(DEPTH):
        x = hybrid_layer(x, cos, sin, norm1_g[l], w_in[l], w_gate_up[l], b_gate[l], gla_norm_g[l],
                         w_pool[l], pool_scale[l], w_out[l], norm2_g[l], w_up[l], conv_w[l],
                         conv_b[l], w_down[l])
    return rms_norm_2(x, final_norm_g)


def setup_inputs(seed=0):
    out = dict(first_inputs(seed))
    for name, value in second_inputs(seed + 1).items():
        if name != "x":
            out[name + "_2"] = value
    return out


def reference(
    x, c, ctx, c_ctx, w_ada, b_ada, g_mix, g_ffn, w_in, g_q, w_uq, g_kv, w_ukv, lam_q1, lam_k1,
    lam_q2, lam_k2, g_sub, w_br_a, w_br_b, w_out, w_up, conv_w, conv_b, w_down, g_final,
    positions_2, norm1_g_2, w_in_2, w_gate_up_2, b_gate_2, gla_norm_g_2, w_pool_2, pool_scale_2,
    w_out_2, norm2_g_2, w_up_2, conv_w_2, conv_b_2, w_down_2, final_norm_g_2,
):
    x = first_block(
        x, c, ctx, c_ctx, w_ada, b_ada, g_mix, g_ffn, w_in, g_q, w_uq, g_kv, w_ukv, lam_q1,
        lam_k1, lam_q2, lam_k2, g_sub, w_br_a, w_br_b, w_out, w_up, conv_w, conv_b, w_down,
        g_final,
    )
    return second_block(
        x, positions_2, norm1_g_2, w_in_2, w_gate_up_2, b_gate_2, gla_norm_g_2, w_pool_2,
        pool_scale_2, w_out_2, norm2_g_2, w_up_2, conv_w_2, conv_b_2, w_down_2, final_norm_g_2,
    )


_drawn_inputs = setup_inputs


def setup_inputs(seed=0):
    import zlib

    import numpy as np

    out = dict(_drawn_inputs(seed))
    spreads = {}
    factors = {'g_mix': 5.568,
     'g_ffn': 3.047,
     'g_q': 8.0,
     'g_kv': 8.0,
     'lam_q1': 4.593,
     'lam_k1': 4.801,
     'lam_q2': 4.577,
     'lam_k2': 5.167,
     'g_sub': 4.843,
     'conv_b': 4.653,
     'b_gate_2': 8.0,
     'gla_norm_g_2': 5.886,
     'norm2_g_2': 2.749,
     'conv_b_2': 6.677,
     'final_norm_g_2': 2.842}
    for name, (base, spread) in spreads.items():
        noise = np.random.default_rng([zlib.crc32(name.encode()), seed]).standard_normal(out[name].shape)
        drawn = base * np.exp(spread * noise) if base else spread * noise
        out[name] = __import__('jax').numpy.asarray(drawn.astype(out[name].dtype))
    for name, factor in factors.items():
        out[name] = (out[name] * factor).astype(out[name].dtype)
    return out
```

```python
import math

import numpy as np
import concourse.bass as bass
import concourse.mybir as mybir
from concourse.alu_op_type import AluOpType as ALU

P = 128
D = 1024
DC = D // P
CTX, SEQ = 256, 512
TOK = CTX + SEQ
LAYERS = 2
EPS = 1e-6

H_A, NOPE, ROPE_A, V_A = 8, 64, 32, 64
QK_A = NOPE + ROPE_A
Q_LORA, KV_LORA = 384, 256
H_B, DH_B = 4, 64
F = 2816
FC = F // P
GRID_W = 64
ROPE_BASE = 10000.0
MODS = 6 * DC

HEADS, HD = 8, 64
IDX_HEADS = 4
TOPK = min(256, SEQ // 4)
IDX_SCALE = (HD ** -0.5) * (IDX_HEADS ** -0.5)
ROPE_THETA, ROT = 500000.0, 16
GLA_HEADS, DK, DV = 4, 32, 64
GATE_RANK, GATE_TAU = 16, 16.0
POOL_WINDOWS = (2, 4, 8, 16)
PAD = max(POOL_WINDOWS)
QT = SEQ // P

NORM_BANK = 7
TILE_COLS = P
SLAB_TILES = 8
SLAB = SLAB_TILES * TILE_COLS
RAW_SLOTS, SPLIT_SLOTS = 4, 2
ACC_BANKS = 4
NEG = -1e30
TAKEN = -3e38
BANK = 512

F32, F32R, I32 = mybir.dt.float32, mybir.dt.float32r, mybir.dt.int32
ACT = mybir.ActivationFunctionType
AX = mybir.AxisListType


def lam_init(l):
    return 0.8 - 0.6 * math.exp(-0.3 * l)


def param_columns():
    at, n = {}, 0
    for name, width in (
        [(f"{name}{l}", w) for l in range(LAYERS) for name, w in (
            ("b_ada", MODS), ("g_mix", 2 * DC), ("g_ffn", 2 * DC), ("conv_w", 3 * 2 * FC), ("conv_b", 2 * FC),
            ("g_q", Q_LORA // P), ("g_kv", KV_LORA // P), ("g_sub", 1), ("lam", 4))]
        + [("g_final", DC)]
        + [(f"{name}{l}", w) for l in range(LAYERS) for name, w in (
            ("norm1", DC), ("norm2", DC), ("conv_w_2", 3 * FC), ("conv_b_2", FC), ("b_gate", 1), ("gla_g", 2),
            ("pool_scale", 2), ("w_gate", P), ("w_pool", 2 * P))]
        + [("final_g", DC), ("ident", P), ("ones", P), ("headsum", P), ("perm_a", P), ("perm_b", P),
           ("perm_2", P), ("tril", P), ("above", P), ("gla_mask", 3 * P), ("inv_freq", 1), ("zero", 1)]):
        at[name] = (n, width)
        n += width
    return at, n


COLS, NCOLS = param_columns()

LORA_SLABS, UP_A_SLABS = 6, H_A // 2 + 1 + 1
DIFF_SLABS = 12
MERGE_SLABS, OUT_SLABS = 3 * DC, DC
FFN_SLABS = 2 * FC + 3 * DC
IN2_SLABS = 18 + 4 + 2 + 1
USED_SLABS = (LAYERS * (LORA_SLABS + UP_A_SLABS + DIFF_SLABS + MERGE_SLABS + OUT_SLABS + FFN_SLABS)
              + FFN_SLABS + LAYERS * (IN2_SLABS + OUT_SLABS + FFN_SLABS))
N_SLABS = -(-USED_SLABS // RAW_SLOTS) * RAW_SLOTS
ADA_GROUPS = (2 * DC, MODS - 2 * DC, MODS)
ADA_SLOTS = (4, 3, 4)
ADA_PER_SLAB, ADA_PER_OUT = 4, MODS // DC
DIFF_AT = LORA_SLABS + UP_A_SLABS
DOWN_AT = DIFF_AT + DIFF_SLABS + MERGE_SLABS + OUT_SLABS + 2 * FC


def ada_loads(group, slot):
    return sum(len(range(slot, n, slots)) for n, slots in zip(ADA_GROUPS[:group], ADA_SLOTS) if slot < slots)


class Count:

    def __init__(self, n=0):
        self.n, self.i, self.per = n, None, 0

    def add(self, k=1):
        self.n += k
        return self

    def now(self, back=0, times=1):
        v = (self.n - back) * times
        return v if self.i is None else self.i * (self.per * times) + v

    def enter(self, i, per):
        self.i, self.per, self.start = i, per, self.n

    def leave(self, turns):
        assert self.n == self.start + self.per, (self.n, self.start, self.per)
        self.i, self.n = None, self.start + self.per * turns


class Loop:

    def __init__(self, eng, turns, *counts):
        self.fori, self.turns, self.counts = eng.Fori(0, turns), turns, counts

    def __enter__(self):
        i = self.fori.__enter__()
        for c, per in self.counts:
            c.enter(i, per)
        return i

    def __exit__(self, *e):
        self.fori.__exit__(*e)
        for c, _ in self.counts:
            c.leave(self.turns)


def groups_of(l):
    return [(0, CTX), (CTX, SEQ)] if l == 0 else [(CTX, SEQ)]


BOTH = [(0, CTX), (CTX, SEQ)]
LAT = [(CTX, SEQ)]


def roped(tiles):
    events, pending = [], None
    for name, groups, rope in tiles:
        events += [("gemm", name, g) for g in groups]
        if pending is not None:
            events.append(("rot", pending, None))
        pending = name if rope else None
    if pending is not None:
        events.append(("rot", pending, None))
    return events


def lora_events(l):
    return roped([(("cq", m), groups_of(l), False) for m in range(3)]
                 + [(("ckv", m), BOTH, False) for m in range(2)] + [("kr", BOTH, True)])


def up_events(l):
    return (roped([(("q", h), groups_of(l), True) for h in range(H_A)])
            + [("gemm", ("kn", j), g) for j in range(H_A // 2) for g in BOTH])


def diff_events(l):
    return roped([(("dq", m), groups_of(l), True) for m in range(H_B)]
                 + [(("dk", m), BOTH, True) for m in range(H_B)])


IN2_TILES = ([(("qa", m), LAT, True) for m in range(4)] + [(("ka", m), LAT, True) for m in range(4)]
             + [(("qi", m), LAT, True) for m in range(2)] + [("ki", LAT, True)]
             + [("qb", LAT, False), ("kb", LAT, False)] + [(("rb", m), LAT, False) for m in range(2)]
             + [(("uc", m), LAT, False) for m in range(2)] + [("gl", LAT, False)])
IN2_EVENTS = roped(IN2_TILES)


def items_a(l, heads):
    return [(h, CTX + P * t, TOK) for h in range(heads) for t in range(QT)] + (
        [(h, P * t, CTX) for h in range(heads) for t in range(CTX // P)] if l == 0 else [])


ITEMS_2 = [(h, t) for t in range(QT) for h in range(HEADS)]


def build(nc, wstream, ada_w, c_in, params, x_in, rope_tab, pos_in, cnt_in, out, stop=None):
    from contextlib import ExitStack

    ctx = ExitStack()
    with ctx:
        top = [16512]

        def sb(name, shape, dt=F32, at=None):
            n = 4 * int(np.prod(shape[1:]))
            n = -(-n // 32) * 32
            if at is None:
                at = top[0]
                top[0] += n
            assert at + n <= 229344, (name, at + n)
            return nc.alloc_sbuf_tensor_at(name, shape, dt, offset=at)

        raw = sb("raw", [P, RAW_SLOTS, SLAB])
        split = sb("split", [P, SPLIT_SLOTS, 2, SLAB], F32R)
        x = sb("x", [P, DC, TOK])
        par = sb("par", [P, NCOLS])
        mod = sb("mod", [P, LAYERS, MODS, 2])
        gain = sb("gain", [P, 2, DC, 2])
        lam_p = sb("lam_p", [P, LAYERS, 2])
        lam_e = sb("lam_e", [P, LAYERS, 2])
        neg_lam = sb("neg_lam", [P, LAYERS])
        ms = sb("ms", [P, 24])
        rstd = sb("rstd", [P, 24])
        newton = sb("newton", [P, 24])
        gsub = sb("gsub", [P, 1])
        stat = sb("stat", [P, 2, 8])
        PH = top[0]
        KB = 1024

        def ph(name, kb, shape, dt=F32):
            return sb(name, shape, dt, at=PH + int(kb * KB))

        ada_c = [ph(f"ada_c{i}", a, [P, 2, D]) for i, a in enumerate((0, 48 + 81, 0))]
        ada_t = [[ph(f"ada_t{i}{j}", a + 4 * j, [P, D]) for j in range(ADA_SLOTS[i])]
                 for i, a in enumerate((8, 48 + 63, 8))]
        h_hl = ph("h_hl", 0, [P, 2, DC, TOK], F32R)
        M = 48
        qA = ph("qA", M, [P, H_A, TOK])
        cq = ph("cq", M + 24, [P, 3, TOK])
        cq_hl = ph("cq_hl", M + 33, [P, 2, 3, TOK], F32R)
        kA = ph("kA", M + 24, [P, H_A, TOK])
        vA = ph("vA", M + 51, [P, TOK // P, H_A * V_A])
        ckv_hl = ph("ckv_hl", M + 63, [P, 2, 2, TOK], F32R)
        oA = ph("oA", M + 63, [P, 4, TOK])
        ckv = ph("ckv", M + 75, [P, 2, TOK])
        ropeA = ph("ropeA", M + 81, [P, 2, SEQ])
        kr = ph("kr", M + 85, [P, TOK])
        rot = [ph(f"rot{i}", a, [P, SEQ]) for i, a in ((0, M + 51), (1, M + 88))]
        pA = [ph(f"pA{i}", M + 75 + 3 * i, [P, TOK]) for i in range(2)]
        pT = ph("pT", M + 87, [P, TOK])
        oA_hl = ph("oA_hl", M, [P, 2, 4, TOK], F32R)
        dq = ph("dq", M + 24, [P, H_B, TOK])
        dk = ph("dk", M + 36, [P, H_B, TOK])
        ropeB = ph("ropeB", M + 75, [P, 2, SEQ])
        rotB = [ph(f"rotB{i}", a, [P, SEQ]) for i, a in ((0, M + 79), (1, M + 60))]
        vB = ph("vB", M + 48, [P, TOK // P, H_B * P])
        oB = ph("oB", M + 63, [P, H_B, TOK])
        pB = [ph(f"pB{i}", M + 75 + 3 * i, [P, TOK]) for i in range(4)]
        sumB = [ph(f"sumB{i}", M + 48 + 3 * i, [P, TOK]) for i in range(H_B)]
        unB = [ph(f"unB{i}", M + 81 + 3 * i, [P, TOK]) for i in range(2)]
        oB_hl = ph("oB_hl", M + 24, [P, 2, 4, TOK], F32R)
        merged = ph("merged", M + 48, [P, DC, TOK])
        mg = ph("mg", M + 72, [P, 4, TOK])
        m_hl = ph("m_hl", 0, [P, 2, DC, TOK], F32R)
        evo = [ph(f"evo{i}", M + 2 * i, [P, SEQ]) for i in range(4)]
        sumN = [ph(f"sumN{i}", M + 15 * i, [P, TOK]) for i in range(2)]
        sqN = [ph(f"sqN{i}", M + 3 + 3 * i, [P, TOK]) for i in range(2)]
        unN = [ph(f"unN{i}", M + 9 + 3 * i, [P, TOK]) for i in range(2)]
        h2 = ph("h2", 0, [P, 2, DC, SEQ], F32R)
        g_hl = ph("g_hl", 32, [P, 2, FC, SEQ], F32R)
        FT = 32 + 2 * FC * 2
        ua = [ph(f"ua{i}", FT + 2.0625 * i, [P, SEQ + 2]) for i in range(2)]
        ub = [ph(f"ub{i}", FT + 4.125 + 2.0625 * i, [P, SEQ + 2]) for i in range(2)]
        ca = ph("ca", FT + 8.25, [P, SEQ])
        cb = ph("cb", FT + 10.25, [P, SEQ])
        sa = ph("sa", FT + 12.25, [P, SEQ])
        evd = [ph(f"evd{i}", FT + 2 * i, [P, SEQ]) for i in range(4)]
        qa = ph("qa", 32, [P, 4, SEQ])
        ka = ph("ka", 40, [P, 4, SEQ])
        va = ph("va", 48, [P, QT, 512])
        qi = ph("qi", 56, [P, 2, SEQ])
        ki = ph("ki", 60, [P, SEQ])
        qb = ph("qb", 62, [P, SEQ])
        kb = ph("kb", 64, [P, SEQ])
        vb = ph("vb", 66, [P, QT, 256])
        rb = ph("rb", 70, [P, 2, SEQ])
        uc = ph("uc", 74, [P, 2, PAD + SEQ])
        gl = ph("gl", 78.5, [P, SEQ])
        wi = ph("wi", 80.5, [P, QT, IDX_HEADS])
        cos2 = ph("cos2", 81, [P, SEQ])
        sin2 = ph("sin2", 83, [P, SEQ])
        bias2 = ph("bias2", 86, [P, QT, SEQ])
        score = ph("score", 94, [P, SEQ])
        work = ph("work", 96, [P, SEQ])
        relu = [ph(f"relu{i}", 98 + 2 * i, [P, SEQ]) for i in range(2)]
        qd = ph("qd", 102, [P, 5, SEQ])
        kd = ph("kd", 112, [P, 5, SEQ])
        attT = ph("attT", 122, [P, QT, SEQ])
        tmp = [ph(f"tmp{i}", 130 + 2 * i, [P, SEQ]) for i in range(4)]
        pos = ph("pos", 86, [P, SEQ], I32)
        win = [ph(f"win{i}", 102 + 4.125 * i, [P, 2, PAD + SEQ]) for i in range(4)]
        cnt = ph("cnt", 122, [P, 2, SEQ])
        rot2 = [ph(f"rot2{i}", 126 + 2 * i, [P, SEQ]) for i in range(2)]
        gcum = ph("gcum", 94, [P, SEQ])
        ones2 = ph("ones2", 96, [P, SEQ])
        mix = ph("mix", 0, [P, DC, SEQ])
        sumG = [ph(f"sumG{i}", 102 + 3 * i, [P, TOK]) for i in range(2)]
        unG = [ph(f"unG{i}", 114 + 3 * i, [P, TOK]) for i in range(2)]
        silu_r = ph("silu_r", 120, [P, 2, SEQ])
        p2 = [ph(f"p2{i}", 102 + 2 * i, [P, SEQ]) for i in range(2)]
        pT2 = ph("pT2", 106, [P, SEQ])
        top8 = ph("top8", 108, [P, 8])
        mix_hl = ph("mix_hl", 32, [P, 2, DC, SEQ], F32R)
        evo2 = [ph(f"evo2{i}", 64 + 2 * i, [P, SEQ]) for i in range(4)]
        ps = ctx.enter_context(nc.psum_tensor("ps", [P, 8, BANK], F32))

        def col(name, j=0, w=1, rows=slice(0, P)):
            a, _ = COLS[name]
            return par[rows, a + j:a + j + w]

        def banks(b, n):
            return ps[:, b:b + 2, :].rearrange("p b n -> p (b n)")[:, 0:n]

        def sem(name):
            return ctx.enter_context(nc.semaphore(name))

        loaded = sem("loaded")
        raw_ready = [sem(f"raw_ready{i}") for i in range(RAW_SLOTS)]
        split_done = sem("split_done")
        slab_used = sem("slab_used")
        acc_ready = sem("acc_ready")
        ada_space = sem("ada_space")
        c_loaded = sem("c_loaded")
        c_ready = sem("c_ready")
        ada_ready = [sem(f"ada_ready{i}") for i in range(max(ADA_SLOTS))]
        ada_used = sem("ada_used")
        mod_ready = sem("mod_ready")
        v_lam = sem("v_lam")
        acc_taken = sem("acc_taken")
        sq_ready = sem("sq_ready")
        sq_summed = sem("sq_summed")
        sums_ready = sem("sums_ready")
        var_ready = sem("var_ready")
        root_ready = sem("root_ready")
        rstd_ready = sem("rstd_ready")
        rstd_spread = sem("rstd_spread")
        full_ready = sem("full_ready")
        hi_ready = sem("hi_ready")
        hl_ready = sem("hl_ready")
        v_step = sem("v_step")
        a_step = sem("a_step")
        x_ready = sem("x_ready")
        rot_done = sem("rot_done")
        rope_in = sem("rope_in")
        conv_done = sem("conv_done")
        silu_done = sem("silu_done")
        merge_done = sem("merge_done")
        s_ready = sem("s_ready")
        s_max = sem("s_max")
        p_ready = sem("p_ready")
        p_normed = sem("p_normed")
        t_ready = sem("t_ready")
        t_taken = sem("t_taken")
        o_ready = sem("o_ready")
        o_taken = sem("o_taken")
        gate_ln = sem("gate_ln")
        lev_d = sem("lev_d")
        lev_e = sem("lev_e")
        qk_ready = sem("qk_ready")
        att_ready = sem("att_ready")
        att_off = sem("att_off")
        att_masked = sem("att_masked")
        ang_ready = sem("ang_ready")
        trig_ready = sem("trig_ready")
        idx_ready = sem("idx_ready")
        relu_ready = sem("relu_ready")
        score_step = sem("score_step")
        pool_ready = sem("pool_ready")
        stored = sem("stored")
        final_ready = sem("final_ready")

        block = ctx.enter_context(nc.Block())
        stages = ["ada0", "mla0", "attna0", "diff0", "attnb0", "mixed0", "ffn0", "ffn0c",
                  "mla1", "attna1", "diff1", "attnb1", "mixed1", "ffn1", "first",
                  "in20", "gla20", "dsa20", "mixed20", "ffn20", "in21", "gla21", "dsa21", "mixed21", "ffn21", "final"]
        stop_at = len(stages) if stop is None else stages.index(stop) + 1

        def on(stage):
            return stages.index(stage) < stop_at

        @block.sync
        def _(sp):
            def load(turn, s):
                sp.dma_start(raw[:, s, :], wstream[bass.ds(turn * RAW_SLOTS + s, 1)].rearrange("a p n -> (a p) n"))\
                    .then_inc(raw_ready[s], 16)

            def reload(turn, s):
                sp.wait_ge(split_done, turn * (2 * RAW_SLOTS) + 2 * (s + 1 - RAW_SLOTS))
                load(turn, s)

            def load_turns(first, end):
                with sp.Fori(first, end) as i:
                    for s in range(RAW_SLOTS):
                        reload(i, s)

            def load_c(group):
                if group:
                    sp.wait_ge(ada_space, group)
                sp.dma_start(ada_c[group][:, :, :], c_in).then_inc(c_loaded, 16)

            def load_tile(group, n):
                slots, first = ADA_SLOTS[group], sum(ADA_GROUPS[:group])
                if n >= slots:
                    sp.wait_ge(ada_used, 2 * (first + n - slots + 1))
                sp.dma_start(ada_t[group][n % slots][:, :], ada_w[first + n]).then_inc(ada_ready[n % slots], 16)

            load_c(0)
            for n in range(ADA_SLOTS[0]):
                load_tile(0, n)
            sp.dma_start(par[:, :], params).then_inc(loaded, 16)
            sp.dma_start(x[:, :, :], x_in).then_inc(loaded, 16)
            for n in range(ADA_SLOTS[0], ADA_GROUPS[0]):
                load_tile(0, n)
            for s in range(RAW_SLOTS):
                load(0, s)
            load_turns(1, DIFF_AT // RAW_SLOTS + 1)
            n = 0
            for turn in range(DIFF_AT // RAW_SLOTS + 1, (DIFF_AT + DIFF_SLABS) // RAW_SLOTS):
                for s in range(RAW_SLOTS):
                    reload(turn, s)
                    if n == 0:
                        load_c(1)
                    for _ in range(ADA_PER_SLAB):
                        load_tile(1, n)
                        n += 1
            assert n == ADA_GROUPS[1]
            load_turns((DIFF_AT + DIFF_SLABS) // RAW_SLOTS, DOWN_AT // RAW_SLOTS)
            start, per = DOWN_AT // RAW_SLOTS, MODS * RAW_SLOTS // (3 * DC)
            before = sum(ADA_GROUPS[:2])
            reload(start, 0)
            load_c(2)
            with sp.Fori(start, start + 3 * DC // RAW_SLOTS) as i:
                for s in range(RAW_SLOTS):
                    for k in range(s * per // RAW_SLOTS, (s + 1) * per // RAW_SLOTS):
                        sp.wait_ge(ada_used, i * (2 * per) + 2 * (before + k - ADA_SLOTS[2] + 1 - start * per))
                        sp.dma_start(ada_t[2][k % ADA_SLOTS[2]][:, :], ada_w[bass.ds(i * per + (before + k - start * per), 1)]
                                     .rearrange("a p n -> (a p) n")).then_inc(ada_ready[k % ADA_SLOTS[2]], 16)
                    reload(i if s < RAW_SLOTS - 1 else i + 1, (s + 1) % RAW_SLOTS)
            start += 3 * DC // RAW_SLOTS
            for s in range(1, RAW_SLOTS):
                reload(start, s)
            load_turns(start + 1, N_SLABS // RAW_SLOTS)
            if on("final"):
                sp.wait_ge(final_ready, DC)
                sp.dma_start(out, x[:, :, CTX:TOK]).then_inc(stored, 16)
                sp.wait_ge(stored, 16)

        @block.gpsimd
        def _(pool):
            zero = col("zero").to_broadcast([P, SLAB])

            def split_slab(s, turn, first_use):
                n = turn * RAW_SLOTS + s
                hi, lo = split[:, s % SPLIT_SLOTS, 0, :], split[:, s % SPLIT_SLOTS, 1, :]
                pool.wait_ge(raw_ready[s], turn * 16 + 16)
                if not first_use:
                    pool.wait_ge(slab_used, n - SPLIT_SLOTS + 1)
                nc.gpsimd.tensor_tensor(hi, raw[:, s, :], zero, ALU.add).then_inc(split_done, 1)
                pool.wait_ge(split_done, n * 2 + 1)
                nc.gpsimd.tensor_tensor(lo, raw[:, s, :], hi.bitcast(F32), ALU.subtract).then_inc(split_done, 1)

            pool.wait_ge(loaded, 32)
            for s in range(RAW_SLOTS):
                split_slab(s, 0, s < SPLIT_SLOTS)
            with pool.Fori(1, N_SLABS // RAW_SLOTS) as i:
                for s in range(RAW_SLOTS):
                    split_slab(s, i, False)
        @block.tensor
        def _(pe):
            slab, res, sq, hl = Count(), Count(), Count(), Count()
            items, outs, norms, added = Count(), Count(), Count(), Count()

            def open_slab():
                slab.add()
                pe.wait_ge(split_done, slab.now(times=2))
                return split[:, (slab.n - 1) % SPLIT_SLOTS]

            def open_acc(n):
                res.add()
                if res.n > ACC_BANKS or res.i is not None:
                    pe.wait_ge(acc_taken, res.now(back=ACC_BANKS))
                return ps[:, (res.n - 1) % ACC_BANKS, 0:n]

            def product(o, w, t, a, first, last):
                wh, wl = (w[:, j, t * P:(t + 1) * P] for j in range(2))
                nc.tensor.matmul(o, wh, a[0], start=first, stop=False)
                nc.tensor.matmul(o, wh, a[1], start=False, stop=False)
                return nc.tensor.matmul(o, wl, a[0], start=False, stop=last)

            def gemm(w, t0, K, act, g, closes):
                o = open_acc(g[1])
                for k in range(K):
                    mm = product(o, w, t0 + k, act(k, g), k == 0, k == K - 1)
                if closes:
                    mm.then_inc(slab_used, 1)
                else:
                    mm.then_inc(acc_ready, 1)

            def rotate(perm, rows, src, after):
                pe.wait_ge(acc_taken, after)
                o = open_acc(SEQ)
                nc.tensor.matmul(o[rows], col(perm, 0, P)[rows, rows], src, start=True, stop=True).then_inc(acc_ready, 1)

            def norm(segs, sums, first_bank=ACC_BANKS, heads=1):
                norms.add()
                if norms.n > 1:
                    pe.wait_ge(var_ready, norms.now(back=1))
                weight = col("ones") if heads == 1 else col("headsum", 0, P)[:, 0:P:DV]
                tiles = [[c0 + t * P for c0, n in groups for t in range(n // P)] for _, groups in segs]
                count, at = sum(map(len, tiles)), 0
                for j, ((K, _), columns) in enumerate(zip(segs, tiles)):
                    sq.add(K)
                    if K == 1:
                        pe.wait_ge(sq_ready, sq.now())
                    else:
                        added.add(K - 1)
                        pe.wait_ge(sq_summed, added.now())
                    for c in columns:
                        o = ps[:, NORM_BANK, at * heads:(at + 1) * heads]
                        at += 1
                        mm = nc.tensor.matmul(o, sums[j][:, c:c + P], weight, start=at == 1, stop=at == count)
                mm.then_inc(sums_ready, 1)
                pe.wait_ge(rstd_ready, norms.now())
                for j in range(at):
                    for h in range(heads):
                        n = P // heads
                        mm = nc.tensor.matmul(ps[h * n:(h + 1) * n, first_bank + j // QT, (j % QT) * P:(j % QT + 1) * P],
                                              rstd[:, j * heads + h:j * heads + h + 1].to_broadcast([P, n]),
                                              col("ident", 0, P), start=True, stop=True)
                mm.then_inc(rstd_spread, 1)

            def wait_hl(n):
                hl.add(n)
                pe.wait_ge(hl_ready, hl.now())

            def cols(t):
                return lambda k, g: (t[:, 0, k, g[0]:g[0] + g[1]], t[:, 1, k, g[0]:g[0] + g[1]])

            def own(t):
                return lambda k, g: (t[:, 0, k, 0:g[1]], t[:, 1, k, 0:g[1]])

            def lambdas():
                pe.wait_ge(loaded, 32)
                pe.wait_ge(v_lam, LAYERS)
                o = open_acc(2 * LAYERS)
                nc.tensor.matmul(o, col("ones", 0, P), lam_p[:, :, :].rearrange("p l j -> p (l j)"), start=True, stop=True)\
                    .then_inc(acc_ready, 1)

            def first_two(groups, act):
                ws = [open_slab() for _ in groups]
                accs = [[open_acc(g[1]) for g in gs] for gs in groups]
                for k in range(DC):
                    wait_hl(1)
                    for w, os, gs in zip(ws, accs, groups):
                        for o, g in zip(os, gs):
                            mm = product(o, w, k, act(k, g), k == 0, k == DC - 1)
                            if k == DC - 1:
                                mm.then_inc(slab_used if g == gs[-1] else acc_ready, 1)

            def project(events, weight, act, perm, rows, src, fresh=False):
                at, w = {}, None
                if fresh:
                    names = [events[0][1], next(n for _, n, _ in events if n != events[0][1])]
                    first = [[g for kind, n, g in events if kind == "gemm" and n == name] for name in names]
                    before = res.n
                    first_two(first, act(names[0]))
                    at = {names[0]: before + len(first[0]), names[1]: res.n}
                    events = events[sum(map(len, first)):]
                for kind, name, g in events:
                    if kind == "gemm":
                        t0, K, opens, closes, last = weight(name)
                        if opens and (name not in at):
                            w = open_slab()
                        gemm(w, t0, K, act(name), g, closes and g == last)
                        at[name] = res.n
                    else:
                        rotate(perm(name), rows(name), src(name), at[name])

            def mla(l):
                norm([(DC, BOTH)], sumN)
                G = groups_of(l)
                project(lora_events(l), lambda name: (0, DC, True, True, (G if name[0] == "cq" else BOTH)[-1]),
                        lambda name: cols(h_hl), lambda name: "perm_a", lambda name: slice(0, P),
                        lambda name: kr[:, CTX:TOK], fresh=True)
                norm([(3, G), (2, BOTH)], sumN)
                wait_hl(5)

                def weight(name):
                    if name[0] == "q":
                        return (3 * (name[1] % 2), 3, name[1] % 2 == 0, name[1] % 2 == 1, G[-1])
                    return (2 * name[1], 2, name[1] == 0, name[1] == H_A // 2 - 1, BOTH[-1])

                project(up_events(l), weight, lambda name: cols(cq_hl if name[0] == "q" else ckv_hl),
                        lambda name: "perm_a", lambda name: slice(0, QK_A), lambda name: qA[0:QK_A, name[1], CTX:TOK])
                w = open_slab()
                for t in range(TOK // P):
                    o = open_acc(512)
                    for k in range(2):
                        mm = swapped(o, w, k * 512, 512, ckv_hl, k, t * P, k == 0, k == 1)
                    mm.then_inc(slab_used if t == TOK // P - 1 else acc_ready, 1)

            def swapped(o, w, c0, n, t, k, tok, first, last):
                a = [t[:, j, k, tok:tok + P] for j in range(2)]
                nc.tensor.matmul(o, a[0], w[:, 0, c0:c0 + n], start=first, stop=False)
                nc.tensor.matmul(o, a[0], w[:, 1, c0:c0 + n], start=False, stop=False)
                return nc.tensor.matmul(o, a[1], w[:, 0, c0:c0 + n], start=False, stop=last)

            def attend(n, scores, values):
                pe.wait_ge(acc_taken, res.now())

                def value(i):
                    pe.wait_ge(t_taken, items.now() + i + 1)
                    free = outs.now() + max(i - 1, 0)
                    if free:
                        pe.wait_ge(o_taken, free)
                    values(i, 6 + i % 2).then_inc(o_ready, 1)

                scores(0)
                for i in range(n):
                    if i + 1 < n:
                        scores(i + 1)
                    if i >= 1:
                        value(i - 1)
                    pe.wait_ge(p_normed, items.now() + i + 1)
                    transposes(i).then_inc(t_ready, 1)
                value(n - 1)
                items.add(n)
                outs.add(n)

            def transpose_tiles(p, nk):
                for t in range(nk // P):
                    mm = nc.tensor.transpose(ps[:, 4 + t // 4, (t % 4) * P:(t % 4 + 1) * P], p[:, t * P:(t + 1) * P],
                                             col("ident", 0, P))
                return mm

            def score_pieces(bank, lhsT, keys, nk):
                for c in range(0, nk, BANK):
                    n = min(BANK, nk - c)
                    mm = nc.tensor.matmul(ps[:, bank + c // BANK, 0:n], lhsT, keys(c, n), start=True, stop=True)
                mm.then_inc(s_ready, 1)

            def attn_a(l):
                nonlocal transposes
                its = items_a(l, H_A)
                wait_rot()

                def scores(i):
                    h, c, nk = its[i]
                    score_pieces(2 * (i % 2), qA[0:QK_A, h, c:c + P], lambda c0, n: kA[0:QK_A, h, c0:c0 + n], nk)

                def values(i, bank):
                    h, c, nk = its[i]
                    for t in range(nk // P):
                        mm = nc.tensor.matmul(ps[0:V_A, bank, 0:P], vA[:, t, h * V_A:(h + 1) * V_A],
                                              pT[:, t * P:(t + 1) * P], start=t == 0, stop=t == nk // P - 1)
                    return mm

                transposes = lambda i: transpose_tiles(pA[i % 2], its[i][2])
                attend(len(its), scores, values)

            def attn_b(l):
                nonlocal transposes
                its = items_a(l, H_B)
                wait_rot()

                def scores(i):
                    h, c, nk = its[i]
                    for j in range(2):
                        r = slice(64 * j, 64 * j + 64)
                        if i >= 1:
                            pe.wait_ge(p_ready, maps.now() + 2 * (i - 1) + j + 1)
                        score_pieces(2 * j, dq[r, h, c:c + P], lambda c0, n: dk[r, h, c0:c0 + n], nk)

                def values(i, bank):
                    h, c, nk = its[i]
                    for t in range(nk // P):
                        mm = nc.tensor.matmul(ps[:, bank, 0:P], vB[:, t, h * P:(h + 1) * P],
                                              pT[:, t * P:(t + 1) * P], start=t == 0, stop=t == nk // P - 1)
                    return mm

                transposes = lambda i: transpose_tiles(pB[i % 2], its[i][2])
                attend(len(its), scores, values)

            transposes = None
            maps = Count()
            rots = Count()

            def wait_rot():
                pe.wait_ge(rot_done, rots.now())

            def diff(l):
                project(diff_events(l), lambda name: (0, DC, True, True, (groups_of(l) if name[0] == "dq" else BOTH)[-1]),
                        lambda name: cols(h_hl), lambda name: "perm_b", lambda name: slice(0, P),
                        lambda name: (dq if name[0] == "dq" else dk)[:, name[1], CTX:TOK])
                token_major(h_hl, [t * P for t in range(TOK // P)], 512, 4)

            def token_major(t, tokens, n, slabs):
                pe.wait_ge(acc_taken, res.now())
                per = DC // slabs
                for s in range(slabs):
                    w = open_slab()
                    for j, tok in enumerate(tokens):
                        for k in range(per):
                            mm = swapped(ps[:, j, 0:n], w, k * n, n, t, s * per + k, tok, s == 0 and k == 0,
                                         s == slabs - 1 and k == per - 1)
                        if s == slabs - 1 and j < len(tokens) - 1:
                            mm.then_inc(acc_ready, 1)
                    mm.then_inc(slab_used, 1)
                res.add(len(tokens))
                pe.wait_ge(acc_taken, res.now())

            def mixed(l):
                G = groups_of(l)
                norm([(1, G)] * H_B, sumB, first_bank=0)
                wait_hl(4 + H_B)
                turns, per = (4, 2)
                with Loop(pe, turns, (slab, 3 * per), (res, 4 * len(G) * per)):
                    for _ in range(per):
                        for _ in range(2):
                            w = open_slab()
                            for g in G:
                                gemm(w, 0, DC, cols(h_hl), g, g == G[-1])
                        w = open_slab()
                        for g in G:
                            gemm(w, 0, 4, cols(oA_hl), g, False)
                        for g in G:
                            gemm(w, 4, 4, cols(oB_hl), g, g == G[-1])
                wait_hl(DC)
                per = 4 // len(G)
                with Loop(pe, DC // per, (slab, per), (res, 4)):
                    for _ in range(per):
                        w = open_slab()
                        for g in G:
                            gemm(w, 0, DC, cols(m_hl), g, g == G[-1])

            def ffn(n):
                norm([(DC, [(0, n)])], sumN)
                ffn_products(n)

            def ffn_products(n):
                first_two([[(0, n)]] * 2, own(h2))
                for _ in range(2):
                    gemm(open_slab(), 0, DC, own(h2), (0, n), True)
                with Loop(pe, FC // 2 - 1, (slab, 4), (res, 4)):
                    for _ in range(4):
                        gemm(open_slab(), 0, DC, own(h2), (0, n), True)
                wait_hl(FC)
                act = own(g_hl)
                with Loop(pe, 2, (slab, 12), (res, 4)):
                    for _ in range(4):
                        o = open_acc(n)
                        for k in range(FC):
                            if k % SLAB_TILES == 0:
                                w = open_slab()
                            mm = product(o, w, k % SLAB_TILES, act(k, (0, n)), k == 0, k == FC - 1)
                            if k % SLAB_TILES == SLAB_TILES - 1 or k == FC - 1:
                                mm.then_inc(slab_used, 1)

            def in2(l):
                norm([(DC, [(0, SEQ)])], sumN)
                src = {"qa": qa, "ka": ka, "qi": qi}
                project(IN2_EVENTS, lambda name: (0, DC, True, True, LAT[-1]), lambda name: own(h2),
                        lambda name: "perm_2", lambda name: slice(0, P),
                        lambda name: ki[:, :] if name == "ki" else src[name[0]][:, name[1], :], fresh=True)
                rots.add(11)
                token_major(h2, [t * P for t in range(QT)], 512, 4)
                token_major(h2, [t * P for t in range(QT)], 256, 2)
                pe.wait_ge(acc_taken, res.now())
                w = open_slab()
                for t in range(QT):
                    o = open_acc(IDX_HEADS)
                    for k in range(DC):
                        mm = swapped(o, w, k * P, IDX_HEADS, h2, k, t * P, k == 0, k == DC - 1)
                    mm.then_inc(slab_used if t == QT - 1 else acc_ready, 1)

            heads_done, idx = Count(), Count()

            def gla(l):
                o = open_acc(SEQ)
                nc.tensor.matmul(o, col(f"w_gate{l}", 0, P, slice(0, GATE_RANK)), gl[0:GATE_RANK, :],
                                 start=True, stop=True).then_inc(acc_ready, 1)
                for c in range(2):
                    pe.wait_ge(pool_ready, l + 1)
                    o = open_acc(SEQ)
                    nc.tensor.matmul(o, col(f"w_pool{l}", c * P, P), tmp[c][:, :], start=True, stop=True).then_inc(acc_ready, 1)
                pe.wait_ge(acc_taken, res.now())
                pe.wait_ge(qk_ready, (l + 1) * 10)
                for h in range(GLA_HEADS):
                    r = slice(DK * h, DK * h + DK)
                    n = heads_done.now() + h
                    if n >= 1:
                        pe.wait_ge(att_off, 2 * n)
                        pe.wait_ge(att_masked, n)

                    def block_product(bank, c, lev, j, i0, ni):
                        return nc.tensor.matmul(ps[:, bank, c:c + ni], kd[r, lev, j * P:(j + 1) * P],
                                                qd[r, lev, i0:i0 + ni], start=True, stop=True)

                    block_product(0, 0, 1, 0, P, P)
                    block_product(0, P, 0, 0, 2 * P, 2 * P)
                    block_product(1, 0, 0, 1, 2 * P, 2 * P)
                    block_product(1, 2 * P, 1, 2, 3 * P, P)
                    for lev in range(2, 5):
                        for j in range(QT):
                            mm = block_product(lev, j * P, lev, j, j * P, P)
                    mm.then_inc(att_ready, 1)
                    pe.wait_ge(att_off, 2 * (n + 1))
                    pe.wait_ge(att_masked, n + 1)
                    pe.wait_ge(o_taken, outs.now(back=min(h, 1)))
                    o = ps[0:DV, 6 + h % 2, :]
                    for j in range(QT):
                        mm = nc.tensor.matmul(o[:, j * P:SEQ], vb[:, j, h * DV:(h + 1) * DV], attT[:, j, j * P:SEQ],
                                              start=j == 0, stop=j == QT - 1)
                    mm.then_inc(o_ready, 1)
                    outs.add()
                heads_done.add(GLA_HEADS)
                norm([(1, [(0, SEQ)])] * 2, sumG, heads=2)

            def dsa(l):
                nonlocal transposes
                wait_rot()
                for t in range(1, QT):
                    nk = (t + 1) * P
                    for h in range(IDX_HEADS):
                        r = slice(64 * (h % 2), 64 * (h % 2) + 64)
                        idx.add()
                        if idx.n > 4:
                            pe.wait_ge(relu_ready, idx.now() - 4)
                        nc.tensor.matmul(ps[:, h, 0:nk], qi[r, h // 2, t * P:(t + 1) * P], ki[r, 0:nk],
                                         start=True, stop=True).then_inc(idx_ready, 1)
                pe.wait_ge(relu_ready, idx.now())

                def scores(i):
                    h, t = ITEMS_2[i]
                    r = slice(64 * (h % 2), 64 * (h % 2) + 64)
                    n = maps.now() + i
                    if i >= 4:
                        pe.wait_ge(s_max, maps.now() + i - 3)
                    nc.tensor.matmul(ps[:, i % 4, 0:(t + 1) * P], qa[r, h // 2, t * P:(t + 1) * P],
                                     ka[r, h // 2, 0:(t + 1) * P], start=True, stop=True).then_inc(s_ready, 1)

                def values(i, bank):
                    h, t = ITEMS_2[i]
                    for j in range(t + 1):
                        mm = nc.tensor.matmul(ps[0:HD, bank, 0:P], va[:, j, h * HD:(h + 1) * HD],
                                              pT2[:, j * P:(j + 1) * P], start=j == 0, stop=j == t)
                    return mm

                transposes = lambda i: transpose_tiles(p2[i % 2], (ITEMS_2[i][1] + 1) * P)
                attend(len(ITEMS_2), scores, values)
                maps.add(len(ITEMS_2))

            def mixed2(l):
                wait_hl(DC)
                with Loop(pe, 2, (slab, 4), (res, 4)):
                    for _ in range(4):
                        gemm(open_slab(), 0, DC, own(mix_hl), (0, SEQ), True)

            for l in range(LAYERS):
                if l == 0:
                    lambdas()
                if on(f"mla{l}"):
                    mla(l)
                    rots.add(2 + H_A)
                if on(f"attna{l}"):
                    attn_a(l)
                    maps.add(len(items_a(l, H_A)))
                if on(f"diff{l}"):
                    diff(l)
                    rots.add(2 * H_B)
                if on(f"attnb{l}"):
                    attn_b(l)
                    maps.add(2 * len(items_a(l, H_B)))
                if on(f"mixed{l}"):
                    mixed(l)
                if on(f"ffn{l}"):
                    ffn(SEQ)
                if l == 0 and on("ffn0c"):
                    ffn(CTX)
            if on("first"):
                norm([(DC, [(0, SEQ)])], sumN)
            for l in range(LAYERS):
                if on(f"in2{l}"):
                    in2(l)
                if on(f"gla2{l}"):
                    gla(l)
                if on(f"dsa2{l}"):
                    dsa(l)
                if on(f"mixed2{l}"):
                    mixed2(l)
                if on(f"ffn2{l}"):
                    ffn(SEQ)
            if on("final"):
                norm([(DC, [(0, SEQ)])], sumN)


        @block.scalar
        def _(act):
            res, acc, slab, sq, full = Count(), Count(), Count(), Count(), Count()
            norms, squared, rots, maps, items, outs = (Count() for _ in range(6))
            xs, merges, steps, idx = Count(4), Count(), Count(), Count()
            copy = ACT.Copy

            def take(n, closes, bank=None):
                res.add()
                if closes:
                    slab.add()
                    act.wait_ge(slab_used, slab.now())
                else:
                    acc.add()
                    act.wait_ge(acc_ready, acc.now())
                return ps[:, (res.n - 1) % ACC_BANKS if bank is None else bank, 0:n]

            def bring(dst, src, func=copy, **kw):
                nc.scalar.activation(dst, src, func, **kw).then_inc(acc_taken, 1)

            def step(ins):
                steps.add()
                ins.then_inc(a_step, 1)
                act.wait_ge(a_step, steps.now())

            def squares(src, chunks, groups, first, ring):
                act.wait_ge(acc_taken, res.now())
                c = span(groups)
                for k in range(chunks):
                    dst = first
                    if k:
                        squared.add()
                        dst = ring[squared.n % 2]
                        if squared.n > 2:
                            act.wait_ge(sq_summed, squared.now(back=2))
                    nc.scalar.activation(dst[:, c], src(k), ACT.Square).then_inc(sq_ready, 1)

            def roots(n):
                norms.add()
                act.wait_ge(var_ready, norms.now())
                nc.scalar.activation(rstd[:, 0:n], rstd[:, 0:n], ACT.Sqrt).then_inc(root_ready, 1)

            def highs(chunks, src, dst, groups, shift=None):
                for k in range(chunks):
                    full.add()
                    act.wait_ge(full_ready, full.now())
                    for g in groups:
                        c = slice(g[0], g[0] + g[1])
                        if shift is None:
                            ins = nc.scalar.activation(dst(k)[:, c], src(k)[:, c], copy)
                        else:
                            ins = nc.scalar.activation(dst(k)[:, c], src(k)[:, c], ACT.Identity, bias=shift(k, g))
                    ins.then_inc(hi_ready, 1)

            def span(groups):
                return slice(groups[0][0], groups[-1][0] + groups[-1][1])

            def silu_c(group):
                act.wait_ge(c_loaded, 16 * (group + 1))
                c = ada_c[group][:, :, :]
                nc.scalar.activation(c, c, ACT.Silu).then_inc(c_ready, 1)

            def lambdas():
                bring(lam_e[:, :, :].rearrange("p l j -> p (l j)"), take(2 * LAYERS, False), ACT.Exp)

            def evacuate(events, dst, closes, rows, rotbuf, rot_rows):
                j = 0
                for kind, name, g in events:
                    if kind == "gemm":
                        o = take(g[1], closes(name, g))
                        d = dst(name, g)
                        r = rows(name)
                        bring(d, o[r, :])
                    else:
                        o = take(SEQ, False)
                        if j >= 2:
                            act.wait_ge(rot_done, rots.now() + j - 1)
                        r = rot_rows(name)
                        bring(rotbuf[j % 2][r, :], o[r, :])
                        j += 1

            every = lambda name: slice(0, P)
            rope_rows = slice(NOPE, QK_A)

            def mla(l):
                G = groups_of(l)
                act.wait_ge(x_ready, xs.now())
                act.dma_start(ropeA[:, :, :], rope_tab[:, 0:2, :]).then_inc(rope_in, 16)
                squares(lambda k: x[:, k, :], DC, BOTH, sumN[0], sqN)
                roots(TOK // P)
                highs(DC, lambda k: unN[k % 2], lambda k: h_hl[:, 0, k, :], BOTH, lambda k, g: mod[:, l, k, which(g)])

                def dst(name, g):
                    c = slice(g[0], g[0] + g[1])
                    if name == "kr":
                        return kr[:, c]
                    return (cq if name[0] == "cq" else ckv)[:, name[1], c]

                evacuate(lora_events(l), dst, lambda name, g: g == LAT[0], every, rot, lambda name: rope_rows)
                squares(lambda k: cq[:, k, span(G)], 3, G, sumN[0], sqN)
                squares(lambda k: ckv[:, k, :], 2, BOTH, sumN[1], sqN)
                roots((span(G).stop - span(G).start + TOK) // P)
                highs(3, lambda k: unN[k % 2], lambda k: cq_hl[:, 0, k, :], [(span(G).start, span(G).stop - span(G).start)])
                highs(2, lambda k: unN[(k + 1) % 2], lambda k: ckv_hl[:, 0, k, :], [(0, TOK)])
                j = 1
                for kind, name, g in up_events(l):
                    if kind == "rot":
                        o = take(SEQ, False)
                        if j >= 2:
                            act.wait_ge(rot_done, rots.now() + j - 1)
                        bring(rot[j % 2][rope_rows, :], o[rope_rows, :])
                        j += 1
                        continue
                    c = slice(g[0], g[0] + g[1])
                    kind, m = name
                    if kind == "q":
                        o = take(g[1], m % 2 == 1 and g == LAT[0])
                        bring(qA[0:QK_A, m, c], o[0:QK_A, :])
                    else:
                        o = take(g[1], m == H_A // 2 - 1 and g == LAT[0])
                        nc.scalar.activation(kA[0:NOPE, 2 * m, c], o[0:NOPE, :], copy)
                        bring(kA[0:NOPE, 2 * m + 1, c], o[NOPE:P, :])
                rots.add(2 + H_A)
                act.wait_ge(rot_done, rots.now())
                for t in range(TOK // P):
                    bring(vA[:, t, :], take(512, t == TOK // P - 1))

            def attend(n, exps, transposed, pt):
                def taken(i):
                    act.wait_ge(t_ready, items.now() + i + 1)
                    nk = transposed(i)
                    nc.scalar.activation(pt[:, 0:nk], banks(4, nk), copy).then_inc(t_taken, 1)

                exps(0)
                for i in range(n):
                    if i + 1 < n:
                        exps(i + 1)
                    taken(i)
                items.add(n)

            def attn_a(l):
                its = items_a(l, H_A)

                def exps(i):
                    nk = its[i][2]
                    act.wait_ge(s_max, maps.now() + i + 1)
                    st = stat[:, i % 2, :]
                    nc.scalar.activation(pA[i % 2][:, 0:nk], banks(2 * (i % 2), nk), ACT.Exp, bias=st[:, 0:1],
                                         scale=QK_A ** -0.5, accum_out=st[:, 2:3]).then_inc(p_ready, 1)

                attend(len(its), exps, lambda i: its[i][2], pT)
                maps.add(len(its))

            def attn_b(l):
                its = items_a(l, H_B)

                def exps(i):
                    nk = its[i][2]
                    st = stat[:, i % 2, :]
                    for j in range(2):
                        act.wait_ge(s_max, maps.now() + 2 * i + j + 1)
                        nc.scalar.activation(pB[2 * j + i % 2][:, 0:nk], banks(2 * j, nk), ACT.Exp, bias=st[:, j:j + 1],
                                             scale=DH_B ** -0.5, accum_out=st[:, 2 + j:3 + j]).then_inc(p_ready, 1)

                attend(len(its), exps, lambda i: its[i][2], pT)
                maps.add(2 * len(its))
                outs.add(len(its))

            def diff(l):
                outs.add(len(items_a(l, H_A)))
                act.wait_ge(o_taken, outs.now())
                act.dma_start(ropeB[:, :, :], rope_tab[:, 2:4, :]).then_inc(rope_in, 16)
                for k in range(4):
                    nc.scalar.activation(oA_hl[:, 0, k, span(groups_of(l))], oA[:, k, span(groups_of(l))], copy)\
                        .then_inc(hi_ready, 1)
                if l == 0:
                    silu_c(1)
                evacuate(diff_events(l), lambda name, g: (dq if name[0] == "dq" else dk)[:, name[1], g[0]:g[0] + g[1]],
                         lambda name, g: g == LAT[0], every, rotB, every)
                rots.add(2 * H_B)
                token_major(TOK // P, 512, 4, lambda t: vB[:, t, :])

            def token_major(n, width, slabs, dst, **kw):
                slab.add(slabs - 1)
                for t in range(n):
                    bring(dst(t), take(width, t == n - 1, bank=t))

            def mixed(l):
                G = groups_of(l)
                c = span(G)
                act.wait_ge(o_taken, outs.now())
                if l == 0:
                    act.wait_ge(mod_ready, 2)
                for h in range(H_B):
                    squares(lambda k: oB[:, h, c], 1, G, sumB[h], None)
                roots(H_B * (c.stop - c.start) // P)
                highs(H_B, lambda k: unB[k % 2], lambda k: oB_hl[:, 0, k, :], [(c.start, c.stop - c.start)])
                merges.add(1)
                per = 2
                with Loop(act, 4, (slab, 3 * per), (res, 4 * len(G) * per), (acc, (4 * len(G) - 3) * per), (merges, per)):
                    for _ in range(per):
                        act.wait_ge(merge_done, merges.now())
                        for j, func in enumerate((ACT.Sigmoid, ACT.Sigmoid, copy, copy)):
                            for g in G:
                                bring(mg[:, j, g[0]:g[0] + g[1]], take(g[1], j != 2 and g == G[-1]), func)
                        merges.add(1)
                act.wait_ge(merge_done, merges.now())
                for k in range(DC):
                    nc.scalar.activation(m_hl[:, 0, k, c], merged[:, k, c], copy).then_inc(hi_ready, 1)
                per = 4 // len(G)
                with Loop(act, DC // per, (slab, per), (res, 4), (acc, per * (len(G) - 1)), (xs, 4)) as i:
                    for m in range(per):
                        for g in G:
                            residual_term(evo, g[1], g == G[-1], mod[:, l, bass.ds(i * per + (2 * DC + m), 1), which(g)])

            def which(g):
                return slice(0, 1) if g[0] == CTX else slice(1, 2)

            def residual_term(buf, n, closes, gate):
                xs.add()
                o = take(n, closes)
                act.wait_ge(x_ready, xs.now(back=4))
                dst = buf[(xs.n - 1) % 4][:, 0:n]
                if gate is None:
                    bring(dst, o)
                else:
                    bring(dst, o, ACT.Identity, scale=gate.rearrange("p a v -> p (a v)"))

            def ffn(l, n, c0, gate, off=1, beside=False):
                act.wait_ge(x_ready, xs.now())
                squares(lambda k: x[:, k, c0:c0 + n], DC, [(0, n)], sumN[0], sqN)
                roots(n // P)
                shift = None if gate is None else (lambda k, g: mod[:, l, 3 * DC + k, gate])
                highs(DC, lambda k: unN[k % 2], lambda k: h2[:, 0, k, :], [(0, n)], shift)
                with Loop(act, FC // 2, (slab, 4), (res, 4), (full, 2), (convs, 2)) as i:
                    for j in range(2):
                        full.add()
                        convs.add()
                        act.wait_ge(full_ready, full.now(back=2))
                        bring(ua[j][:, off:n + off], take(n, True))
                        bring(ub[j][:, off:n + off], take(n, True))
                        act.wait_ge(conv_done, convs.now())
                        nc.scalar.activation(sa[:, 0:n], ca[:, 0:n], ACT.Silu).then_inc(silu_done, 1)
                        act.wait_ge(full_ready, full.now())
                        nc.scalar.activation(g_hl[:, 0, bass.ds(i * 2 + j, 1), 0:n].rearrange("p a n -> p (a n)"),
                                             cb[:, 0:n], copy).then_inc(hi_ready, 1)
                if beside:
                    silu_c(2)
                with Loop(act, 2, (slab, 12), (res, 4), (xs, 4)) as i:
                    for m in range(4):
                        slab.add(2)
                        residual_term(evd, n, True, None if gate is None else mod[:, l, bass.ds(i * 4 + (5 * DC + m), 1), gate])

            convs = Count()

            def in2(l):
                act.wait_ge(x_ready, xs.now())
                act.dma_start(pos[:, :], pos_in).then_inc(rope_in, 16)
                act.dma_start(cnt[:, :, :], cnt_in).then_inc(rope_in, 16)
                squares(lambda k: x[:, k, CTX:TOK], DC, [(0, SEQ)], sumN[0], sqN)
                roots(QT)
                highs(DC, lambda k: unN[k % 2], lambda k: h2[:, 0, k, :], [(0, SEQ)])
                for j, table in enumerate((sin2, cos2)):
                    act.wait_ge(ang_ready, 2 * l + j + 1)
                    nc.scalar.activation(table[:, :], table[:, :], ACT.Sin).then_inc(trig_ready, 1)
                dsts = {"qa": qa, "ka": ka, "qi": qi, "rb": rb}

                def dst(name, g):
                    if name[0] == "uc":
                        return uc[:, name[1], PAD:]
                    if name == "gl":
                        return gl[0:GATE_RANK, :]
                    if isinstance(name, str):
                        return {"ki": ki, "qb": qb, "kb": kb}[name][:, :]
                    return dsts[name[0]][:, name[1], :]

                evacuate(IN2_EVENTS, dst, lambda name, g: True,
                         lambda name: slice(0, GATE_RANK) if name == "gl" else slice(0, P), rot2, every)
                rots.add(11)
                token_major(QT, 512, 4, lambda t: va[:, t, :])
                token_major(QT, 256, 2, lambda t: vb[:, t, :])
                for t in range(QT):
                    bring(wi[:, t, :], take(IDX_HEADS, t == QT - 1), scale=IDX_SCALE)

            heads, levels = Count(), Count()

            def gla(l):
                z, t = tmp[2][:, :], tmp[3][:, :]
                act.wait_ge(pool_ready, l + 1)
                bring(z, take(SEQ, False), ACT.Identity, bias=col(f"b_gate{l}"))
                act.wait_ge(acc_taken, res.now())
                step(nc.scalar.activation(t, z, ACT.Abs))
                step(nc.scalar.activation(t, t, ACT.Exp, scale=-1.0))
                nc.scalar.activation(t, t, ACT.Ln, bias=col("ones", 0)).then_inc(gate_ln, 1)
                for c in range(2):
                    bring(mix[:, 6 + c, :], take(SEQ, False), ACT.Identity, scale=col(f"pool_scale{l}", c))
                for lev in range(5):
                    for buf, sign in ((qd, 1.0), (kd, -1.0)):
                        levels.add()
                        act.wait_ge(lev_d, levels.now())
                        nc.scalar.activation(buf[:, lev, :], buf[:, lev, :], ACT.Exp, scale=sign / GATE_TAU).then_inc(lev_e, 1)
                for h in range(GLA_HEADS):
                    heads.add()
                    act.wait_ge(att_ready, heads.now())
                    act.wait_ge(o_ready, outs.now() + h)
                    nc.scalar.activation(attT[:, 0, P:SEQ], ps[:, 0, 0:3 * P], copy).then_inc(att_off, 1)
                    nc.scalar.activation(attT[:, 1, 2 * P:SEQ], ps[:, 1, 0:2 * P], copy)
                    nc.scalar.activation(attT[:, 2, 3 * P:SEQ], ps[:, 1, 2 * P:3 * P], copy).then_inc(att_off, 1)
                outs.add(GLA_HEADS)
                act.wait_ge(o_taken, outs.now())
                for k in range(2):
                    squares(lambda _: mix[:, 4 + k, :], 1, [(0, SEQ)], sumG[k], None)
                nc.scalar.activation(silu_r[:, :, :], rb[:, :, :], ACT.Silu).then_inc(silu_done, 1)
                roots(2 * 2 * QT)

            def dsa(l):
                for t in range(1, QT):
                    nk = (t + 1) * P
                    for h in range(IDX_HEADS):
                        idx.add()
                        act.wait_ge(idx_ready, idx.now())
                        if idx.n > 2:
                            act.wait_ge(score_step, idx.now() - 2)
                        nc.scalar.activation(relu[idx.n % 2][:, 0:nk], ps[:, h, 0:nk], ACT.Relu).then_inc(relu_ready, 1)

                def exps(i):
                    nk = (ITEMS_2[i][1] + 1) * P
                    act.wait_ge(s_max, maps.now() + i + 1)
                    st = stat[:, i % 2, :]
                    nc.scalar.activation(p2[i % 2][:, 0:nk], p2[i % 2][:, 0:nk], ACT.Exp, bias=st[:, 0:1],
                                         scale=HD ** -0.5, accum_out=st[:, 2:3]).then_inc(p_ready, 1)

                attend(len(ITEMS_2), exps, lambda i: (ITEMS_2[i][1] + 1) * P, pT2)
                maps.add(len(ITEMS_2))
                outs.add(len(ITEMS_2))

            def mixed2(l):
                act.wait_ge(o_taken, outs.now())
                act.wait_ge(acc_taken, res.now())
                for k in range(DC):
                    nc.scalar.activation(mix_hl[:, 0, k, :], mix[:, k, :], copy).then_inc(hi_ready, 1)
                with Loop(act, 2, (slab, 4), (res, 4), (xs, 4)):
                    for m in range(4):
                        residual_term(evo2, SEQ, True, None)

            def normed_in_place():
                act.wait_ge(x_ready, xs.now())
                squares(lambda k: x[:, k, CTX:TOK], DC, [(0, SEQ)], sumN[0], sqN)
                roots(QT)

            for l in range(LAYERS):
                if l == 0:
                    silu_c(0)
                    lambdas()
                if on(f"mla{l}"):
                    mla(l)
                if on(f"attna{l}"):
                    attn_a(l)
                if on(f"diff{l}"):
                    diff(l)
                if on(f"attnb{l}"):
                    attn_b(l)
                if on(f"mixed{l}"):
                    mixed(l)
                if on(f"ffn{l}"):
                    ffn(l, SEQ, CTX, slice(0, 1), beside=l == 0)
                if l == 0 and on("ffn0c"):
                    ffn(l, CTX, 0, slice(1, 2))
            if on("first"):
                normed_in_place()
                xs.add(DC)
            for l in range(LAYERS):
                if on(f"in2{l}"):
                    in2(l)
                if on(f"gla2{l}"):
                    gla(l)
                if on(f"dsa2{l}"):
                    dsa(l)
                if on(f"mixed2{l}"):
                    mixed2(l)
                if on(f"ffn2{l}"):
                    ffn(l, SEQ, CTX, None, off=2)
            if on("final"):
                normed_in_place()

        @block.vector
        def _(dve):
            res, vs, sqs, norms, his, added, ada = (Count() for _ in range(7))
            items, outs, maps, silus, merges = Count(), Count(), Count(), Count(), Count()
            idx, heads, levels, tables = Count(), Count(), Count(), Count()
            rots = Count()

            def v(ins):
                vs.add()
                ins.then_inc(v_step, 1)
                dve.wait_ge(v_step, vs.now())

            def span(groups):
                return slice(groups[0][0], groups[-1][0] + groups[-1][1])

            def inverse(segs, sums, ring, heads=1):
                for j, (K, groups, _) in enumerate(segs):
                    sqs.add()
                    c = span(groups)
                    for _ in range(1, K):
                        sqs.add()
                        added.add()
                        dve.wait_ge(sq_ready, sqs.now())
                        nc.vector.tensor_tensor(sums[j][:, c], sums[j][:, c], ring[added.n % 2][:, c], ALU.add)\
                            .then_inc(sq_summed, 1)
                        dve.wait_ge(sq_summed, added.now())
                norms.add()
                dve.wait_ge(sums_ready, norms.now())
                at = 0
                for _, groups, n_feat in segs:
                    tiles = sum(n for _, n in groups) // P
                    n = tiles * heads
                    v(nc.vector.tensor_scalar(ms[:, at:at + n], ps[:, NORM_BANK, at:at + n], 1.0 / n_feat, EPS,
                                              ALU.mult, ALU.add))
                    at += n
                r, t = rstd[:, 0:at], newton[:, 0:at]
                nc.vector.reciprocal(r, ms[:, 0:at]).then_inc(var_ready, 1)
                dve.wait_ge(root_ready, norms.now())
                v(nc.vector.tensor_tensor(t, r, r, ALU.mult))
                v(nc.vector.tensor_tensor(t, t, ms[:, 0:at], ALU.mult))
                v(nc.vector.tensor_scalar(t, t, -0.5, 1.5, ALU.mult, ALU.add))
                nc.vector.tensor_tensor(r, r, t, ALU.mult).then_inc(rstd_ready, 1)
                dve.wait_ge(rstd_spread, norms.now())

            def spread(first_bank, tile, n):
                c = first_bank * BANK + tile * P
                return ps[:, :, :].rearrange("p b n -> p (b n)")[:, c:c + n]

            def low(src, dst, shift=None):
                dve.wait_ge(hi_ready, his.add().now())
                if shift is None:
                    ins = nc.vector.tensor_tensor(dst[1], src, dst[0].bitcast(F32), ALU.subtract)
                else:
                    for c, value in shift:
                        ins = nc.vector.scalar_tensor_tensor(dst[1][:, c], src[:, c], value, dst[0][:, c].bitcast(F32),
                                                             ALU.add, ALU.subtract)
                ins.then_inc(hl_ready, 1)

            def norm(segs, sums, ring, un, first_bank=ACC_BANKS):
                inverse([seg[0:3] for seg in segs], sums, ring)
                at, j, last = 0, 0, None
                for K, groups, _, src, gains, shift, dst in segs:
                    c = span(groups)
                    for k in range(K):
                        u = un[j % 2]
                        if his.n:
                            dve.wait_ge(hl_ready, his.now())
                        for g in groups:
                            cg = slice(g[0], g[0] + g[1])
                            ins = nc.vector.scalar_tensor_tensor(u[:, cg], src(k, cg), gains(k, g),
                                                                 spread(first_bank, at + (g[0] - c.start) // P, g[1]),
                                                                 ALU.mult, ALU.mult)
                        ins.then_inc(full_ready, 1)
                        if last is not None:
                            low(*last)
                        shifts = None if shift is None else [
                            (slice(g[0] - c.start, g[0] - c.start + g[1]), shift(k, g)) for g in groups]
                        last = (u[:, c], dst(k, c), shifts)
                        j += 1
                    at += (c.stop - c.start) // P
                low(*last)

            def normed_in_place(signal):
                inverse([(DC, [(0, SEQ)], D)], sumN, sqN)
                g = "g_final" if signal is x_ready else "final_g"
                for k in range(DC):
                    xk = x[:, k, CTX:TOK]
                    nc.vector.scalar_tensor_tensor(xk, xk, col(g, k), spread(ACC_BANKS, 0, SEQ), ALU.mult, ALU.mult)\
                        .then_inc(signal, 1)

            def pair(t):
                return lambda k, c: (t[:, 0, k, c], t[:, 1, k, c])

            def lat_col(g):
                return slice(0, 1) if g[0] == CTX else slice(1, 2)

            def ada_tile(w, group, at):
                for j in range(2):
                    if ada.n:
                        dve.wait_ge(ada_used, ada.now())
                    nc.vector.tensor_tensor_reduce(
                        out=ps[:, 6:8, :].rearrange("p b n -> p (b n)"), in0=w, in1=ada_c[group][:, j, :], scale=1.0, scalar=0.0,
                        op0=ALU.mult, op1=ALU.add, accum_out=at[j]).then_inc(ada_used, 1)
                    ada.add()

            def ada_tiles(group, first, n):
                slots, m = ADA_SLOTS[group], sum(ADA_GROUPS[:group])
                for t in range(first, first + n):
                    dve.wait_ge(ada_ready[t % slots], 16 * (ada_loads(group, t % slots) + t // slots + 1))
                    ada_tile(ada_t[group][t % slots][:, :], group, [mod[:, (m + t) // MODS, (m + t) % MODS, j:j + 1]
                                                                     for j in range(2)])

            def add_bias(group, l, m, n):
                dve.wait_ge(ada_used, ada.now())
                tiles = mod[:, l, m:m + n, :]
                nc.vector.tensor_tensor(tiles, tiles, col(f"b_ada{l}", m, n).unsqueeze(2).to_broadcast([P, n, 2]), ALU.add)\
                    .then_inc(mod_ready, 1)
                dve.wait_ge(mod_ready, group + 1)

            def free_place():
                dve.wait_ge(hl_ready, his.now())
                nc.vector.memset(stat[:, 0, 7:8], 0.0).then_inc(ada_space, 1)

            def start():
                dve.wait_ge(c_ready, 1)
                ada_tiles(0, 0, ADA_GROUPS[0])
                dve.wait_ge(loaded, 32)
                add_bias(0, 0, 0, ADA_GROUPS[0])
                for j in range(4):
                    nc.vector.memset(stat[:, 0, 4 + j:5 + j], 0.0).then_inc(x_ready, 1)
                for l in range(LAYERS):
                    nc.vector.tensor_tensor(lam_p[:, l, :], col(f"lam{l}", 0, 2), col(f"lam{l}", 2, 2), ALU.mult)\
                        .then_inc(v_lam, 1)
                res.add()
                dve.wait_ge(acc_taken, res.now())
                for l in range(LAYERS):
                    v(nc.vector.scalar_tensor_tensor(neg_lam[:, l:l + 1], lam_e[:, l, 1:2], -lam_init(l), lam_e[:, l, 0:1],
                                                     ALU.add, ALU.subtract))

            def gains_of(l, j):
                m = DC * (1 + 3 * j)
                name = ("g_mix", "g_ffn")[j]
                v(nc.vector.scalar_tensor_tensor(gain[:, j, :, :], mod[:, l, m:m + DC, :], 1.0,
                                                 col(f"{name}{l}", 0, 2 * DC).rearrange("p (k v) -> p k v", v=2),
                                                 ALU.add, ALU.mult))

            def rope(dst, rotated, cos, sin):
                v(nc.vector.tensor_tensor(rotated, rotated, sin, ALU.mult))
                v(nc.vector.tensor_tensor(dst, dst, cos, ALU.mult))
                return nc.vector.tensor_tensor(dst, dst, rotated, ALU.add)

            def rope_results(events, dst, rows, rotbuf, table, j=0, beside=None):
                for kind, name, g in events:
                    res.add()
                    if kind == "rot":
                        dve.wait_ge(acc_taken, res.now())
                        r = rows(name)
                        rope(dst(name), rotbuf[j % 2][r, :], table[0][r, :], table[1][r, :]).then_inc(rot_done, 1)
                        if beside is not None:
                            beside(j)
                        j += 1

            rope_rows = slice(NOPE, QK_A)

            def mla(l):
                G = groups_of(l)
                gains_of(l, 0)
                norm([(DC, BOTH, D, lambda k, c: x[:, k, c], lambda k, g: gain[:, 0, k, lat_col(g)],
                       lambda k, g: mod[:, l, k, lat_col(g)], pair(h_hl))], sumN, sqN, unN)
                tables.add(16)
                dve.wait_ge(rope_in, tables.now())
                tab = (ropeA[:, 0, :], ropeA[:, 1, :])
                rope_results(lora_events(l), lambda name: kr[rope_rows, CTX:TOK], lambda name: rope_rows, rot, tab)
                norm([(3, G, Q_LORA, lambda k, c: cq[:, k, c], lambda k, g: col(f"g_q{l}", k), None, pair(cq_hl)),
                      (2, BOTH, KV_LORA, lambda k, c: ckv[:, k, c], lambda k, g: col(f"g_kv{l}", k), None, pair(ckv_hl))],
                     sumN, sqN, unN)
                rope_results([e for e in up_events(l) if e[1][0] == "q"], lambda name: qA[rope_rows, name[1], CTX:TOK],
                             lambda name: rope_rows, rot, tab, j=1)
                dve.wait_ge(rot_done, rots.now() + 1 + H_A)
                nc.vector.tensor_copy(kA[rope_rows, :, :], kr[rope_rows, :].unsqueeze(1).to_broadcast([ROPE_A, H_A, TOK]))\
                    .then_inc(rot_done, 1)
                rots.add(2 + H_A)
                res.add(H_A // 2 * 2 + TOK // P)

            def attend(n, maxima, normalise, output):
                def out_tile(i):
                    outs.add()
                    dve.wait_ge(o_ready, outs.now())
                    output(i, 6 + i % 2).then_inc(o_taken, 1)

                maxima(0)
                for i in range(n):
                    normalise(i)
                    if i + 1 < n:
                        maxima(i + 1)
                    if i >= 1:
                        out_tile(i - 1)
                out_tile(n - 1)

            def row_max(n, bank, nk, scale, st, j=0):
                dve.wait_ge(s_ready, n)
                v(nc.vector.reduce_max(st[:, 6 + j:7 + j], banks(bank, nk), AX.X))
                nc.vector.tensor_scalar(st[:, j:j + 1], st[:, 6 + j:7 + j], -scale, None, ALU.mult).then_inc(s_max, 1)

            def attn_a(l):
                its = items_a(l, H_A)

                def maxima(i):
                    row_max(maps.now() + i + 1, 2 * (i % 2), its[i][2], QK_A ** -0.5, stat[:, i % 2, :])

                def normalise(i):
                    st, p = stat[:, i % 2, :], pA[i % 2][:, 0:its[i][2]]
                    dve.wait_ge(p_ready, maps.now() + i + 1)
                    v(nc.vector.reciprocal(st[:, 4:5], st[:, 2:3]))
                    nc.vector.tensor_scalar(p, p, st[:, 4:5], None, ALU.mult).then_inc(p_normed, 1)

                def output(i, bank):
                    h, c, _ = its[i]
                    r = (h % 2) * V_A
                    return nc.vector.tensor_copy(oA[r:r + V_A, h // 2, c:c + P], ps[0:V_A, bank, 0:P])

                attend(len(its), maxima, normalise, output)
                maps.add(len(its))

            def attn_b(l):
                its = items_a(l, H_B)

                def maxima(i):
                    for j in range(2):
                        row_max(maps.now() + 2 * i + j + 1, 2 * j, its[i][2], DH_B ** -0.5, stat[:, i % 2, :], j)

                def normalise(i):
                    nk, st = its[i][2], stat[:, i % 2, :]
                    p1, q1 = pB[i % 2][:, 0:nk], pB[2 + i % 2][:, 0:nk]
                    dve.wait_ge(p_ready, maps.now() + 2 * i + 2)
                    v(nc.vector.reciprocal(st[:, 4:6], st[:, 2:4]))
                    v(nc.vector.tensor_scalar(st[:, 5:6], st[:, 5:6], neg_lam[:, l:l + 1], None, ALU.mult))
                    v(nc.vector.tensor_scalar(p1, p1, st[:, 4:5], None, ALU.mult))
                    nc.vector.scalar_tensor_tensor(p1, q1, st[:, 5:6], p1, ALU.mult, ALU.add).then_inc(p_normed, 1)

                def output(i, bank):
                    h, c, _ = its[i]
                    return nc.vector.tensor_copy(oB[:, h, c:c + P], ps[:, bank, 0:P])

                attend(len(its), maxima, normalise, output)
                maps.add(2 * len(its))

            def diff(l):
                c = span(groups_of(l))
                for k in range(4):
                    low(oA[:, k, c], pair(oA_hl)(k, c))
                if l == 0:
                    free_place()
                    dve.wait_ge(c_ready, 2)
                tables.add(16)
                dve.wait_ge(rope_in, tables.now())
                some = ADA_GROUPS[1] // (2 * H_B + 2)
                rope_results(diff_events(l), lambda name: (dq if name[0] == "dq" else dk)[:, name[1], CTX:TOK],
                             lambda name: slice(0, P), rotB, (ropeB[:, 0, :], ropeB[:, 1, :]),
                             beside=(lambda j: ada_tiles(1, j * some, some)) if l == 0 else None)
                if l == 0:
                    ada_tiles(1, 2 * H_B * some, ADA_GROUPS[1] - 2 * H_B * some)
                    add_bias(1, 0, ADA_GROUPS[0], ADA_GROUPS[1])
                rots.add(2 * H_B)
                res.add(TOK // P)

            def mixed(l):
                G = groups_of(l)
                c = span(G)
                v(nc.vector.tensor_scalar(gsub[:, :], col(f"g_sub{l}"), 1.0 - lam_init(l), None, ALU.mult))
                def head(h):
                    return (1, G, 2 * DH_B, lambda k, cg: oB[:, h, cg], lambda k, g: gsub[:, :], None,
                            lambda k, cg: pair(oB_hl)(h, cg))

                norm([head(h) for h in range(H_B)], sumB, None, unB, first_bank=0)
                nc.vector.memset(stat[:, 0, 5:6], 0.0).then_inc(merge_done, 1)
                merges.add(1)
                per = 2
                with Loop(dve, 4, (res, 4 * len(G) * per), (vs, 2 * per), (merges, per)) as i:
                    for m in range(per):
                        res.add(4 * len(G))
                        dve.wait_ge(acc_taken, res.now())
                        v(nc.vector.tensor_tensor(mg[:, 2, c], mg[:, 0, c], mg[:, 2, c], ALU.mult))
                        v(nc.vector.tensor_tensor(mg[:, 3, c], mg[:, 1, c], mg[:, 3, c], ALU.mult))
                        nc.vector.tensor_tensor(merged[:, bass.ds(i * per + m, 1), c].rearrange("p a n -> p (a n)"),
                                                mg[:, 2, c], mg[:, 3, c], ALU.add).then_inc(merge_done, 1)
                        merges.add(1)
                for k in range(DC):
                    low(merged[:, k, c], pair(m_hl)(k, c))
                per = 4 // len(G)
                with Loop(dve, DC // per, (res, 4)) as i:
                    for m in range(per):
                        for j, g in enumerate(G):
                            residual(evo[m * len(G) + j], g, i * per + m)

            def residual(buf, g, m):
                res.add()
                dve.wait_ge(acc_taken, res.now())
                if isinstance(m, int):
                    xm = x[:, m, g[0]:g[0] + g[1]]
                else:
                    xm = x[:, bass.ds(m, 1), g[0]:g[0] + g[1]].rearrange("p a n -> p (a n)")
                nc.vector.tensor_tensor(xm, xm, buf[:, 0:g[1]], ALU.add).then_inc(x_ready, 1)

            def conv(dst, u, n, w, b, taps, m):
                wc = lambda t: par[:, bass.ds(m + (w + t * taps), 1)]
                v(nc.vector.tensor_scalar(dst[:, 0:n], u[:, 0:n], wc(0), par[:, bass.ds(m + b, 1)], ALU.mult, ALU.add))
                v(nc.vector.scalar_tensor_tensor(dst[:, 0:n], u[:, 1:n + 1], wc(1), dst[:, 0:n], ALU.mult, ALU.add))
                return nc.vector.scalar_tensor_tensor(dst[:, 0:n], u[:, 2:n + 2], wc(2), dst[:, 0:n], ALU.mult, ALU.add)

            def ffn(l, n, c0, second, beside=False):
                if second:
                    gains, shift = (lambda k, g: col(f"norm2{l}", k)), None
                else:
                    j = slice(0, 1) if c0 == CTX else slice(1, 2)
                    gains_of(l, 1)
                    gains, shift = (lambda k, g: gain[:, 1, k, j]), (lambda k, g: mod[:, l, 3 * DC + k, j])
                norm([(DC, [(0, n)], D, lambda k, c: x[:, k, c0:c0 + n], gains, shift, pair(h2))], sumN, sqN, unN)
                for t in ua + ub:
                    pads = t[:, 0:2] if second else t[:, 0:n + 2:n + 1]
                    v(nc.vector.memset(pads, 0.0))
                w, b = COLS[f"conv_w_2{l}" if second else f"conv_w{l}"][0], COLS[f"conv_b_2{l}" if second else f"conv_b{l}"][0]
                taps = FC if second else 2 * FC
                with Loop(dve, FC // 2, (res, 4), (vs, 4 if second else 10), (silus, 2), (his, 2)) as i:
                    for j in range(2):
                        m = i * 2 + j
                        res.add()
                        dve.wait_ge(acc_taken, res.now())
                        conv(ca, ua[j], n, w, b, taps, m).then_inc(conv_done, 1)
                        res.add()
                        dve.wait_ge(acc_taken, res.now())
                        if second:
                            other = ub[j][:, 2:n + 2]
                        else:
                            v(conv(cb, ub[j], n, w + FC, b + FC, taps, m))
                            other = cb[:, 0:n]
                        silus.add()
                        dve.wait_ge(silu_done, silus.now())
                        nc.vector.tensor_tensor(cb[:, 0:n], sa[:, 0:n], other, ALU.mult).then_inc(full_ready, 1)
                        low(cb[:, 0:n], [g_hl[:, p, bass.ds(m, 1), 0:n].rearrange("p a n -> p (a n)") for p in range(2)])
                if not beside:
                    with Loop(dve, 2, (res, 4)) as i:
                        for m in range(4):
                            residual(evd[m], (c0, n), i * 4 + m)
                    return
                free_place()
                dve.wait_ge(c_ready, 3)
                for m in range(DC):
                    ada_tiles(2, m * ADA_PER_OUT, ADA_PER_OUT)
                    residual(evd[m % 4], (c0, n), m)
                add_bias(2, l + 1, 0, MODS)

            def angles():
                two_pi = 2 * math.pi
                big, c1 = 1.5 * 2.0 ** 23, 6.28125
                a, n, t = cos2[:, :], sin2[:, :], tmp[3][:, :]
                tables.add(32)
                dve.wait_ge(rope_in, tables.now())
                v(nc.vector.tensor_copy(a, pos[:, :]))
                v(nc.vector.tensor_scalar(a, a, col("inv_freq"), None, ALU.mult))
                v(nc.vector.tensor_scalar(n, a, 1.0 / two_pi, None, ALU.mult))
                v(nc.vector.tensor_scalar(n, n, big, None, ALU.add))
                v(nc.vector.tensor_scalar(n, n, -big, None, ALU.add))
                v(nc.vector.scalar_tensor_tensor(a, n, -c1, a, ALU.mult, ALU.add))
                v(nc.vector.scalar_tensor_tensor(a, n, -(two_pi - c1), a, ALU.mult, ALU.add))
                lim = 3.1415925
                nc.vector.tensor_scalar(n, a, lim, -lim, ALU.min, ALU.max).then_inc(ang_ready, 1)
                v(nc.vector.tensor_scalar(t, a, math.pi / 2, -two_pi, ALU.is_gt, ALU.mult))
                v(nc.vector.scalar_tensor_tensor(a, a, math.pi / 2, t, ALU.add, ALU.add))
                nc.vector.tensor_scalar(a, a, lim, -lim, ALU.min, ALU.max).then_inc(ang_ready, 1)

            def in2(l):
                norm([(DC, [(0, SEQ)], D, lambda k, c: x[:, k, CTX:TOK], lambda k, g: col(f"norm1{l}", k), None,
                       pair(h2))], sumN, sqN, unN)
                angles()
                v(nc.vector.memset(uc[:, :, 0:PAD], 0.0))
                dve.wait_ge(trig_ready, 2 * (l + 1))
                dsts = {"qa": qa, "ka": ka, "qi": qi}
                rope_results(IN2_EVENTS, lambda name: ki[:, :] if name == "ki" else dsts[name[0]][:, name[1], :],
                             lambda name: slice(0, P), rot2, (cos2, sin2))
                rots.add(11)
                res.add(3 * QT)

            def gla(l):
                dve.wait_ge(acc_taken, res.now())
                for wbuf in win:
                    v(nc.vector.memset(wbuf[:, :, 0:PAD], 0.0))
                last = uc
                for wbuf, width in zip(win, POOL_WINDOWS):
                    back = width // 2
                    v(nc.vector.tensor_tensor(wbuf[:, :, PAD:], last[:, :, PAD:], last[:, :, PAD - back:PAD + SEQ - back],
                                              ALU.add))
                    last = wbuf
                for g, wbuf in enumerate(win):
                    r, c = slice(64 * (g % 2), 64 * (g % 2) + 64), g // 2
                    v(nc.vector.tensor_tensor(tmp[c][r, :], wbuf[r, c, PAD:], cnt[r, c, :], ALU.mult))
                v(nc.vector.tensor_tensor(tmp[0][:, :], tmp[0][:, :], uc[:, 0, PAD:], ALU.subtract))
                nc.vector.tensor_tensor(tmp[1][:, :], tmp[1][:, :], uc[:, 1, PAD:], ALU.subtract).then_inc(pool_ready, 1)
                z = tmp[2][:, :]
                v(nc.vector.memset(ones2[:, :], 1.0))
                res.add()
                dve.wait_ge(gate_ln, l + 1)
                v(nc.vector.scalar_tensor_tensor(z, z, 0.0, tmp[3][:, :], ALU.min, ALU.subtract))
                v(nc.vector.tensor_tensor_scan(gcum[:, :], ones2[:, :], z, 0.0, ALU.mult, ALU.add))
                res.add(2)
                for lev, half in enumerate((256, 128, 64, 32, 16)):
                    b = 2 * half
                    view = lambda t: t.rearrange("p (n b) -> p n b", b=b)
                    cum = view(gcum[:, :])
                    if lev:
                        dve.wait_ge(lev_d, levels.now() + 2 * lev)
                    v(nc.vector.tensor_tensor(view(z), cum, cum[:, :, half - 1:half].to_broadcast([P, SEQ // b, b]),
                                              ALU.subtract))
                    limit = 0.0 if lev < 4 else -NEG
                    nc.vector.tensor_scalar(qd[:, lev, :], z, limit, None, ALU.min).then_inc(lev_d, 1)
                    nc.vector.tensor_scalar(kd[:, lev, :], z, -limit, None, ALU.max).then_inc(lev_d, 1)
                for lev in range(5):
                    levels.add(2)
                    dve.wait_ge(lev_e, levels.now())
                    nc.vector.scalar_tensor_tensor(qd[:, lev, :], qb[:, :], DK ** -0.5, qd[:, lev, :], ALU.mult, ALU.mult)\
                        .then_inc(qk_ready, 1)
                    nc.vector.tensor_tensor(kd[:, lev, :], kb[:, :], kd[:, lev, :], ALU.mult).then_inc(qk_ready, 1)
                t0, t1 = tmp[2], tmp[3]
                for h in range(GLA_HEADS):
                    heads.add()
                    dve.wait_ge(att_ready, heads.now())
                    blocks = lambda t: t.rearrange("p (j i) -> p j i", i=P)

                    def masked(dst, lev):
                        mask = col("gla_mask", (lev - 2) * P, P).unsqueeze(1).to_broadcast([P, QT, P])
                        v(nc.vector.tensor_tensor(blocks(dst[:, :]), blocks(ps[:, lev, :]), mask, ALU.mult))

                    masked(t0, 2)
                    masked(t1, 3)
                    v(nc.vector.tensor_tensor(t0[:, :], t0[:, :], t1[:, :], ALU.add))
                    masked(t1, 4)
                    for j in range(QT):
                        c = slice(j * P, (j + 1) * P)
                        ins = nc.vector.tensor_tensor(attT[:, j, c], t0[:, c], t1[:, c], ALU.add)
                    ins.then_inc(att_masked, 1)
                    outs.add()
                    dve.wait_ge(o_ready, outs.now())
                    r = (h % 2) * DV
                    nc.vector.tensor_copy(mix[r:r + DV, 4 + h // 2, :], ps[0:DV, 6 + h % 2, :]).then_inc(o_taken, 1)
                inverse([(1, [(0, SEQ)], DV)] * 2, sumG, None, heads=2)
                silus.add()
                dve.wait_ge(silu_done, silus.now())
                for k in range(2):
                    v(nc.vector.scalar_tensor_tensor(unG[k][:, 0:SEQ], mix[:, 4 + k, :], col(f"gla_g{l}", k),
                                                     spread(ACC_BANKS, k * QT, SEQ), ALU.mult, ALU.mult))
                    v(nc.vector.tensor_tensor(mix[:, 4 + k, :], unG[k][:, 0:SEQ], silu_r[:, k, :], ALU.mult))

            def dsa(l):
                tril, above = col("tril", 0, P), col("above", 0, P)
                v(nc.vector.tensor_copy(bias2[:, 0, 0:P], above))
                for t in range(1, QT):
                    nk = (t + 1) * P
                    diag = slice(t * P, nk)
                    for h in range(IDX_HEADS):
                        idx.add()
                        dve.wait_ge(relu_ready, idx.now())
                        r = relu[idx.n % 2][:, 0:nk]
                        if h == 0:
                            ins = nc.vector.tensor_scalar(score[:, 0:nk], r, wi[:, t, 0:1], None, ALU.mult)
                        else:
                            ins = nc.vector.scalar_tensor_tensor(score[:, 0:nk], r, wi[:, t, h:h + 1], score[:, 0:nk],
                                                                 ALU.mult, ALU.add)
                        ins.then_inc(score_step, 1)
                        dve.wait_ge(score_step, idx.now())
                    v(nc.vector.tensor_tensor(score[:, diag], score[:, diag], tril, ALU.mult))
                    v(nc.vector.tensor_tensor(score[:, diag], score[:, diag], above, ALU.add))
                    src = score
                    for _ in range(TOPK // 8):
                        v(nc.vector.max(top8[:, :], src[:, 0:nk]))
                        v(nc.vector.match_replace(work[:, 0:nk], top8[:, :], src[:, 0:nk], TAKEN))
                        src = work
                    b = bias2[:, t, 0:nk]
                    v(nc.vector.tensor_scalar(b, work[:, 0:nk], TAKEN, -NEG, ALU.is_equal, ALU.mult))
                    v(nc.vector.tensor_scalar(b, b, NEG, None, ALU.add))
                    v(nc.vector.tensor_tensor(bias2[:, t, diag], bias2[:, t, diag], above, ALU.add))

                def maxima(i):
                    h, t = ITEMS_2[i]
                    nk, st = (t + 1) * P, stat[:, i % 2, :]
                    dve.wait_ge(s_ready, maps.now() + i + 1)
                    v(nc.vector.tensor_tensor_reduce(out=p2[i % 2][:, 0:nk], in0=ps[:, i % 4, 0:nk], in1=bias2[:, t, 0:nk],
                                                     scale=1.0, scalar=TAKEN, op0=ALU.add, op1=ALU.max,
                                                     accum_out=st[:, 6:7]))
                    nc.vector.tensor_scalar(st[:, 0:1], st[:, 6:7], -HD ** -0.5, None, ALU.mult).then_inc(s_max, 1)

                def normalise(i):
                    nk, st = (ITEMS_2[i][1] + 1) * P, stat[:, i % 2, :]
                    dve.wait_ge(p_ready, maps.now() + i + 1)
                    v(nc.vector.reciprocal(st[:, 4:5], st[:, 2:3]))
                    nc.vector.tensor_scalar(p2[i % 2][:, 0:nk], p2[i % 2][:, 0:nk], st[:, 4:5], None, ALU.mult)\
                        .then_inc(p_normed, 1)

                def output(i, bank):
                    h, t = ITEMS_2[i]
                    r = (h % 2) * HD
                    return nc.vector.tensor_copy(mix[r:r + HD, h // 2, t * P:(t + 1) * P], ps[0:HD, bank, 0:P])

                attend(len(ITEMS_2), maxima, normalise, output)
                maps.add(len(ITEMS_2))

            def mixed2(l):
                for k in range(DC):
                    low(mix[:, k, :], (mix_hl[:, 0, k, :], mix_hl[:, 1, k, :]))
                with Loop(dve, 2, (res, 4)) as i:
                    for m in range(4):
                        residual(evo2[m], (CTX, SEQ), i * 4 + m)

            for l in range(LAYERS):
                if l == 0:
                    start()
                if on(f"mla{l}"):
                    mla(l)
                if on(f"attna{l}"):
                    attn_a(l)
                if on(f"diff{l}"):
                    diff(l)
                if on(f"attnb{l}"):
                    attn_b(l)
                if on(f"mixed{l}"):
                    mixed(l)
                if on(f"ffn{l}"):
                    ffn(l, SEQ, CTX, False, beside=l == 0)
                if l == 0 and on("ffn0c"):
                    ffn(l, CTX, 0, False)
            if on("first"):
                normed_in_place(x_ready)
            for l in range(LAYERS):
                if on(f"in2{l}"):
                    in2(l)
                if on(f"gla2{l}"):
                    gla(l)
                if on(f"dsa2{l}"):
                    dsa(l)
                if on(f"mixed2{l}"):
                    mixed2(l)
                if on(f"ffn2{l}"):
                    ffn(l, SEQ, CTX, True)
            if on("final"):
                normed_in_place(final_ready)


def columns(v):
    return np.ascontiguousarray(v).reshape(-1, P).T


def swap_matrix(dims, q, per, offset=0):
    m = np.zeros((P, P), np.float32)
    for b in range(offset, P, per):
        for base in range(0, dims, 2 * q):
            for j in range(q):
                if b + base + q + j < P:
                    m[b + base + q + j, b + base + j] = -1.0
                    m[b + base + j, b + base + q + j] = 1.0
    return m


def axial_table(dims, per, offset):
    q = dims // 4
    freqs = (ROPE_BASE ** (-np.arange(q, dtype=np.float32) / q)).astype(np.float32)
    t = np.arange(SEQ)
    where = ((t // GRID_W).astype(np.float32), (t % GRID_W).astype(np.float32))
    tab = np.zeros((P, 2, SEQ), np.float32)
    tab[:, 0] = 1.0
    for b in range(offset, P, per):
        for d in range(dims):
            if b + d < P:
                ang = where[d // (2 * q)] * freqs[d % q]
                tab[b + d, 0], tab[b + d, 1] = np.cos(ang), np.sin(ang)
    return tab


def constants():
    c = {"ident": np.eye(P), "ones": np.ones((P, P)), "zero": np.zeros((P, 1))}
    i = np.arange(P)
    c["headsum"] = (i[:, None] // DV == i[None, :] // DV) * 1.0
    c["perm_a"] = swap_matrix(ROPE_A, ROPE_A // 4, P, NOPE)
    c["perm_b"] = swap_matrix(DH_B, DH_B // 4, DH_B)
    c["perm_2"] = swap_matrix(ROT, ROT // 2, HD)
    c["tril"] = (i[None, :] <= i[:, None]) * 1.0
    c["above"] = np.where(i[None, :] <= i[:, None], 0.0, NEG)
    j, q = i[:, None], i[None, :]
    masks = [(j // (2 * half) == q // (2 * half)) & (q % (2 * half) >= half) & (j % (2 * half) < half) for half in (64, 32)]
    masks.append((j // 32 == q // 32) & (j <= q))
    c["gla_mask"] = np.concatenate(masks, 1) * 1.0
    inv = (ROPE_THETA ** (-np.arange(0, ROT, 2, dtype=np.float32) / ROT)).astype(np.float32)
    f = np.zeros((P, 1), np.float32)
    for b in range(0, P, HD):
        f[b:b + ROT, 0] = np.tile(inv, 2)
    c["inv_freq"] = f
    return c


def pack_params(a):
    par = np.zeros((P, NCOLS), np.float32)

    def put(name, v):
        o, w = COLS[name]
        par[0:v.shape[0], o:o + w] = v

    twice = lambda v: np.repeat(columns(v), 2, axis=1)
    for l in range(LAYERS):
        put(f"b_ada{l}", columns(a["b_ada"][l]))
        put(f"g_mix{l}", twice(a["g_mix"][l]))
        put(f"g_ffn{l}", twice(a["g_ffn"][l]))
        put(f"conv_w{l}", columns(a["conv_w"][l]))
        put(f"conv_b{l}", columns(a["conv_b"][l]))
        put(f"g_q{l}", columns(a["g_q"][l]))
        put(f"g_kv{l}", columns(a["g_kv"][l]))
        put(f"g_sub{l}", columns(a["g_sub"][l]))
        put(f"lam{l}", np.stack([a[f"lam_{n}"][l] for n in ("q1", "q2", "k1", "k2")], 1))
        put(f"norm1{l}", columns(a["norm1_g_2"][l]))
        put(f"norm2{l}", columns(a["norm2_g_2"][l]))
        put(f"conv_w_2{l}", columns(a["conv_w_2"][l]))
        put(f"conv_b_2{l}", columns(a["conv_b_2"][l]))
        put(f"b_gate{l}", columns(a["b_gate_2"][l]))
        put(f"gla_g{l}", columns(a["gla_norm_g_2"][l]))
        put(f"pool_scale{l}", columns(a["pool_scale_2"][l]))
        put(f"w_gate{l}", a["w_gate_up_2"][l])
        wp = np.zeros((2, P, P), np.float32)
        for g in range(4):
            r = slice(64 * (g % 2), 64 * (g % 2) + 64)
            wp[g // 2, r, r] = a["w_pool_2"][l, g]
        put(f"w_pool{l}", wp.transpose(1, 0, 2).reshape(P, -1))
    put("g_final", columns(a["g_final"]))
    put("final_g", columns(a["final_norm_g_2"]))
    for name, v in constants().items():
        put(name, np.asarray(v, np.float32))
    return par


def weight_stream(a):
    stream = np.zeros((N_SLABS, P, SLAB_TILES, P), np.float32)
    at = [0]

    def slab(tiles):
        for j, t in enumerate(tiles):
            stream[at[0], :, j, 0:t.shape[1]] = t
        at[0] += 1

    def rows(w, cols):
        return [w[k * P:(k + 1) * P, cols] for k in range(w.shape[0] // P)]

    def span(c0, n=P):
        return slice(c0, c0 + n)

    def by_k(w, c0, n, slabs):
        per = DC // slabs
        for s in range(slabs):
            slab([w[k * P:(k + 1) * P, span(c0 + j * P)] for k in range(s * per, (s + 1) * per) for j in range(n // P)])

    def ffn(up, down):
        for m in range(FC):
            slab(rows(up, span(m * P)))
            slab(rows(up, span(F + m * P)))
        for m in range(DC):
            t = rows(down, span(m * P))
            for k in range(0, FC, SLAB_TILES):
                slab(t[k:k + SLAB_TILES])

    for l in range(LAYERS):
        w = a["w_in"][l]
        for m in range((Q_LORA + KV_LORA) // P):
            slab(rows(w, span(m * P)))
        slab(rows(w, span(Q_LORA + KV_LORA - NOPE)))
        for h in range(0, H_A, 2):
            slab(rows(a["w_uq"][l], span(h * QK_A, QK_A)) + rows(a["w_uq"][l], span((h + 1) * QK_A, QK_A)))
        ukv = a["w_ukv"][l].reshape(KV_LORA, H_A, NOPE + V_A)
        kn = np.ascontiguousarray(ukv[:, :, 0:NOPE]).reshape(KV_LORA, -1)
        vv = np.ascontiguousarray(ukv[:, :, NOPE:]).reshape(KV_LORA, -1)
        slab([t for j in range(H_A // 2) for t in rows(kn, span(j * P))])
        slab([vv[k * P:(k + 1) * P, span(j * P)] for k in range(2) for j in range(4)])
        c0 = Q_LORA + KV_LORA + ROPE_A
        for m in range(2 * H_B):
            slab(rows(w, span(c0 + m * P)))
        by_k(w, c0 + 2 * H_B * P, H_B * P, 4)
        c0 += 3 * H_B * P
        for m in range(DC):
            slab(rows(w, span(c0 + m * P)))
            slab(rows(w, span(c0 + D + m * P)))
            slab(rows(a["w_br_a"][l], span(m * P)) + rows(a["w_br_b"][l], span(m * P)))
        for m in range(DC):
            slab(rows(a["w_out"][l], span(m * P)))
        for _ in range(2 if l == 0 else 1):
            ffn(a["w_up"][l], a["w_down"][l])
    for l in range(LAYERS):
        w = a["w_in_2"][l]
        for m in range(8):
            slab(rows(w, span(m * P)))
        for m in range(2):
            slab(rows(w, span(1536 + m * P)))
        slab([np.concatenate([t, t], 1) for t in rows(w, span(1792, IDX_D))])
        for c0 in (1860, 1988, 2372, 2500, 2644, 2772):
            slab(rows(w, span(c0)))
        slab(rows(w, span(2628, GATE_RANK)))
        by_k(w, 1024, 512, 4)
        by_k(w, 2116, 256, 2)
        slab(rows(w, span(1856, IDX_HEADS)))
        for m in range(DC):
            slab(rows(a["w_out_2"][l], span(m * P)))
        ffn(a["w_up_2"][l], a["w_down_2"][l])
    assert at[0] == USED_SLABS, (at[0], USED_SLABS)
    return stream.reshape(N_SLABS, P, SLAB)


IDX_D = 64


def tokens_last(v):
    return np.ascontiguousarray(v.T.reshape(DC, P, -1).transpose(1, 0, 2))


def host_inputs(a):
    count = np.minimum(np.arange(SEQ)[None, :] + 1, np.array(POOL_WINDOWS)[:, None]).astype(np.float32)
    cnt = np.repeat(np.float32(1.0) / count, 64, axis=0).reshape(2, P, SEQ).transpose(1, 0, 2)
    return {
        "wstream": weight_stream(a),
        "ada_w": np.ascontiguousarray(a["w_ada"].transpose(0, 2, 1)).reshape(LAYERS * MODS, P, D),
        "c_in": np.ascontiguousarray(np.broadcast_to(np.stack([a["c"][0], a["c_ctx"]]), (P, 2, D))),
        "params": pack_params(a),
        "x_in": tokens_last(np.concatenate([a["ctx"][0], a["x"][0]], 0)),
        "rope_tab": np.concatenate([axial_table(ROPE_A, P, NOPE), axial_table(DH_B, DH_B, 0)], 1),
        "pos_in": np.ascontiguousarray(np.broadcast_to(a["positions_2"], (P, SEQ))),
        "cnt_in": np.ascontiguousarray(cnt),
    }


def program(nc, arrays, stop=None):
    args = [nc.dram_tensor(name, v.shape, mybir.dt.from_np(v.dtype), kind="ExternalInput").ap()
            for name, v in arrays.items()]
    out = nc.dram_tensor("out_0", (P, DC, SEQ), F32, kind="ExternalOutput").ap()
    build(nc, *args, out, stop=stop)


def kernel(**inputs):
    import concourse.bacc as bacc
    from concourse.bass_utils import run_bass_kernel_spmd

    nc = bacc.Bacc("TRN2", target_bir_lowering=False, num_devices=1)
    arrays = host_inputs({k: np.asarray(v) for k, v in inputs.items()})
    program(nc, arrays)
    r = run_bass_kernel_spmd(nc, [arrays], core_ids=[0])
    got = r.results[0]["out_0"]
    return np.ascontiguousarray(got.transpose(1, 0, 2).reshape(D, SEQ).T).reshape(1, SEQ, D)
```

```python
import math

import numpy as np
import concourse.bass as bass
import concourse.mybir as mybir
from concourse.alu_op_type import AluOpType as ALU

P = 128
D = 1024
DC = D // P
CTX, SEQ = 256, 512
TOK = CTX + SEQ
LAYERS = 2
EPS = 1e-6

H_A, NOPE, ROPE_A, V_A = 8, 64, 32, 64
QK_A = NOPE + ROPE_A
Q_LORA, KV_LORA = 384, 256
H_B, DH_B = 4, 64
F = 2816
FC = F // P
GRID_W = 64
ROPE_BASE = 10000.0
MODS = 6 * DC

HEADS, HD = 8, 64
IDX_HEADS = 4
TOPK = min(256, SEQ // 4)
IDX_SCALE = (HD ** -0.5) * (IDX_HEADS ** -0.5)
ROPE_THETA, ROT = 500000.0, 16
GLA_HEADS, DK, DV = 4, 32, 64
GATE_RANK, GATE_TAU = 16, 16.0
POOL_WINDOWS = (2, 4, 8, 16)
PAD = max(POOL_WINDOWS)
HALVES = (256, 128, 64, 32, 16)
QT = SEQ // P

NORM_BANK = 7
TILE_COLS = P
SLAB_TILES = 8
SLAB = SLAB_TILES * TILE_COLS
RAW_SLOTS, SPLIT_SLOTS = 4, 2
ACC_BANKS = 4
NEG = -1e30
TAKEN = -3e38
BANK = 512

F32, F32R, I32 = mybir.dt.float32, mybir.dt.float32r, mybir.dt.int32
ACT = mybir.ActivationFunctionType
AX = mybir.AxisListType


def lam_init(l):
    return 0.8 - 0.6 * math.exp(-0.3 * l)


def param_columns():
    at, n = {}, 0
    for name, width in (
        [(f"{name}{l}", w) for l in range(LAYERS) for name, w in (
            ("b_ada", MODS), ("g_mix", 2 * DC), ("g_ffn", 2 * DC), ("conv_w", 3 * 2 * FC), ("conv_b", 2 * FC),
            ("g_q", Q_LORA // P), ("g_kv", KV_LORA // P), ("g_sub", 1), ("lam", 4))]
        + [("g_final", DC)]
        + [(f"{name}{l}", w) for l in range(LAYERS) for name, w in (
            ("norm1", DC), ("norm2", DC), ("conv_w_2", 3 * FC), ("conv_b_2", FC), ("b_gate", 1), ("gla_g", 2),
            ("pool_scale", 2), ("w_gate", P), ("w_pool", 2 * P))]
        + [("final_g", DC), ("ident", P), ("ones", P), ("headsum", P), ("perm_a", P), ("perm_b", P),
           ("perm_2", P), ("tril", P), ("above", P), ("gla_mask", 3 * P), ("inv_freq", 1), ("zero", 1)]):
        at[name] = (n, width)
        n += width
    return at, n


COLS, NCOLS = param_columns()

LORA_SLABS, UP_A_SLABS = 6, H_A // 2 + 1 + 1
DIFF_SLABS = 12
MERGE_SLABS, OUT_SLABS = 3 * DC, DC
FFN_SLABS = 2 * FC + 3 * DC
HALF = FC // 2
BOTH_DOWN = HALF * DC // SLAB_TILES
BOTH_SLABS = 2 * (2 * HALF + BOTH_DOWN)
APART = CTX + 2
WIDE = APART + SEQ
IN2_SLABS = 18 + 4 + 2 + 1
USED_SLABS = (LAYERS * (LORA_SLABS + UP_A_SLABS + DIFF_SLABS + MERGE_SLABS + OUT_SLABS)
              + BOTH_SLABS + FFN_SLABS + LAYERS * (IN2_SLABS + OUT_SLABS + FFN_SLABS))
N_SLABS = -(-USED_SLABS // RAW_SLOTS) * RAW_SLOTS
ADA_GROUPS = ([(0, m) for m in range(2 * DC)], [(0, m) for m in range(2 * DC, MODS)],
              [(1, m) for m in range(2 * DC, MODS)], [(1, m) for m in range(2 * DC)])
ADA_VECTORS = (2, 2, 1, 2)
ADA_SLOTS = (16, 3, 2, 4)
ADA_PER_SLAB = 4
DIFF_AT = LORA_SLABS + UP_A_SLABS
DOWN_AT = [DIFF_AT + DIFF_SLABS + MERGE_SLABS + OUT_SLABS + 2 * HALF + half * (2 * HALF + BOTH_DOWN) for half in range(2)]


def ada_before(group):
    return sum(map(len, ADA_GROUPS[:group]))


def ada_loads(group, slot):
    return sum(len(range(slot, len(tiles), slots)) for tiles, slots in zip(ADA_GROUPS[:group], ADA_SLOTS) if slot < slots)


class Count:

    def __init__(self, n=0):
        self.n, self.i, self.per = n, None, 0

    def add(self, k=1):
        self.n += k
        return self

    def now(self, back=0, times=1):
        v = (self.n - back) * times
        return v if self.i is None else self.i * (self.per * times) + v

    def enter(self, i, per):
        self.i, self.per, self.start = i, per, self.n

    def leave(self, turns):
        assert self.n == self.start + self.per, (self.n, self.start, self.per)
        self.i, self.n = None, self.start + self.per * turns


class Loop:

    def __init__(self, eng, turns, *counts):
        self.fori, self.turns, self.counts = eng.Fori(0, turns), turns, counts

    def __enter__(self):
        i = self.fori.__enter__()
        for c, per in self.counts:
            c.enter(i, per)
        return i

    def __exit__(self, *e):
        self.fori.__exit__(*e)
        for c, _ in self.counts:
            c.leave(self.turns)


def groups_of(l):
    return [(0, CTX), (CTX, SEQ)] if l == 0 else [(CTX, SEQ)]


BOTH = [(0, CTX), (CTX, SEQ)]
LAT = [(CTX, SEQ)]


def roped(tiles):
    events, pending = [], None
    for name, groups, rope in tiles:
        events += [("gemm", name, g) for g in groups]
        if pending is not None:
            events.append(("rot", pending, None))
        pending = name if rope else None
    if pending is not None:
        events.append(("rot", pending, None))
    return events


def lora_events(l):
    return roped([(("cq", m), groups_of(l), False) for m in range(3)]
                 + [(("ckv", m), BOTH, False) for m in range(2)] + [("kr", BOTH, True)])


def up_events(l):
    return (roped([(("q", h), groups_of(l), True) for h in range(H_A)])
            + [("gemm", ("kn", j), g) for j in range(H_A // 2) for g in BOTH])


def diff_events(l):
    return roped([(("dq", m), groups_of(l), True) for m in range(H_B)]
                 + [(("dk", m), BOTH, True) for m in range(H_B)])


def indexed(t):
    return [("idx", (t, h), None) for h in range(IDX_HEADS)]


def plain(*names):
    return [("gemm", name, g) for name in names for g in LAT]


IN2_INDEX = roped([(("qi", m), LAT, True) for m in range(2)] + [("ki", LAT, True)])
IN2_PLAIN = (plain("qb") + indexed(1) + plain("kb", ("rb", 0)) + indexed(2) + plain(("rb", 1), ("uc", 0), ("uc", 1))
             + indexed(3) + plain("gl"))
IN2_ROPED = roped([((name, m), LAT, True) for name in ("qa", "ka") for m in range(HEADS * HD // P)])
INDEX_ROTS, IN2_ROTS = 3, 3 + 2 * HEADS * HD // P


def items_a(l, heads):
    return [(h, CTX + P * t, TOK) for h in range(heads) for t in range(QT)] + (
        [(h, P * t, CTX) for h in range(heads) for t in range(CTX // P)] if l == 0 else [])


ITEMS_2 = [(h, t) for t in range(QT) for h in range(HEADS)]


def build(nc, wstream, ada_w, c_in, params, x_in, rope_tab, pos_in, cnt_in, out):
    from contextlib import ExitStack

    ctx = ExitStack()
    with ctx:
        top = [16512]

        def sb(name, shape, dt=F32, at=None):
            n = 4 * int(np.prod(shape[1:]))
            n = -(-n // 32) * 32
            if at is None:
                at = top[0]
                top[0] += n
            assert at + n <= 229344, (name, at + n)
            return nc.alloc_sbuf_tensor_at(name, shape, dt, offset=at)

        raw = sb("raw", [P, RAW_SLOTS, SLAB])
        split = sb("split", [P, SPLIT_SLOTS, 2, SLAB], F32R)
        x = sb("x", [P, DC, TOK])
        par = sb("par", [P, NCOLS])
        mod = sb("mod", [P, LAYERS, MODS, 2])
        gain = sb("gain", [P, 2, DC, 2])
        lam_p = sb("lam_p", [P, LAYERS, 2])
        lam_e = sb("lam_e", [P, LAYERS, 2])
        neg_lam = sb("neg_lam", [P, LAYERS])
        ms = sb("ms", [P, 24])
        rstd = sb("rstd", [P, 24])
        newton = sb("newton", [P, 24])
        gsub = sb("gsub", [P, 1])
        stat = sb("stat", [P, 2, 8])
        PH = top[0]
        KB = 1024

        def ph(name, kb, shape, dt=F32):
            return sb(name, shape, dt, at=PH + int(kb * KB))

        FW = 48 + -(-2 * HALF * WIDE * 4 // 32) * 32 / KB
        ada_c = [ph(f"ada_c{i}", a, [P, ADA_VECTORS[i], D]) for i, a in enumerate((0, 48 + 81, FW, 0))]
        ada_t = [[ph(f"ada_t{i}{j}", a + 4 * j, [P, D]) for j in range(ADA_SLOTS[i])]
                 for i, a in enumerate((8, 48 + 63, FW + 4, 8))]
        h_hl = ph("h_hl", 0, [P, 2, DC, TOK], F32R)
        M = 48
        qA = ph("qA", M, [P, H_A, TOK])
        cq = ph("cq", M + 24, [P, 3, TOK])
        cq_hl = ph("cq_hl", M + 33, [P, 2, 3, TOK], F32R)
        kA = ph("kA", M + 24, [P, H_A, TOK])
        vA = ph("vA", M + 51, [P, TOK // P, H_A * V_A])
        ckv_hl = ph("ckv_hl", M + 63, [P, 2, 2, TOK], F32R)
        oA = ph("oA", M + 63, [P, 4, TOK])
        ckv = ph("ckv", M + 75, [P, 2, TOK])
        ropeA = ph("ropeA", M + 81, [P, 2, SEQ])
        kr = ph("kr", M + 85, [P, TOK])
        rot = [ph(f"rot{i}", a, [P, SEQ]) for i, a in ((0, M + 51), (1, M + 88))]
        pA = [ph(f"pA{i}", M + 75 + 3 * i, [P, TOK]) for i in range(2)]
        pT = ph("pT", M + 87, [P, TOK])
        oA_hl = ph("oA_hl", M, [P, 2, 4, TOK], F32R)
        dq = ph("dq", M + 24, [P, H_B, TOK])
        dk = ph("dk", M + 36, [P, H_B, TOK])
        ropeB = ph("ropeB", M + 75, [P, 2, SEQ])
        rotB = [ph(f"rotB{i}", a, [P, SEQ]) for i, a in ((0, M + 79), (1, M + 60))]
        vB = ph("vB", M + 48, [P, TOK // P, H_B * P])
        oB = ph("oB", M + 63, [P, H_B, TOK])
        pB = [ph(f"pB{i}", M + 75 + 3 * i, [P, TOK]) for i in range(4)]
        sumB = [ph(f"sumB{i}", M + 48 + 3 * i, [P, TOK]) for i in range(H_B)]
        unB = [ph(f"unB{i}", M + 81 + 3 * i, [P, TOK]) for i in range(2)]
        oB_hl = ph("oB_hl", M + 24, [P, 2, 4, TOK], F32R)
        merged = ph("merged", M + 48, [P, DC, TOK])
        mg = ph("mg", M + 72, [P, 4, TOK])
        m_hl = ph("m_hl", 0, [P, 2, DC, TOK], F32R)
        evo = [ph(f"evo{i}", M + 2 * i, [P, SEQ]) for i in range(4)]
        sumN = [ph(f"sumN{i}", M + 15 * i, [P, TOK]) for i in range(2)]
        sqN = [ph(f"sqN{i}", M + 3 + 3 * i, [P, TOK]) for i in range(2)]
        unN = [ph(f"unN{i}", M + 9 + 3 * i, [P, TOK]) for i in range(2)]
        h2 = ph("h2", 0, [P, 2, DC, SEQ], F32R)
        g_hl = ph("g_hl", 32, [P, 2, FC, SEQ], F32R)
        FT = 32 + 2 * FC * 2
        ua = [ph(f"ua{i}", FT + 2.0625 * i, [P, SEQ + 2]) for i in range(2)]
        ub = [ph(f"ub{i}", FT + 4.125 + 2.0625 * i, [P, SEQ + 2]) for i in range(2)]
        ca = ph("ca", FT + 8.25, [P, SEQ])
        cb = ph("cb", FT + 10.25, [P, SEQ])
        sa = ph("sa", FT + 12.25, [P, SEQ])
        evd = [ph(f"evd{i}", FT + 2 * i, [P, SEQ]) for i in range(4)]
        h2w = ph("h2w", 0, [P, 2, DC, TOK], F32R)
        gw_hl = ph("gw_hl", 48, [P, 2, HALF, WIDE], F32R)
        uaw, ubw = ([ph(f"{n}{i}", FW + (2 * i + j) * 3.0625, [P, WIDE + 2]) for i in range(2)]
                    for j, n in enumerate(("uaw", "ubw")))
        caw, cbw, saw = (ph(n, FW + 12.25 + 3.03125 * j, [P, WIDE]) for j, n in enumerate(("caw", "cbw", "saw")))
        evw = [ph(f"evw{i}", FW + 12.25 + 2 * i, [P, SEQ]) for i in range(4)]
        qa = ph("qa", 32, [P, 4, SEQ])
        ka = ph("ka", 40, [P, 4, SEQ])
        va = ph("va", 48, [P, QT, 512])
        qi = ph("qi", 56, [P, 2, SEQ])
        ki = ph("ki", 60, [P, SEQ])
        qb = ph("qb", 62, [P, SEQ])
        kb = ph("kb", 64, [P, SEQ])
        vb = ph("vb", 66, [P, QT, 256])
        rb = ph("rb", 70, [P, 2, SEQ])
        uc = ph("uc", 74, [P, 2, PAD + SEQ])
        gl = ph("gl", 78.5, [P, SEQ])
        wi = ph("wi", 80.5, [P, QT, IDX_HEADS])
        cos2 = ph("cos2", 81, [P, SEQ])
        sin2 = ph("sin2", 83, [P, SEQ])
        bias2 = ph("bias2", 86, [P, QT, SEQ])
        score = ph("score", 94, [P, SEQ])
        work = ph("work", 96, [P, SEQ])
        relu = [ph(f"relu{i}", 98 + 2 * i, [P, SEQ]) for i in range(IDX_HEADS)]
        qd = ph("qd", 102, [P, 5, SEQ])
        kd = ph("kd", 112, [P, 5, SEQ])
        attT = [ph(f"attT{i}", a, [P, QT, SEQ]) for i, a in enumerate((122, 94))]
        tmp = [ph(f"tmp{i}", 130 + 2 * i, [P, SEQ]) for i in range(4)]
        pos = ph("pos", 86, [P, SEQ], I32)
        win = [ph(f"win{i}", 102 + 4.125 * i, [P, 2, PAD + SEQ]) for i in range(4)]
        cnt = ph("cnt", 122, [P, 2, SEQ])
        rot2 = [ph(f"rot2{i}", 126 + 2 * i, [P, SEQ]) for i in range(2)]
        gcum = ph("gcum", 94, [P, SEQ])
        ones2 = ph("ones2", 96, [P, SEQ])
        mix = ph("mix", 0, [P, DC, SEQ])
        sumG = [ph(f"sumG{i}", 102 + 3 * i, [P, TOK]) for i in range(2)]
        unG = [ph(f"unG{i}", 114 + 3 * i, [P, TOK]) for i in range(2)]
        silu_r = ph("silu_r", 120, [P, 2, SEQ])
        p2 = [ph(f"p2{i}", 102 + 2 * i, [P, SEQ]) for i in range(2)]
        pT2 = ph("pT2", 106, [P, SEQ])
        top8 = ph("top8", 108, [P, 8])
        mix_hl = ph("mix_hl", 32, [P, 2, DC, SEQ], F32R)
        evo2 = [ph(f"evo2{i}", 64 + 2 * i, [P, SEQ]) for i in range(4)]
        ps = ctx.enter_context(nc.psum_tensor("ps", [P, 8, BANK], F32))

        def col(name, j=0, w=1, rows=slice(0, P)):
            a, _ = COLS[name]
            return par[rows, a + j:a + j + w]

        def banks(b, n):
            return ps[:, b:b + 2, :].rearrange("p b n -> p (b n)")[:, 0:n]

        def sem(name):
            return ctx.enter_context(nc.semaphore(name))

        loaded = sem("loaded")
        raw_ready = [sem(f"raw_ready{i}") for i in range(RAW_SLOTS)]
        split_done = sem("split_done")
        slab_used = sem("slab_used")
        acc_ready = sem("acc_ready")
        ada_space = sem("ada_space")
        c_loaded = sem("c_loaded")
        c_ready = sem("c_ready")
        ada_ready = [sem(f"ada_ready{i}") for i in range(max(ADA_SLOTS))]
        ada_used = sem("ada_used")
        mod_ready = sem("mod_ready")
        v_lam = sem("v_lam")
        acc_taken = sem("acc_taken")
        sq_ready = sem("sq_ready")
        sq_summed = sem("sq_summed")
        sums_ready = sem("sums_ready")
        var_ready = sem("var_ready")
        root_ready = sem("root_ready")
        rstd_ready = sem("rstd_ready")
        rstd_spread = sem("rstd_spread")
        full_ready = sem("full_ready")
        hi_ready = sem("hi_ready")
        hl_ready = sem("hl_ready")
        v_step = sem("v_step")
        a_step = sem("a_step")
        x_ready = sem("x_ready")
        rot_done = sem("rot_done")
        rope_in = sem("rope_in")
        conv_done = sem("conv_done")
        silu_done = sem("silu_done")
        merge_done = sem("merge_done")
        s_ready = sem("s_ready")
        s_max = sem("s_max")
        p_ready = sem("p_ready")
        p_normed = sem("p_normed")
        t_ready = sem("t_ready")
        t_taken = sem("t_taken")
        o_ready = sem("o_ready")
        o_taken = sem("o_taken")
        gate_ln = sem("gate_ln")
        lev_d = sem("lev_d")
        lev_e = sem("lev_e")
        qk_ready = sem("qk_ready")
        att_ready = sem("att_ready")
        att_off = sem("att_off")
        att_read = sem("att_read")
        att_masked = sem("att_masked")
        ang_ready = sem("ang_ready")
        trig_ready = sem("trig_ready")
        idx_ready = sem("idx_ready")
        relu_ready = sem("relu_ready")
        score_step = sem("score_step")
        pool_ready = sem("pool_ready")
        stored = sem("stored")
        final_ready = sem("final_ready")

        block = ctx.enter_context(nc.Block())

        @block.sync
        def _(sp):
            def load(turn, s):
                sp.dma_start(raw[:, s, :], wstream[bass.ds(turn * RAW_SLOTS + s, 1)].rearrange("a p n -> (a p) n"))\
                    .then_inc(raw_ready[s], 16)

            def reload(turn, s):
                sp.wait_ge(split_done, turn * (2 * RAW_SLOTS) + 2 * (s + 1 - RAW_SLOTS))
                load(turn, s)

            def load_turns(first, end):
                with sp.Fori(first, end) as i:
                    for s in range(RAW_SLOTS):
                        reload(i, s)

            def load_c(group):
                if group:
                    sp.wait_ge(ada_space, group)
                sp.dma_start(ada_c[group][:, :, :], c_in[:, 0:ADA_VECTORS[group], :]).then_inc(c_loaded, 16)

            def load_tile(group, n):
                slots, first = ADA_SLOTS[group], ada_before(group)
                if n >= slots:
                    sp.wait_ge(ada_used, first + n - slots + 1)
                sp.dma_start(ada_t[group][n % slots][:, :], ada_w[first + n]).then_inc(ada_ready[n % slots], 16)

            load_c(0)
            for n in range(len(ADA_GROUPS[0])):
                load_tile(0, n)
            sp.dma_start(par[:, :], params).then_inc(loaded, 16)
            sp.dma_start(x[:, :, :], x_in).then_inc(loaded, 16)
            for s in range(RAW_SLOTS):
                load(0, s)
            load_turns(1, DIFF_AT // RAW_SLOTS + 1)
            n = 0
            for turn in range(DIFF_AT // RAW_SLOTS + 1, (DIFF_AT + DIFF_SLABS) // RAW_SLOTS):
                for s in range(RAW_SLOTS):
                    reload(turn, s)
                    if n == 0:
                        load_c(1)
                    for _ in range(ADA_PER_SLAB):
                        load_tile(1, n)
                        n += 1
            assert n == len(ADA_GROUPS[1])
            end = DIFF_AT + DIFF_SLABS
            for group, first in ((2, DOWN_AT[0]), (3, DOWN_AT[1])):
                load_turns(end // RAW_SLOTS, first // RAW_SLOTS)
                ahead, tiles, n = first + RAW_SLOTS, len(ADA_GROUPS[group]), 0
                end = -(-(ahead + BOTH_DOWN) // RAW_SLOTS) * RAW_SLOTS
                for g in range(first // RAW_SLOTS * RAW_SLOTS, end):
                    reload(g // RAW_SLOTS, g % RAW_SLOTS)
                    if g == ahead:
                        load_c(group)
                    if g >= ahead:
                        for _ in range(min(-(-tiles // BOTH_DOWN), tiles - n)):
                            load_tile(group, n)
                            n += 1
                assert n == tiles
            load_turns(end // RAW_SLOTS, N_SLABS // RAW_SLOTS)
            sp.wait_ge(final_ready, DC)
            sp.dma_start(out, x[:, :, CTX:TOK]).then_inc(stored, 16)
            sp.wait_ge(stored, 16)

        @block.gpsimd
        def _(pool):
            zero = col("zero").to_broadcast([P, SLAB])

            def split_slab(s, turn, first_use):
                n = turn * RAW_SLOTS + s
                hi, lo = split[:, s % SPLIT_SLOTS, 0, :], split[:, s % SPLIT_SLOTS, 1, :]
                pool.wait_ge(raw_ready[s], turn * 16 + 16)
                if not first_use:
                    pool.wait_ge(slab_used, n - SPLIT_SLOTS + 1)
                nc.gpsimd.tensor_tensor(hi, raw[:, s, :], zero, ALU.add).then_inc(split_done, 1)
                pool.wait_ge(split_done, n * 2 + 1)
                nc.gpsimd.tensor_tensor(lo, raw[:, s, :], hi.bitcast(F32), ALU.subtract).then_inc(split_done, 1)

            pool.wait_ge(loaded, 32)
            for s in range(RAW_SLOTS):
                split_slab(s, 0, s < SPLIT_SLOTS)
            with pool.Fori(1, N_SLABS // RAW_SLOTS) as i:
                for s in range(RAW_SLOTS):
                    split_slab(s, i, False)
        @block.tensor
        def _(pe):
            slab, res, sq, hl = Count(), Count(), Count(), Count()
            items, outs, norms, added = Count(), Count(), Count(), Count()

            def open_slab():
                slab.add()
                pe.wait_ge(split_done, slab.now(times=2))
                return split[:, (slab.n - 1) % SPLIT_SLOTS]

            def open_acc(n):
                res.add()
                if res.n > ACC_BANKS or res.i is not None:
                    pe.wait_ge(acc_taken, res.now(back=ACC_BANKS))
                return ps[:, (res.n - 1) % ACC_BANKS, 0:n]

            def product(o, w, t, a, first, last):
                wh, wl = (w[:, j, t * P:(t + 1) * P] for j in range(2))
                nc.tensor.matmul(o, wh, a[0], start=first, stop=False)
                nc.tensor.matmul(o, wh, a[1], start=False, stop=False)
                return nc.tensor.matmul(o, wl, a[0], start=False, stop=last)

            def gemm(w, t0, K, act, g, closes):
                o = open_acc(g[1])
                for k in range(K):
                    mm = product(o, w, t0 + k, act(k, g), k == 0, k == K - 1)
                if closes:
                    mm.then_inc(slab_used, 1)
                else:
                    mm.then_inc(acc_ready, 1)

            def rotate(perm, rows, src, after):
                pe.wait_ge(acc_taken, after)
                o = open_acc(SEQ)
                nc.tensor.matmul(o[rows], col(perm, 0, P)[rows, rows], src, start=True, stop=True).then_inc(acc_ready, 1)

            def norm(segs, sums, first_bank=ACC_BANKS, heads=1):
                norms.add()
                if norms.n > 1:
                    pe.wait_ge(var_ready, norms.now(back=1))
                weight = col("ones") if heads == 1 else col("headsum", 0, P)[:, 0:P:DV]
                tiles = [[c0 + t * P for c0, n in groups for t in range(n // P)] for _, groups in segs]
                count, at = sum(map(len, tiles)), 0
                for j, ((K, _), columns) in enumerate(zip(segs, tiles)):
                    sq.add(K)
                    if K == 1:
                        pe.wait_ge(sq_ready, sq.now())
                    else:
                        added.add(K - 1)
                        pe.wait_ge(sq_summed, added.now())
                    for c in columns:
                        o = ps[:, NORM_BANK, at * heads:(at + 1) * heads]
                        at += 1
                        mm = nc.tensor.matmul(o, sums[j][:, c:c + P], weight, start=at == 1, stop=at == count)
                mm.then_inc(sums_ready, 1)
                pe.wait_ge(rstd_ready, norms.now())
                for j in range(at):
                    for h in range(heads):
                        n = P // heads
                        mm = nc.tensor.matmul(ps[h * n:(h + 1) * n, first_bank + j // QT, (j % QT) * P:(j % QT + 1) * P],
                                              rstd[:, j * heads + h:j * heads + h + 1].to_broadcast([P, n]),
                                              col("ident", 0, P), start=True, stop=True)
                mm.then_inc(rstd_spread, 1)

            def wait_hl(n):
                hl.add(n)
                pe.wait_ge(hl_ready, hl.now())

            def cols(t):
                return lambda k, g: (t[:, 0, k, g[0]:g[0] + g[1]], t[:, 1, k, g[0]:g[0] + g[1]])

            def own(t):
                return lambda k, g: (t[:, 0, k, 0:g[1]], t[:, 1, k, 0:g[1]])

            def lambdas():
                pe.wait_ge(loaded, 32)
                pe.wait_ge(v_lam, LAYERS)
                o = open_acc(2 * LAYERS)
                nc.tensor.matmul(o, col("ones", 0, P), lam_p[:, :, :].rearrange("p l j -> p (l j)"), start=True, stop=True)\
                    .then_inc(acc_ready, 1)

            def first_two(groups, act):
                ws = [open_slab() for _ in groups]
                accs = [[open_acc(g[1]) for g in gs] for gs in groups]
                for k in range(DC):
                    wait_hl(1)
                    for w, os, gs in zip(ws, accs, groups):
                        for o, g in zip(os, gs):
                            mm = product(o, w, k, act(k, g), k == 0, k == DC - 1)
                            if k == DC - 1:
                                mm.then_inc(slab_used if g == gs[-1] else acc_ready, 1)

            def project(events, weight, act, perm, rows, src, fresh=False):
                at, w = {}, None
                if fresh:
                    names = [events[0][1], next(n for _, n, _ in events if n != events[0][1])]
                    first = [[g for kind, n, g in events if kind == "gemm" and n == name] for name in names]
                    before = res.n
                    first_two(first, act(names[0]))
                    at = {names[0]: before + len(first[0]), names[1]: res.n}
                    events = events[sum(map(len, first)):]
                for kind, name, g in events:
                    if kind == "gemm":
                        t0, K, opens, closes, last = weight(name)
                        if opens and (name not in at):
                            w = open_slab()
                        gemm(w, t0, K, act(name), g, closes and g == last)
                        at[name] = res.n
                    elif kind == "idx":
                        index_logits(*name)
                    else:
                        rotate(perm(name), rows(name), src(name), at[name])

            def mla(l):
                norm([(DC, BOTH)], sumN)
                G = groups_of(l)
                project(lora_events(l), lambda name: (0, DC, True, True, (G if name[0] == "cq" else BOTH)[-1]),
                        lambda name: cols(h_hl), lambda name: "perm_a", lambda name: slice(0, P),
                        lambda name: kr[:, CTX:TOK], fresh=True)
                norm([(3, G), (2, BOTH)], sumN)
                wait_hl(5)

                def weight(name):
                    if name[0] == "q":
                        return (3 * (name[1] % 2), 3, name[1] % 2 == 0, name[1] % 2 == 1, G[-1])
                    return (2 * name[1], 2, name[1] == 0, name[1] == H_A // 2 - 1, BOTH[-1])

                project(up_events(l), weight, lambda name: cols(cq_hl if name[0] == "q" else ckv_hl),
                        lambda name: "perm_a", lambda name: slice(0, QK_A), lambda name: qA[0:QK_A, name[1], CTX:TOK])
                w = open_slab()
                for t in range(TOK // P):
                    o = open_acc(512)
                    for k in range(2):
                        mm = swapped(o, w, k * 512, 512, ckv_hl, k, t * P, k == 0, k == 1)
                    mm.then_inc(slab_used if t == TOK // P - 1 else acc_ready, 1)

            def swapped(o, w, c0, n, t, k, tok, first, last):
                a = [t[:, j, k, tok:tok + P] for j in range(2)]
                nc.tensor.matmul(o, a[0], w[:, 0, c0:c0 + n], start=first, stop=False)
                nc.tensor.matmul(o, a[0], w[:, 1, c0:c0 + n], start=False, stop=False)
                return nc.tensor.matmul(o, a[1], w[:, 0, c0:c0 + n], start=False, stop=last)

            def attend(n, scores, values):
                pe.wait_ge(acc_taken, res.now())

                def value(i):
                    pe.wait_ge(t_taken, items.now() + i + 1)
                    free = outs.now() + max(i - 1, 0)
                    if free:
                        pe.wait_ge(o_taken, free)
                    values(i, 6 + i % 2).then_inc(o_ready, 1)

                scores(0)
                for i in range(n):
                    if i + 1 < n:
                        scores(i + 1)
                    if i >= 1:
                        value(i - 1)
                    pe.wait_ge(p_normed, items.now() + i + 1)
                    transposes(i).then_inc(t_ready, 1)
                value(n - 1)
                items.add(n)
                outs.add(n)

            def transpose_tiles(p, nk):
                for t in range(nk // P):
                    mm = nc.tensor.transpose(ps[:, 4 + t // 4, (t % 4) * P:(t % 4 + 1) * P], p[:, t * P:(t + 1) * P],
                                             col("ident", 0, P))
                return mm

            def score_pieces(bank, lhsT, keys, nk):
                for c in range(0, nk, BANK):
                    n = min(BANK, nk - c)
                    mm = nc.tensor.matmul(ps[:, bank + c // BANK, 0:n], lhsT, keys(c, n), start=True, stop=True)
                mm.then_inc(s_ready, 1)

            def attn_a(l):
                nonlocal transposes
                its = items_a(l, H_A)
                wait_rot()

                def scores(i):
                    h, c, nk = its[i]
                    score_pieces(2 * (i % 2), qA[0:QK_A, h, c:c + P], lambda c0, n: kA[0:QK_A, h, c0:c0 + n], nk)

                def values(i, bank):
                    h, c, nk = its[i]
                    for t in range(nk // P):
                        mm = nc.tensor.matmul(ps[0:V_A, bank, 0:P], vA[:, t, h * V_A:(h + 1) * V_A],
                                              pT[:, t * P:(t + 1) * P], start=t == 0, stop=t == nk // P - 1)
                    return mm

                transposes = lambda i: transpose_tiles(pA[i % 2], its[i][2])
                attend(len(its), scores, values)

            def attn_b(l):
                nonlocal transposes
                its = items_a(l, H_B)
                wait_rot()

                def scores(i):
                    h, c, nk = its[i]
                    for j in range(2):
                        r = slice(64 * j, 64 * j + 64)
                        if i >= 1:
                            pe.wait_ge(p_ready, maps.now() + 2 * (i - 1) + j + 1)
                        score_pieces(2 * j, dq[r, h, c:c + P], lambda c0, n: dk[r, h, c0:c0 + n], nk)

                def values(i, bank):
                    h, c, nk = its[i]
                    for t in range(nk // P):
                        mm = nc.tensor.matmul(ps[:, bank, 0:P], vB[:, t, h * P:(h + 1) * P],
                                              pT[:, t * P:(t + 1) * P], start=t == 0, stop=t == nk // P - 1)
                    return mm

                transposes = lambda i: transpose_tiles(pB[i % 2], its[i][2])
                attend(len(its), scores, values)

            transposes = None
            maps = Count()
            rots = Count()

            def wait_rot():
                pe.wait_ge(rot_done, rots.now())

            def diff(l):
                project(diff_events(l), lambda name: (0, DC, True, True, (groups_of(l) if name[0] == "dq" else BOTH)[-1]),
                        lambda name: cols(h_hl), lambda name: "perm_b", lambda name: slice(0, P),
                        lambda name: (dq if name[0] == "dq" else dk)[:, name[1], CTX:TOK])
                token_major(h_hl, [t * P for t in range(TOK // P)], 512, 4)

            def token_major(t, tokens, n, slabs):
                pe.wait_ge(acc_taken, res.now())
                per = DC // slabs
                for s in range(slabs):
                    w = open_slab()
                    for j, tok in enumerate(tokens):
                        for k in range(per):
                            mm = swapped(ps[:, j, 0:n], w, k * n, n, t, s * per + k, tok, s == 0 and k == 0,
                                         s == slabs - 1 and k == per - 1)
                        if s == slabs - 1 and j < len(tokens) - 1:
                            mm.then_inc(acc_ready, 1)
                    mm.then_inc(slab_used, 1)
                res.add(len(tokens))
                pe.wait_ge(acc_taken, res.now())

            def mixed(l):
                G = groups_of(l)
                norm([(1, G)] * H_B, sumB, first_bank=0)
                wait_hl(4 + H_B)
                turns, per = (4, 2)
                with Loop(pe, turns, (slab, 3 * per), (res, 4 * len(G) * per)):
                    for _ in range(per):
                        for _ in range(2):
                            w = open_slab()
                            for g in G:
                                gemm(w, 0, DC, cols(h_hl), g, g == G[-1])
                        w = open_slab()
                        for g in G:
                            gemm(w, 0, 4, cols(oA_hl), g, False)
                        for g in G:
                            gemm(w, 4, 4, cols(oB_hl), g, g == G[-1])
                wait_hl(DC)
                per = 4 // len(G)
                with Loop(pe, DC // per, (slab, per), (res, 4)):
                    for _ in range(per):
                        w = open_slab()
                        for g in G:
                            gemm(w, 0, DC, cols(m_hl), g, g == G[-1])

            def ffn(n):
                norm([(DC, [(0, n)])], sumN)
                ffn_products(n)

            def ffn_products(n):
                first_two([[(0, n)]] * 2, own(h2))
                for _ in range(2):
                    gemm(open_slab(), 0, DC, own(h2), (0, n), True)
                with Loop(pe, FC // 2 - 1, (slab, 4), (res, 4)):
                    for _ in range(4):
                        gemm(open_slab(), 0, DC, own(h2), (0, n), True)
                wait_hl(FC)
                act = own(g_hl)
                with Loop(pe, 2, (slab, 12), (res, 4)):
                    for _ in range(4):
                        o = open_acc(n)
                        for k in range(FC):
                            if k % SLAB_TILES == 0:
                                w = open_slab()
                            mm = product(o, w, k % SLAB_TILES, act(k, (0, n)), k == 0, k == FC - 1)
                            if k % SLAB_TILES == SLAB_TILES - 1 or k == FC - 1:
                                mm.then_inc(slab_used, 1)

            def wide(k, g):
                c = 0 if g[0] == 0 else APART
                return gw_hl[:, 0, k, c:c + g[1]], gw_hl[:, 1, k, c:c + g[1]]

            def ffn_both():
                norm([(DC, BOTH)], sumN)
                for half in range(2):
                    if half == 0:
                        first_two([BOTH, BOTH], cols(h2w))
                    else:
                        for _ in range(2):
                            up_slab()
                    with Loop(pe, HALF // 2, (slab, 4), (res, 8)):
                        for _ in range(4):
                            up_slab()
                    wait_hl(HALF)
                    for m in range(DC):
                        os = [open_acc(g[1]) for g in BOTH]
                        for k in range(HALF):
                            t = m * HALF + k
                            if t % SLAB_TILES == 0:
                                w = open_slab()
                            for o, g in zip(os, BOTH):
                                mm = product(o, w, t % SLAB_TILES, wide(k, g), k == 0, k == HALF - 1)
                                if g == BOTH[-1] and t % SLAB_TILES == SLAB_TILES - 1:
                                    mm.then_inc(slab_used, 1)
                                elif k == HALF - 1:
                                    mm.then_inc(acc_ready, 1)

            def up_slab():
                w = open_slab()
                for g in BOTH:
                    gemm(w, 0, DC, cols(h2w), g, g == BOTH[-1])

            def in2(l):
                norm([(DC, [(0, SEQ)])], sumN)
                src = {"qa": qa, "ka": ka, "qi": qi}

                def projections(events, fresh=False):
                    project(events, lambda name: (0, DC, True, True, LAT[-1]), lambda name: own(h2),
                            lambda name: "perm_2", lambda name: slice(0, P),
                            lambda name: ki[:, :] if name == "ki" else src[name[0]][:, name[1], :], fresh=fresh)

                projections(IN2_INDEX, fresh=True)
                w = open_slab()
                for t in range(QT):
                    o = open_acc(IDX_HEADS)
                    for k in range(DC):
                        mm = swapped(o, w, k * P, IDX_HEADS, h2, k, t * P, k == 0, k == DC - 1)
                    mm.then_inc(slab_used if t == QT - 1 else acc_ready, 1)
                projections(IN2_PLAIN)
                token_major(h2, [t * P for t in range(QT)], 512, 4)
                token_major(h2, [t * P for t in range(QT)], 256, 2)
                o = open_acc(SEQ)
                nc.tensor.matmul(o, col(f"w_gate{l}", 0, P, slice(0, GATE_RANK)), gl[0:GATE_RANK, :],
                                 start=True, stop=True).then_inc(acc_ready, 1)
                projections(IN2_ROPED)
                rots.add(IN2_ROTS)

            def index_logits(t, h):
                nk = (t + 1) * P
                r = slice(64 * (h % 2), 64 * (h % 2) + 64)
                idx.add()
                pe.wait_ge(rot_done, rots.now() + INDEX_ROTS)
                if idx.n > IDX_HEADS:
                    pe.wait_ge(relu_ready, idx.now() - IDX_HEADS)
                nc.tensor.matmul(ps[:, ACC_BANKS + h, 0:nk], qi[r, h // 2, t * P:(t + 1) * P], ki[r, 0:nk],
                                 start=True, stop=True).then_inc(idx_ready, 1)

            heads_done, idx = Count(), Count()

            def gla(l):
                for c in range(2):
                    pe.wait_ge(pool_ready, l + 1)
                    o = open_acc(SEQ)
                    nc.tensor.matmul(o, col(f"w_pool{l}", c * P, P), tmp[c][:, :], start=True, stop=True).then_inc(acc_ready, 1)
                pe.wait_ge(acc_taken, res.now())
                pe.wait_ge(qk_ready, (l + 1) * 10)

                def products(h):
                    r = slice(DK * h, DK * h + DK)

                    def block_product(bank, c, lev, j, i0, ni):
                        return nc.tensor.matmul(ps[:, bank, c:c + ni], kd[r, lev, j * P:(j + 1) * P],
                                                qd[r, lev, i0:i0 + ni], start=True, stop=True)

                    block_product(0, 0, 1, 0, P, P)
                    block_product(0, P, 0, 0, 2 * P, 2 * P)
                    block_product(1, 0, 0, 1, 2 * P, 2 * P)
                    block_product(1, 2 * P, 1, 2, 3 * P, P)
                    for lev in range(2, len(HALVES)):
                        for j in range(QT):
                            mm = block_product(lev, j * P, lev, j, j * P, P)
                    mm.then_inc(att_ready, 1)

                products(0)
                for h in range(GLA_HEADS):
                    n = heads_done.now() + h + 1
                    if h + 1 < GLA_HEADS:
                        pe.wait_ge(att_off, 2 * n)
                        pe.wait_ge(att_read, n)
                        products(h + 1)
                    pe.wait_ge(att_off, 2 * n)
                    pe.wait_ge(att_masked, n)
                    pe.wait_ge(o_taken, outs.now(back=min(h, 1)))
                    o = ps[0:DV, 6 + h % 2, :]
                    for j in range(QT):
                        mm = nc.tensor.matmul(o[:, j * P:SEQ], vb[:, j, h * DV:(h + 1) * DV], attT[h % 2][:, j, j * P:SEQ],
                                              start=j == 0, stop=j == QT - 1)
                    mm.then_inc(o_ready, 1)
                    outs.add()
                heads_done.add(GLA_HEADS)
                norm([(1, [(0, SEQ)])] * 2, sumG, heads=2)

            def dsa(l):
                nonlocal transposes
                wait_rot()

                def scores(i):
                    h, t = ITEMS_2[i]
                    r = slice(64 * (h % 2), 64 * (h % 2) + 64)
                    n = maps.now() + i
                    if i >= 4:
                        pe.wait_ge(s_max, maps.now() + i - 3)
                    nc.tensor.matmul(ps[:, i % 4, 0:(t + 1) * P], qa[r, h // 2, t * P:(t + 1) * P],
                                     ka[r, h // 2, 0:(t + 1) * P], start=True, stop=True).then_inc(s_ready, 1)

                def values(i, bank):
                    h, t = ITEMS_2[i]
                    for j in range(t + 1):
                        mm = nc.tensor.matmul(ps[0:HD, bank, 0:P], va[:, j, h * HD:(h + 1) * HD],
                                              pT2[:, j * P:(j + 1) * P], start=j == 0, stop=j == t)
                    return mm

                transposes = lambda i: transpose_tiles(p2[i % 2], (ITEMS_2[i][1] + 1) * P)
                attend(len(ITEMS_2), scores, values)
                maps.add(len(ITEMS_2))

            def mixed2(l):
                wait_hl(DC)
                with Loop(pe, 2, (slab, 4), (res, 4)):
                    for _ in range(4):
                        gemm(open_slab(), 0, DC, own(mix_hl), (0, SEQ), True)

            for l in range(LAYERS):
                if l == 0:
                    lambdas()
                mla(l)
                rots.add(2 + H_A)
                attn_a(l)
                maps.add(len(items_a(l, H_A)))
                diff(l)
                rots.add(2 * H_B)
                attn_b(l)
                maps.add(2 * len(items_a(l, H_B)))
                mixed(l)
                ffn_both() if l == 0 else ffn(SEQ)
            norm([(DC, [(0, SEQ)])], sumN)
            for l in range(LAYERS):
                in2(l)
                gla(l)
                dsa(l)
                mixed2(l)
                ffn(SEQ)
            norm([(DC, [(0, SEQ)])], sumN)


        @block.scalar
        def _(act):
            res, acc, slab, sq, full = Count(), Count(), Count(), Count(), Count()
            norms, squared, rots, maps, items, outs = (Count() for _ in range(6))
            xs, merges, steps, idx = Count(4), Count(), Count(), Count()
            copy = ACT.Copy

            def take(n, closes, bank=None):
                res.add()
                if closes:
                    slab.add()
                    act.wait_ge(slab_used, slab.now())
                else:
                    acc.add()
                    act.wait_ge(acc_ready, acc.now())
                return ps[:, (res.n - 1) % ACC_BANKS if bank is None else bank, 0:n]

            def bring(dst, src, func=copy, **kw):
                nc.scalar.activation(dst, src, func, **kw).then_inc(acc_taken, 1)

            def step(ins):
                steps.add()
                ins.then_inc(a_step, 1)
                act.wait_ge(a_step, steps.now())

            def squares(src, chunks, groups, first, ring, ready=None):
                act.wait_ge(acc_taken, res.now())
                c = span(groups)
                for k in range(chunks):
                    if ready is not None:
                        act.wait_ge(x_ready, ready(k))
                    dst = first
                    if k:
                        squared.add()
                        dst = ring[squared.n % 2]
                        if squared.n > 2:
                            act.wait_ge(sq_summed, squared.now(back=2))
                    nc.scalar.activation(dst[:, c], src(k), ACT.Square).then_inc(sq_ready, 1)

            def roots(n):
                norms.add()
                act.wait_ge(var_ready, norms.now())
                nc.scalar.activation(rstd[:, 0:n], rstd[:, 0:n], ACT.Sqrt).then_inc(root_ready, 1)

            def highs(chunks, src, dst, groups, shift=None):
                for k in range(chunks):
                    full.add()
                    act.wait_ge(full_ready, full.now())
                    for g in groups:
                        c = slice(g[0], g[0] + g[1])
                        if shift is None:
                            ins = nc.scalar.activation(dst(k)[:, c], src(k)[:, c], copy)
                        else:
                            ins = nc.scalar.activation(dst(k)[:, c], src(k)[:, c], ACT.Identity, bias=shift(k, g))
                    ins.then_inc(hi_ready, 1)

            def span(groups):
                return slice(groups[0][0], groups[-1][0] + groups[-1][1])

            def silu_c(group):
                act.wait_ge(c_loaded, 16 * (group + 1))
                c = ada_c[group][:, :, :]
                nc.scalar.activation(c, c, ACT.Silu).then_inc(c_ready, 1)

            def lambdas():
                bring(lam_e[:, :, :].rearrange("p l j -> p (l j)"), take(2 * LAYERS, False), ACT.Exp)

            def evacuate(events, dst, closes, rows, rotbuf, rot_rows, j=0, beside=None):
                for kind, name, g in events:
                    if kind == "idx":
                        index_relu(*name)
                    elif kind == "gemm":
                        o = take(g[1], closes(name, g))
                        d = dst(name, g)
                        r = rows(name)
                        bring(d, o[r, :])
                    else:
                        o = take(SEQ, False)
                        if j >= 2:
                            act.wait_ge(rot_done, rots.now() + j - 1)
                        r = rot_rows(name)
                        bring(rotbuf[j % 2][r, :], o[r, :])
                        if beside is not None:
                            beside(j)
                        j += 1

            every = lambda name: slice(0, P)
            rope_rows = slice(NOPE, QK_A)

            def mla(l):
                G = groups_of(l)
                act.wait_ge(x_ready, xs.now())
                act.dma_start(ropeA[:, :, :], rope_tab[:, 0:2, :]).then_inc(rope_in, 16)
                squares(lambda k: x[:, k, :], DC, BOTH, sumN[0], sqN)
                roots(TOK // P)
                highs(DC, lambda k: unN[k % 2], lambda k: h_hl[:, 0, k, :], BOTH, lambda k, g: mod[:, l, k, which(g)])

                def dst(name, g):
                    c = slice(g[0], g[0] + g[1])
                    if name == "kr":
                        return kr[:, c]
                    return (cq if name[0] == "cq" else ckv)[:, name[1], c]

                evacuate(lora_events(l), dst, lambda name, g: g == LAT[0], every, rot, lambda name: rope_rows)
                squares(lambda k: cq[:, k, span(G)], 3, G, sumN[0], sqN)
                squares(lambda k: ckv[:, k, :], 2, BOTH, sumN[1], sqN)
                roots((span(G).stop - span(G).start + TOK) // P)
                highs(3, lambda k: unN[k % 2], lambda k: cq_hl[:, 0, k, :], [(span(G).start, span(G).stop - span(G).start)])
                highs(2, lambda k: unN[(k + 1) % 2], lambda k: ckv_hl[:, 0, k, :], [(0, TOK)])
                j = 1
                for kind, name, g in up_events(l):
                    if kind == "rot":
                        o = take(SEQ, False)
                        if j >= 2:
                            act.wait_ge(rot_done, rots.now() + j - 1)
                        bring(rot[j % 2][rope_rows, :], o[rope_rows, :])
                        j += 1
                        continue
                    c = slice(g[0], g[0] + g[1])
                    kind, m = name
                    if kind == "q":
                        o = take(g[1], m % 2 == 1 and g == LAT[0])
                        bring(qA[0:QK_A, m, c], o[0:QK_A, :])
                    else:
                        o = take(g[1], m == H_A // 2 - 1 and g == LAT[0])
                        nc.scalar.activation(kA[0:NOPE, 2 * m, c], o[0:NOPE, :], copy)
                        bring(kA[0:NOPE, 2 * m + 1, c], o[NOPE:P, :])
                rots.add(2 + H_A)
                act.wait_ge(rot_done, rots.now())
                for t in range(TOK // P):
                    bring(vA[:, t, :], take(512, t == TOK // P - 1))

            def attend(n, exps, transposed, pt):
                def taken(i):
                    act.wait_ge(t_ready, items.now() + i + 1)
                    nk = transposed(i)
                    nc.scalar.activation(pt[:, 0:nk], banks(4, nk), copy).then_inc(t_taken, 1)

                exps(0)
                for i in range(n):
                    if i + 1 < n:
                        exps(i + 1)
                    taken(i)
                items.add(n)

            def attn_a(l):
                its = items_a(l, H_A)

                def exps(i):
                    nk = its[i][2]
                    act.wait_ge(s_max, maps.now() + i + 1)
                    st = stat[:, i % 2, :]
                    nc.scalar.activation(pA[i % 2][:, 0:nk], banks(2 * (i % 2), nk), ACT.Exp, bias=st[:, 0:1],
                                         scale=QK_A ** -0.5, accum_out=st[:, 2:3]).then_inc(p_ready, 1)

                attend(len(its), exps, lambda i: its[i][2], pT)
                maps.add(len(its))

            def attn_b(l):
                its = items_a(l, H_B)

                def exps(i):
                    nk = its[i][2]
                    st = stat[:, i % 2, :]
                    for j in range(2):
                        act.wait_ge(s_max, maps.now() + 2 * i + j + 1)
                        nc.scalar.activation(pB[2 * j + i % 2][:, 0:nk], banks(2 * j, nk), ACT.Exp, bias=st[:, j:j + 1],
                                             scale=DH_B ** -0.5, accum_out=st[:, 2 + j:3 + j]).then_inc(p_ready, 1)

                attend(len(its), exps, lambda i: its[i][2], pT)
                maps.add(2 * len(its))
                outs.add(len(its))

            def diff(l):
                outs.add(len(items_a(l, H_A)))
                act.wait_ge(o_taken, outs.now())
                act.dma_start(ropeB[:, :, :], rope_tab[:, 2:4, :]).then_inc(rope_in, 16)
                for k in range(4):
                    nc.scalar.activation(oA_hl[:, 0, k, span(groups_of(l))], oA[:, k, span(groups_of(l))], copy)\
                        .then_inc(hi_ready, 1)
                if l == 0:
                    silu_c(1)
                evacuate(diff_events(l), lambda name, g: (dq if name[0] == "dq" else dk)[:, name[1], g[0]:g[0] + g[1]],
                         lambda name, g: g == LAT[0], every, rotB, every)
                rots.add(2 * H_B)
                token_major(TOK // P, 512, 4, lambda t: vB[:, t, :])

            def token_major(n, width, slabs, dst, **kw):
                slab.add(slabs - 1)
                for t in range(n):
                    bring(dst(t), take(width, t == n - 1, bank=t))

            def mixed(l):
                G = groups_of(l)
                c = span(G)
                act.wait_ge(o_taken, outs.now())
                if l == 0:
                    act.wait_ge(mod_ready, 2)
                for h in range(H_B):
                    squares(lambda k: oB[:, h, c], 1, G, sumB[h], None)
                roots(H_B * (c.stop - c.start) // P)
                highs(H_B, lambda k: unB[k % 2], lambda k: oB_hl[:, 0, k, :], [(c.start, c.stop - c.start)])
                merges.add(1)
                per = 2
                with Loop(act, 4, (slab, 3 * per), (res, 4 * len(G) * per), (acc, (4 * len(G) - 3) * per), (merges, per)):
                    for _ in range(per):
                        act.wait_ge(merge_done, merges.now())
                        for j, func in enumerate((ACT.Sigmoid, ACT.Sigmoid, copy, copy)):
                            for g in G:
                                bring(mg[:, j, g[0]:g[0] + g[1]], take(g[1], j != 2 and g == G[-1]), func)
                        merges.add(1)
                act.wait_ge(merge_done, merges.now())
                for k in range(DC):
                    nc.scalar.activation(m_hl[:, 0, k, c], merged[:, k, c], copy).then_inc(hi_ready, 1)
                per = 4 // len(G)
                with Loop(act, DC // per, (slab, per), (res, 4), (acc, per * (len(G) - 1)), (xs, 4)) as i:
                    for m in range(per):
                        for g in G:
                            residual_term(evo, g[1], g == G[-1], mod[:, l, bass.ds(i * per + (2 * DC + m), 1), which(g)])

            def which(g):
                return slice(0, 1) if g[0] == CTX else slice(1, 2)

            def residual_term(buf, n, closes, gate):
                xs.add()
                o = take(n, closes)
                act.wait_ge(x_ready, xs.now(back=4))
                dst = buf[(xs.n - 1) % 4][:, 0:n]
                if gate is None:
                    bring(dst, o)
                else:
                    bring(dst, o, ACT.Identity, scale=gate if len(gate.shape) == 2 else gate.rearrange("p a v -> p (a v)"))

            def ffn(l, n, c0, gate, off=1):
                act.wait_ge(x_ready, xs.now())
                squares(lambda k: x[:, k, c0:c0 + n], DC, [(0, n)], sumN[0], sqN)
                roots(n // P)
                shift = None if gate is None else (lambda k, g: mod[:, l, 3 * DC + k, gate])
                highs(DC, lambda k: unN[k % 2], lambda k: h2[:, 0, k, :], [(0, n)], shift)
                with Loop(act, FC // 2, (slab, 4), (res, 4), (full, 2), (convs, 2)) as i:
                    for j in range(2):
                        full.add()
                        convs.add()
                        act.wait_ge(full_ready, full.now(back=2))
                        bring(ua[j][:, off:n + off], take(n, True))
                        bring(ub[j][:, off:n + off], take(n, True))
                        act.wait_ge(conv_done, convs.now())
                        nc.scalar.activation(sa[:, 0:n], ca[:, 0:n], ACT.Silu).then_inc(silu_done, 1)
                        act.wait_ge(full_ready, full.now())
                        nc.scalar.activation(g_hl[:, 0, bass.ds(i * 2 + j, 1), 0:n].rearrange("p a n -> p (a n)"),
                                             cb[:, 0:n], copy).then_inc(hi_ready, 1)
                with Loop(act, 2, (slab, 12), (res, 4), (xs, 4)) as i:
                    for m in range(4):
                        slab.add(2)
                        residual_term(evd, n, True, None if gate is None else mod[:, l, bass.ds(i * 4 + (5 * DC + m), 1), gate])

            def ffn_both(l):
                act.wait_ge(x_ready, xs.now())
                squares(lambda k: x[:, k, :], DC, BOTH, sumN[0], sqN)
                roots(TOK // P)
                highs(DC, lambda k: unN[k % 2], lambda k: h2w[:, 0, k, :], BOTH, lambda k, g: mod[:, l, 3 * DC + k, which(g)])

                def tile(m, j):
                    full.add()
                    convs.add()
                    act.wait_ge(full_ready, full.now(back=2))
                    for u in (uaw[j], ubw[j]):
                        for g in BOTH:
                            c = 1 if g[0] == 0 else APART + 1
                            bring(u[:, c:c + g[1]], take(g[1], g == BOTH[-1]))
                    act.wait_ge(conv_done, convs.now())
                    nc.scalar.activation(saw[:, :], caw[:, :], ACT.Silu).then_inc(silu_done, 1)
                    act.wait_ge(full_ready, full.now())
                    dst = gw_hl[:, 0, m, :] if isinstance(m, int) else \
                        gw_hl[:, 0, bass.ds(m, 1), :].rearrange("p a n -> p (a n)")
                    nc.scalar.activation(dst, cbw[:, :], copy).then_inc(hi_ready, 1)

                for half in range(2):
                    act.wait_ge(x_ready, xs.now())
                    tile(0, 0)
                    with Loop(act, HALF // 2, (slab, 4), (res, 8), (acc, 4), (full, 2), (convs, 2)) as i:
                        for j in range(2):
                            tile(i * 2 + (1 + j), (1 + j) % 2)
                    silu_c(2 + half)
                    for m in range(DC):
                        for g in BOTH:
                            closes = m == DC - 1 and g == BOTH[-1]
                            if closes:
                                slab.add(BOTH_DOWN - 1)
                            residual_term(evw, g[1], closes, mod[:, l, 5 * DC + m, which(g)])

            convs = Count()

            def in2(l):
                act.wait_ge(x_ready, xs.now(back=0 if l else DC))
                act.dma_start(pos[:, :], pos_in).then_inc(rope_in, 16)
                act.dma_start(cnt[:, :, :], cnt_in).then_inc(rope_in, 16)
                squares(lambda k: x[:, k, CTX:TOK], DC, [(0, SEQ)], sumN[0], sqN,
                        ready=lambda k: xs.now(back=DC - 1 - k))
                roots(QT)
                highs(DC, lambda k: unN[k % 2], lambda k: h2[:, 0, k, :], [(0, SEQ)])
                for j, table in enumerate((sin2, cos2)):
                    act.wait_ge(ang_ready, 2 * l + j + 1)
                    nc.scalar.activation(table[:, :], table[:, :], ACT.Sin).then_inc(trig_ready, 1)
                dsts = {"qa": qa, "ka": ka, "qi": qi, "rb": rb}

                def dst(name, g):
                    if name[0] == "uc":
                        return uc[:, name[1], PAD:]
                    if name == "gl":
                        return gl[0:GATE_RANK, :]
                    if isinstance(name, str):
                        return {"ki": ki, "qb": qb, "kb": kb}[name][:, :]
                    return dsts[name[0]][:, name[1], :]

                def projections(events, j, beside=None):
                    evacuate(events, dst, lambda name, g: True,
                             lambda name: slice(0, GATE_RANK) if name == "gl" else slice(0, P), rot2, every, j, beside)

                projections(IN2_INDEX, 0)
                for t in range(QT):
                    bring(wi[:, t, :], take(IDX_HEADS, t == QT - 1), scale=IDX_SCALE)
                projections(IN2_PLAIN, 0)
                token_major(QT, 512, 4, lambda t: va[:, t, :])
                token_major(QT, 256, 2, lambda t: vb[:, t, :])
                z, t = tmp[2][:, :], tmp[3][:, :]
                bring(z, take(SEQ, False), ACT.Identity, bias=col(f"b_gate{l}"))
                act.wait_ge(acc_taken, res.now())
                step(nc.scalar.activation(t, z, ACT.Abs))
                step(nc.scalar.activation(t, t, ACT.Exp, scale=-1.0))
                nc.scalar.activation(t, t, ACT.Ln, bias=col("ones", 0)).then_inc(gate_ln, 1)
                projections(IN2_ROPED, INDEX_ROTS, beside=lambda j: decays(j - INDEX_ROTS - 2))
                rots.add(IN2_ROTS)

            def decays(lev):
                if 0 <= lev < len(HALVES):
                    for buf, sign in ((qd, 1.0), (kd, -1.0)):
                        levels.add()
                        act.wait_ge(lev_d, levels.now())
                        nc.scalar.activation(buf[:, lev, :], buf[:, lev, :], ACT.Exp, scale=sign / GATE_TAU).then_inc(lev_e, 1)

            def index_relu(t, h):
                nk = (t + 1) * P
                idx.add()
                act.wait_ge(idx_ready, idx.now())
                if idx.n > IDX_HEADS:
                    act.wait_ge(score_step, idx.now() - IDX_HEADS)
                nc.scalar.activation(relu[h][:, 0:nk], ps[:, ACC_BANKS + h, 0:nk], ACT.Relu).then_inc(relu_ready, 1)

            heads, levels = Count(), Count()

            def gla(l):
                for c in range(2):
                    bring(mix[:, 6 + c, :], take(SEQ, False), ACT.Identity, scale=col(f"pool_scale{l}", c))
                for h in range(GLA_HEADS):
                    heads.add()
                    act.wait_ge(att_ready, heads.now())
                    act.wait_ge(o_ready, outs.now() + max(h - 1, 0))
                    nc.scalar.activation(attT[h % 2][:, 0, P:SEQ], ps[:, 0, 0:3 * P], copy).then_inc(att_off, 1)
                    nc.scalar.activation(attT[h % 2][:, 1, 2 * P:SEQ], ps[:, 1, 0:2 * P], copy)
                    nc.scalar.activation(attT[h % 2][:, 2, 3 * P:SEQ], ps[:, 1, 2 * P:3 * P], copy).then_inc(att_off, 1)
                outs.add(GLA_HEADS)
                act.wait_ge(o_taken, outs.now())
                for k in range(2):
                    squares(lambda _: mix[:, 4 + k, :], 1, [(0, SEQ)], sumG[k], None)
                nc.scalar.activation(silu_r[:, :, :], rb[:, :, :], ACT.Silu).then_inc(silu_done, 1)
                roots(2 * 2 * QT)

            def dsa(l):
                def exps(i):
                    nk = (ITEMS_2[i][1] + 1) * P
                    act.wait_ge(s_max, maps.now() + i + 1)
                    st = stat[:, i % 2, :]
                    nc.scalar.activation(p2[i % 2][:, 0:nk], p2[i % 2][:, 0:nk], ACT.Exp, bias=st[:, 0:1],
                                         scale=HD ** -0.5, accum_out=st[:, 2:3]).then_inc(p_ready, 1)

                attend(len(ITEMS_2), exps, lambda i: (ITEMS_2[i][1] + 1) * P, pT2)
                maps.add(len(ITEMS_2))
                outs.add(len(ITEMS_2))

            def mixed2(l):
                act.wait_ge(o_taken, outs.now())
                act.wait_ge(acc_taken, res.now())
                for k in range(DC):
                    nc.scalar.activation(mix_hl[:, 0, k, :], mix[:, k, :], copy).then_inc(hi_ready, 1)
                with Loop(act, 2, (slab, 4), (res, 4), (xs, 4)):
                    for m in range(4):
                        residual_term(evo2, SEQ, True, None)

            def normed_in_place():
                act.wait_ge(x_ready, xs.now())
                squares(lambda k: x[:, k, CTX:TOK], DC, [(0, SEQ)], sumN[0], sqN)
                roots(QT)

            for l in range(LAYERS):
                if l == 0:
                    silu_c(0)
                    lambdas()
                mla(l)
                attn_a(l)
                diff(l)
                attn_b(l)
                mixed(l)
                ffn_both(l) if l == 0 else ffn(l, SEQ, CTX, slice(0, 1))
            normed_in_place()
            xs.add(DC)
            for l in range(LAYERS):
                in2(l)
                gla(l)
                dsa(l)
                mixed2(l)
                ffn(l, SEQ, CTX, None, off=2)
            normed_in_place()

        @block.vector
        def _(dve):
            res, vs, sqs, norms, his, added, ada = (Count() for _ in range(7))
            items, outs, maps, silus, merges = Count(), Count(), Count(), Count(), Count()
            idx, heads, levels, measured, tables = Count(), Count(), Count(), Count(), Count()
            rots = Count()

            def v(ins):
                vs.add()
                ins.then_inc(v_step, 1)
                dve.wait_ge(v_step, vs.now())

            def span(groups):
                return slice(groups[0][0], groups[-1][0] + groups[-1][1])

            def inverse(segs, sums, ring, heads=1):
                for j, (K, groups, _) in enumerate(segs):
                    sqs.add()
                    c = span(groups)
                    for _ in range(1, K):
                        sqs.add()
                        added.add()
                        dve.wait_ge(sq_ready, sqs.now())
                        nc.vector.tensor_tensor(sums[j][:, c], sums[j][:, c], ring[added.n % 2][:, c], ALU.add)\
                            .then_inc(sq_summed, 1)
                        dve.wait_ge(sq_summed, added.now())
                norms.add()
                dve.wait_ge(sums_ready, norms.now())
                at = 0
                for _, groups, n_feat in segs:
                    tiles = sum(n for _, n in groups) // P
                    n = tiles * heads
                    v(nc.vector.tensor_scalar(ms[:, at:at + n], ps[:, NORM_BANK, at:at + n], 1.0 / n_feat, EPS,
                                              ALU.mult, ALU.add))
                    at += n
                r, t = rstd[:, 0:at], newton[:, 0:at]
                nc.vector.reciprocal(r, ms[:, 0:at]).then_inc(var_ready, 1)
                dve.wait_ge(root_ready, norms.now())
                v(nc.vector.tensor_tensor(t, r, r, ALU.mult))
                v(nc.vector.tensor_tensor(t, t, ms[:, 0:at], ALU.mult))
                v(nc.vector.tensor_scalar(t, t, -0.5, 1.5, ALU.mult, ALU.add))
                nc.vector.tensor_tensor(r, r, t, ALU.mult).then_inc(rstd_ready, 1)
                dve.wait_ge(rstd_spread, norms.now())

            def spread(first_bank, tile, n):
                c = first_bank * BANK + tile * P
                return ps[:, :, :].rearrange("p b n -> p (b n)")[:, c:c + n]

            def low(src, dst, shift=None):
                dve.wait_ge(hi_ready, his.add().now())
                if shift is None:
                    ins = nc.vector.tensor_tensor(dst[1], src, dst[0].bitcast(F32), ALU.subtract)
                else:
                    for c, value in shift:
                        ins = nc.vector.scalar_tensor_tensor(dst[1][:, c], src[:, c], value, dst[0][:, c].bitcast(F32),
                                                             ALU.add, ALU.subtract)
                ins.then_inc(hl_ready, 1)

            def norm(segs, sums, ring, un, first_bank=ACC_BANKS):
                inverse([seg[0:3] for seg in segs], sums, ring)
                at, j, last = 0, 0, None
                for K, groups, _, src, gains, shift, dst in segs:
                    c = span(groups)
                    for k in range(K):
                        u = un[j % 2]
                        if his.n:
                            dve.wait_ge(hl_ready, his.now())
                        for g in groups:
                            cg = slice(g[0], g[0] + g[1])
                            ins = nc.vector.scalar_tensor_tensor(u[:, cg], src(k, cg), gains(k, g),
                                                                 spread(first_bank, at + (g[0] - c.start) // P, g[1]),
                                                                 ALU.mult, ALU.mult)
                        ins.then_inc(full_ready, 1)
                        if last is not None:
                            low(*last)
                        shifts = None if shift is None else [
                            (slice(g[0] - c.start, g[0] - c.start + g[1]), shift(k, g)) for g in groups]
                        last = (u[:, c], dst(k, c), shifts)
                        j += 1
                    at += (c.stop - c.start) // P
                low(*last)

            def normed_in_place(signal):
                inverse([(DC, [(0, SEQ)], D)], sumN, sqN)
                g = "g_final" if signal is x_ready else "final_g"
                for k in range(DC):
                    xk = x[:, k, CTX:TOK]
                    nc.vector.scalar_tensor_tensor(xk, xk, col(g, k), spread(ACC_BANKS, 0, SEQ), ALU.mult, ALU.mult)\
                        .then_inc(signal, 1)

            def pair(t):
                return lambda k, c: (t[:, 0, k, c], t[:, 1, k, c])

            def lat_col(g):
                return slice(0, 1) if g[0] == CTX else slice(1, 2)

            def ada_tiles(group, first, n):
                slots = ADA_SLOTS[group]
                for t in range(first, first + n):
                    l, m = ADA_GROUPS[group][t]
                    w = ada_t[group][t % slots][:, :]
                    dve.wait_ge(ada_ready[t % slots], 16 * (ada_loads(group, t % slots) + t // slots + 1))
                    if ada.n:
                        dve.wait_ge(ada_used, ada.now())
                    count = ADA_VECTORS[group]
                    for j in range(count):
                        ins = nc.vector.tensor_tensor_reduce(
                            out=ps[:, 6:8, :].rearrange("p b n -> p (b n)"), in0=w, in1=ada_c[group][:, j, :], scale=1.0,
                            scalar=0.0, op0=ALU.mult, op1=ALU.add, accum_out=mod[:, l, m, j:j + 1])
                        if j < count - 1:
                            v(ins)
                    ins.then_inc(ada_used, 1)
                    ada.add()

            def add_bias(group):
                dve.wait_ge(ada_used, ada.now())
                (l, m), n = ADA_GROUPS[group][0], len(ADA_GROUPS[group])
                tiles = mod[:, l, m:m + n, :]
                nc.vector.tensor_tensor(tiles, tiles, col(f"b_ada{l}", m, n).unsqueeze(2).to_broadcast([P, n, 2]), ALU.add)\
                    .then_inc(mod_ready, 1)
                dve.wait_ge(mod_ready, group + 1)

            def free_place():
                dve.wait_ge(hl_ready, his.now())
                nc.vector.memset(stat[:, 0, 7:8], 0.0).then_inc(ada_space, 1)

            def start():
                nc.vector.memset(mod[:, LAYERS - 1, :, :], 0.0)
                dve.wait_ge(c_ready, 1)
                ada_tiles(0, 0, len(ADA_GROUPS[0]))
                dve.wait_ge(loaded, 32)
                add_bias(0)
                for j in range(4):
                    nc.vector.memset(stat[:, 0, 4 + j:5 + j], 0.0).then_inc(x_ready, 1)
                for l in range(LAYERS):
                    nc.vector.tensor_tensor(lam_p[:, l, :], col(f"lam{l}", 0, 2), col(f"lam{l}", 2, 2), ALU.mult)\
                        .then_inc(v_lam, 1)
                res.add()
                dve.wait_ge(acc_taken, res.now())
                for l in range(LAYERS):
                    v(nc.vector.scalar_tensor_tensor(neg_lam[:, l:l + 1], lam_e[:, l, 1:2], -lam_init(l), lam_e[:, l, 0:1],
                                                     ALU.add, ALU.subtract))

            def gains_of(l, j):
                m = DC * (1 + 3 * j)
                name = ("g_mix", "g_ffn")[j]
                v(nc.vector.scalar_tensor_tensor(gain[:, j, :, :], mod[:, l, m:m + DC, :], 1.0,
                                                 col(f"{name}{l}", 0, 2 * DC).rearrange("p (k v) -> p k v", v=2),
                                                 ALU.add, ALU.mult))

            def rope(dst, rotated, cos, sin):
                v(nc.vector.tensor_tensor(rotated, rotated, sin, ALU.mult))
                v(nc.vector.tensor_tensor(dst, dst, cos, ALU.mult))
                return nc.vector.tensor_tensor(dst, dst, rotated, ALU.add)

            def rope_results(events, dst, rows, rotbuf, table, j=0, beside=None):
                for kind, name, g in events:
                    res.add()
                    if kind == "rot":
                        dve.wait_ge(acc_taken, res.now())
                        r = rows(name)
                        rope(dst(name), rotbuf[j % 2][r, :], table[0][r, :], table[1][r, :]).then_inc(rot_done, 1)
                        if beside is not None:
                            beside(j)
                        j += 1

            rope_rows = slice(NOPE, QK_A)

            def mla(l):
                G = groups_of(l)
                gains_of(l, 0)
                norm([(DC, BOTH, D, lambda k, c: x[:, k, c], lambda k, g: gain[:, 0, k, lat_col(g)],
                       lambda k, g: mod[:, l, k, lat_col(g)], pair(h_hl))], sumN, sqN, unN)
                tables.add(16)
                dve.wait_ge(rope_in, tables.now())
                tab = (ropeA[:, 0, :], ropeA[:, 1, :])
                rope_results(lora_events(l), lambda name: kr[rope_rows, CTX:TOK], lambda name: rope_rows, rot, tab)
                norm([(3, G, Q_LORA, lambda k, c: cq[:, k, c], lambda k, g: col(f"g_q{l}", k), None, pair(cq_hl)),
                      (2, BOTH, KV_LORA, lambda k, c: ckv[:, k, c], lambda k, g: col(f"g_kv{l}", k), None, pair(ckv_hl))],
                     sumN, sqN, unN)
                rope_results([e for e in up_events(l) if e[1][0] == "q"], lambda name: qA[rope_rows, name[1], CTX:TOK],
                             lambda name: rope_rows, rot, tab, j=1)
                dve.wait_ge(rot_done, rots.now() + 1 + H_A)
                nc.vector.tensor_copy(kA[rope_rows, :, :], kr[rope_rows, :].unsqueeze(1).to_broadcast([ROPE_A, H_A, TOK]))\
                    .then_inc(rot_done, 1)
                rots.add(2 + H_A)
                res.add(H_A // 2 * 2 + TOK // P)

            def attend(n, maxima, normalise, output):
                def out_tile(i):
                    outs.add()
                    dve.wait_ge(o_ready, outs.now())
                    output(i, 6 + i % 2).then_inc(o_taken, 1)

                maxima(0)
                for i in range(n):
                    normalise(i)
                    if i + 1 < n:
                        maxima(i + 1)
                    if i >= 1:
                        out_tile(i - 1)
                out_tile(n - 1)

            def row_max(n, bank, nk, scale, st, j=0):
                dve.wait_ge(s_ready, n)
                v(nc.vector.reduce_max(st[:, 6 + j:7 + j], banks(bank, nk), AX.X))
                nc.vector.tensor_scalar(st[:, j:j + 1], st[:, 6 + j:7 + j], -scale, None, ALU.mult).then_inc(s_max, 1)

            def attn_a(l):
                its = items_a(l, H_A)

                def maxima(i):
                    row_max(maps.now() + i + 1, 2 * (i % 2), its[i][2], QK_A ** -0.5, stat[:, i % 2, :])

                def normalise(i):
                    st, p = stat[:, i % 2, :], pA[i % 2][:, 0:its[i][2]]
                    dve.wait_ge(p_ready, maps.now() + i + 1)
                    v(nc.vector.reciprocal(st[:, 4:5], st[:, 2:3]))
                    nc.vector.tensor_scalar(p, p, st[:, 4:5], None, ALU.mult).then_inc(p_normed, 1)

                def output(i, bank):
                    h, c, _ = its[i]
                    r = (h % 2) * V_A
                    return nc.vector.tensor_copy(oA[r:r + V_A, h // 2, c:c + P], ps[0:V_A, bank, 0:P])

                attend(len(its), maxima, normalise, output)
                maps.add(len(its))

            def attn_b(l):
                its = items_a(l, H_B)

                def maxima(i):
                    for j in range(2):
                        row_max(maps.now() + 2 * i + j + 1, 2 * j, its[i][2], DH_B ** -0.5, stat[:, i % 2, :], j)

                def normalise(i):
                    nk, st = its[i][2], stat[:, i % 2, :]
                    p1, q1 = pB[i % 2][:, 0:nk], pB[2 + i % 2][:, 0:nk]
                    dve.wait_ge(p_ready, maps.now() + 2 * i + 2)
                    v(nc.vector.reciprocal(st[:, 4:6], st[:, 2:4]))
                    v(nc.vector.tensor_scalar(st[:, 5:6], st[:, 5:6], neg_lam[:, l:l + 1], None, ALU.mult))
                    v(nc.vector.tensor_scalar(p1, p1, st[:, 4:5], None, ALU.mult))
                    nc.vector.scalar_tensor_tensor(p1, q1, st[:, 5:6], p1, ALU.mult, ALU.add).then_inc(p_normed, 1)

                def output(i, bank):
                    h, c, _ = its[i]
                    return nc.vector.tensor_copy(oB[:, h, c:c + P], ps[:, bank, 0:P])

                attend(len(its), maxima, normalise, output)
                maps.add(2 * len(its))

            def diff(l):
                c = span(groups_of(l))
                for k in range(4):
                    low(oA[:, k, c], pair(oA_hl)(k, c))
                if l == 0:
                    free_place()
                    dve.wait_ge(c_ready, 2)
                tables.add(16)
                dve.wait_ge(rope_in, tables.now())
                some = len(ADA_GROUPS[1]) // (2 * H_B + 2)
                rope_results(diff_events(l), lambda name: (dq if name[0] == "dq" else dk)[:, name[1], CTX:TOK],
                             lambda name: slice(0, P), rotB, (ropeB[:, 0, :], ropeB[:, 1, :]),
                             beside=(lambda j: ada_tiles(1, j * some, some)) if l == 0 else None)
                if l == 0:
                    ada_tiles(1, 2 * H_B * some, len(ADA_GROUPS[1]) - 2 * H_B * some)
                    add_bias(1)
                rots.add(2 * H_B)
                res.add(TOK // P)

            def mixed(l):
                G = groups_of(l)
                c = span(G)
                v(nc.vector.tensor_scalar(gsub[:, :], col(f"g_sub{l}"), 1.0 - lam_init(l), None, ALU.mult))
                def head(h):
                    return (1, G, 2 * DH_B, lambda k, cg: oB[:, h, cg], lambda k, g: gsub[:, :], None,
                            lambda k, cg: pair(oB_hl)(h, cg))

                norm([head(h) for h in range(H_B)], sumB, None, unB, first_bank=0)
                nc.vector.memset(stat[:, 0, 5:6], 0.0).then_inc(merge_done, 1)
                merges.add(1)
                per = 2
                with Loop(dve, 4, (res, 4 * len(G) * per), (vs, 2 * per), (merges, per)) as i:
                    for m in range(per):
                        res.add(4 * len(G))
                        dve.wait_ge(acc_taken, res.now())
                        v(nc.vector.tensor_tensor(mg[:, 2, c], mg[:, 0, c], mg[:, 2, c], ALU.mult))
                        v(nc.vector.tensor_tensor(mg[:, 3, c], mg[:, 1, c], mg[:, 3, c], ALU.mult))
                        nc.vector.tensor_tensor(merged[:, bass.ds(i * per + m, 1), c].rearrange("p a n -> p (a n)"),
                                                mg[:, 2, c], mg[:, 3, c], ALU.add).then_inc(merge_done, 1)
                        merges.add(1)
                for k in range(DC):
                    low(merged[:, k, c], pair(m_hl)(k, c))
                per = 4 // len(G)
                with Loop(dve, DC // per, (res, 4)) as i:
                    for m in range(per):
                        for j, g in enumerate(G):
                            residual(evo[m * len(G) + j], g, i * per + m)

            def residual(buf, g, m):
                res.add()
                dve.wait_ge(acc_taken, res.now())
                if isinstance(m, int):
                    xm = x[:, m, g[0]:g[0] + g[1]]
                else:
                    xm = x[:, bass.ds(m, 1), g[0]:g[0] + g[1]].rearrange("p a n -> p (a n)")
                nc.vector.tensor_tensor(xm, xm, buf[:, 0:g[1]], ALU.add).then_inc(x_ready, 1)

            def conv(dst, u, n, w, b, taps, m):
                at = lambda c: par[:, c + m:c + m + 1] if isinstance(m, int) else par[:, bass.ds(m + c, 1)]
                wc = lambda t: at(w + t * taps)
                v(nc.vector.tensor_scalar(dst[:, 0:n], u[:, 0:n], wc(0), at(b), ALU.mult, ALU.add))
                v(nc.vector.scalar_tensor_tensor(dst[:, 0:n], u[:, 1:n + 1], wc(1), dst[:, 0:n], ALU.mult, ALU.add))
                return nc.vector.scalar_tensor_tensor(dst[:, 0:n], u[:, 2:n + 2], wc(2), dst[:, 0:n], ALU.mult, ALU.add)

            def ffn(l, n, c0, second):
                if second:
                    gains, shift = (lambda k, g: col(f"norm2{l}", k)), None
                else:
                    j = slice(0, 1) if c0 == CTX else slice(1, 2)
                    gains_of(l, 1)
                    gains, shift = (lambda k, g: gain[:, 1, k, j]), (lambda k, g: mod[:, l, 3 * DC + k, j])
                norm([(DC, [(0, n)], D, lambda k, c: x[:, k, c0:c0 + n], gains, shift, pair(h2))], sumN, sqN, unN)
                for t in ua + ub:
                    pads = t[:, 0:2] if second else t[:, 0:n + 2:n + 1]
                    v(nc.vector.memset(pads, 0.0))
                w, b = COLS[f"conv_w_2{l}" if second else f"conv_w{l}"][0], COLS[f"conv_b_2{l}" if second else f"conv_b{l}"][0]
                taps = FC if second else 2 * FC
                with Loop(dve, FC // 2, (res, 4), (vs, 4 if second else 10), (silus, 2), (his, 2)) as i:
                    for j in range(2):
                        m = i * 2 + j
                        res.add()
                        dve.wait_ge(acc_taken, res.now())
                        conv(ca, ua[j], n, w, b, taps, m).then_inc(conv_done, 1)
                        res.add()
                        dve.wait_ge(acc_taken, res.now())
                        if second:
                            other = ub[j][:, 2:n + 2]
                        else:
                            v(conv(cb, ub[j], n, w + FC, b + FC, taps, m))
                            other = cb[:, 0:n]
                        silus.add()
                        dve.wait_ge(silu_done, silus.now())
                        nc.vector.tensor_tensor(cb[:, 0:n], sa[:, 0:n], other, ALU.mult).then_inc(full_ready, 1)
                        low(cb[:, 0:n], [g_hl[:, p, bass.ds(m, 1), 0:n].rearrange("p a n -> p (a n)") for p in range(2)])
                with Loop(dve, 2, (res, 4)) as i:
                    for m in range(4):
                        residual(evd[m], (c0, n), i * 4 + m)

            def ffn_both(l):
                gains_of(l, 1)
                norm([(DC, BOTH, D, lambda k, c: x[:, k, c], lambda k, g: gain[:, 1, k, lat_col(g)],
                       lambda k, g: mod[:, l, 3 * DC + k, lat_col(g)], pair(h2w))], sumN, sqN, unN)
                w, b = COLS[f"conv_w{l}"][0], COLS[f"conv_b{l}"][0]

                def tile(m, j, chunk):
                    res.add(2)
                    dve.wait_ge(acc_taken, res.now())
                    conv(caw, uaw[j], WIDE, w, b, 2 * FC, m).then_inc(conv_done, 1)
                    res.add(2)
                    dve.wait_ge(acc_taken, res.now())
                    v(conv(cbw, ubw[j], WIDE, w + FC, b + FC, 2 * FC, m))
                    silus.add()
                    dve.wait_ge(silu_done, silus.now())
                    nc.vector.tensor_tensor(cbw[:, :], saw[:, :], cbw[:, :], ALU.mult).then_inc(full_ready, 1)
                    low(cbw[:, :], [gw_hl[:, p, bass.ds(chunk, 1), :].rearrange("p a n -> p (a n)")
                                    if not isinstance(chunk, int) else gw_hl[:, p, chunk, :] for p in range(2)])

                for half in range(2):
                    for t in uaw + ubw:
                        v(nc.vector.memset(t[:, 0:WIDE + 2:WIDE + 1], 0.0))
                        v(nc.vector.memset(t[:, CTX + 1:APART + 1], 0.0))
                    tile(half * HALF, 0, 0)
                    with Loop(dve, HALF // 2, (res, 8), (vs, 10), (silus, 2), (his, 2)) as i:
                        for j in range(2):
                            tile(i * 2 + (half * HALF + 1 + j), (1 + j) % 2, i * 2 + (1 + j))
                    group = 2 + half
                    free_place()
                    dve.wait_ge(c_ready, group + 1)
                    some = len(ADA_GROUPS[group]) // DC
                    for m in range(DC):
                        ada_tiles(group, m * some, some)
                        for j, g in enumerate(BOTH):
                            residual(evw[2 * (m % 2) + j], g, m)
                    add_bias(group)

            def angles():
                two_pi = 2 * math.pi
                big, c1 = 1.5 * 2.0 ** 23, 6.28125
                a, n, t = cos2[:, :], sin2[:, :], tmp[3][:, :]
                tables.add(32)
                dve.wait_ge(rope_in, tables.now())
                v(nc.vector.tensor_copy(a, pos[:, :]))
                v(nc.vector.tensor_scalar(a, a, col("inv_freq"), None, ALU.mult))
                v(nc.vector.tensor_scalar(n, a, 1.0 / two_pi, None, ALU.mult))
                v(nc.vector.tensor_scalar(n, n, big, None, ALU.add))
                v(nc.vector.tensor_scalar(n, n, -big, None, ALU.add))
                v(nc.vector.scalar_tensor_tensor(a, n, -c1, a, ALU.mult, ALU.add))
                v(nc.vector.scalar_tensor_tensor(a, n, -(two_pi - c1), a, ALU.mult, ALU.add))
                lim = 3.1415925
                nc.vector.tensor_scalar(n, a, lim, -lim, ALU.min, ALU.max).then_inc(ang_ready, 1)
                v(nc.vector.tensor_scalar(t, a, math.pi / 2, -two_pi, ALU.is_gt, ALU.mult))
                v(nc.vector.scalar_tensor_tensor(a, a, math.pi / 2, t, ALU.add, ALU.add))
                nc.vector.tensor_scalar(a, a, lim, -lim, ALU.min, ALU.max).then_inc(ang_ready, 1)

            def in2(l):
                norm([(DC, [(0, SEQ)], D, lambda k, c: x[:, k, CTX:TOK], lambda k, g: col(f"norm1{l}", k), None,
                       pair(h2))], sumN, sqN, unN)
                angles()
                v(nc.vector.memset(uc[:, :, 0:PAD], 0.0))
                dve.wait_ge(trig_ready, 2 * (l + 1))
                dsts = {"qa": qa, "ka": ka, "qi": qi}
                def ropes(events, j, beside=None):
                    rope_results(events, lambda name: ki[:, :] if name == "ki" else dsts[name[0]][:, name[1], :],
                                 lambda name: slice(0, P), rot2, (cos2, sin2), j, beside)

                def gate_beside(j):
                    lev = j - INDEX_ROTS - 1
                    if lev == -1:
                        gate_sums(l)
                    if 0 <= lev < len(HALVES):
                        distances(lev)
                    if 0 <= lev - 2 < len(HALVES):
                        decayed(lev - 2)

                ropes(IN2_INDEX, 0)
                res.add(QT)
                dve.wait_ge(acc_taken, res.now())
                best_keys()
                res.add(sum(kind == "gemm" for kind, *_ in IN2_PLAIN))
                dve.wait_ge(acc_taken, res.now())
                pool_windows()
                res.add(2 * QT + 1)
                ropes(IN2_ROPED, INDEX_ROTS, gate_beside)
                rots.add(IN2_ROTS)

            def pool_windows():
                for wbuf in win:
                    v(nc.vector.memset(wbuf[:, :, 0:PAD], 0.0))
                last = uc
                for wbuf, width in zip(win, POOL_WINDOWS):
                    back = width // 2
                    v(nc.vector.tensor_tensor(wbuf[:, :, PAD:], last[:, :, PAD:], last[:, :, PAD - back:PAD + SEQ - back],
                                              ALU.add))
                    last = wbuf
                for g, wbuf in enumerate(win):
                    r, c = slice(64 * (g % 2), 64 * (g % 2) + 64), g // 2
                    v(nc.vector.tensor_tensor(tmp[c][r, :], wbuf[r, c, PAD:], cnt[r, c, :], ALU.mult))
                v(nc.vector.tensor_tensor(tmp[0][:, :], tmp[0][:, :], uc[:, 0, PAD:], ALU.subtract))
                nc.vector.tensor_tensor(tmp[1][:, :], tmp[1][:, :], uc[:, 1, PAD:], ALU.subtract).then_inc(pool_ready, 1)
            def best_keys():
                tril, above = col("tril", 0, P), col("above", 0, P)
                v(nc.vector.tensor_copy(bias2[:, 0, 0:P], above))
                for t in range(1, QT):
                    nk = (t + 1) * P
                    diag = slice(t * P, nk)
                    for h in range(IDX_HEADS):
                        idx.add()
                        dve.wait_ge(relu_ready, idx.now())
                        r = relu[h][:, 0:nk]
                        if h == 0:
                            ins = nc.vector.tensor_scalar(score[:, 0:nk], r, wi[:, t, 0:1], None, ALU.mult)
                        else:
                            ins = nc.vector.scalar_tensor_tensor(score[:, 0:nk], r, wi[:, t, h:h + 1], score[:, 0:nk],
                                                                 ALU.mult, ALU.add)
                        ins.then_inc(score_step, 1)
                        dve.wait_ge(score_step, idx.now())
                    v(nc.vector.tensor_tensor(score[:, diag], score[:, diag], tril, ALU.mult))
                    v(nc.vector.tensor_tensor(score[:, diag], score[:, diag], above, ALU.add))
                    src = score
                    for _ in range(TOPK // 8):
                        v(nc.vector.max(top8[:, :], src[:, 0:nk]))
                        v(nc.vector.match_replace(work[:, 0:nk], top8[:, :], src[:, 0:nk], TAKEN))
                        src = work
                    b = bias2[:, t, 0:nk]
                    v(nc.vector.tensor_scalar(b, work[:, 0:nk], TAKEN, -NEG, ALU.is_equal, ALU.mult))
                    v(nc.vector.tensor_scalar(b, b, NEG, None, ALU.add))
                    v(nc.vector.tensor_tensor(bias2[:, t, diag], bias2[:, t, diag], above, ALU.add))

            def gate_sums(l):
                z = tmp[2][:, :]
                v(nc.vector.memset(ones2[:, :], 1.0))
                dve.wait_ge(gate_ln, l + 1)
                v(nc.vector.scalar_tensor_tensor(z, z, 0.0, tmp[3][:, :], ALU.min, ALU.subtract))
                v(nc.vector.tensor_tensor_scan(gcum[:, :], ones2[:, :], z, 0.0, ALU.mult, ALU.add))

            def distances(lev):
                z, half = tmp[2][:, :], HALVES[lev]
                b = 2 * half
                view = lambda t: t.rearrange("p (n b) -> p n b", b=b)
                cum = view(gcum[:, :])
                if lev:
                    dve.wait_ge(lev_d, measured.now())
                v(nc.vector.tensor_tensor(view(z), cum, cum[:, :, half - 1:half].to_broadcast([P, SEQ // b, b]),
                                          ALU.subtract))
                limit = 0.0 if lev < len(HALVES) - 1 else -NEG
                nc.vector.tensor_scalar(qd[:, lev, :], z, limit, None, ALU.min).then_inc(lev_d, 1)
                nc.vector.tensor_scalar(kd[:, lev, :], z, -limit, None, ALU.max).then_inc(lev_d, 1)
                measured.add(2)

            def decayed(lev):
                levels.add(2)
                dve.wait_ge(lev_e, levels.now())
                nc.vector.scalar_tensor_tensor(qd[:, lev, :], qb[:, :], DK ** -0.5, qd[:, lev, :], ALU.mult, ALU.mult)\
                    .then_inc(qk_ready, 1)
                nc.vector.tensor_tensor(kd[:, lev, :], kb[:, :], kd[:, lev, :], ALU.mult).then_inc(qk_ready, 1)

            def gla(l):
                res.add(2)
                t0, t1 = tmp[2], tmp[3]
                blocks = lambda t: t.rearrange("p (j i) -> p j i", i=P)

                def masked(dst, lev):
                    mask = col("gla_mask", (lev - 2) * P, P).unsqueeze(1).to_broadcast([P, QT, P])
                    return nc.vector.tensor_tensor(blocks(dst[:, :]), blocks(ps[:, lev, :]), mask, ALU.mult)

                def head_out(h):
                    outs.add()
                    dve.wait_ge(o_ready, outs.now())
                    r = (h % 2) * DV
                    nc.vector.tensor_copy(mix[r:r + DV, 4 + h // 2, :], ps[0:DV, 6 + h % 2, :]).then_inc(o_taken, 1)

                for h in range(GLA_HEADS):
                    if heads.n:
                        dve.wait_ge(att_masked, heads.now())
                    heads.add()
                    dve.wait_ge(att_ready, heads.now())
                    v(masked(t0, 2))
                    v(masked(t1, 3))
                    v(nc.vector.tensor_tensor(t0[:, :], t0[:, :], t1[:, :], ALU.add))
                    masked(t1, 4).then_inc(att_read, 1)
                    dve.wait_ge(att_read, heads.now())
                    for j in range(QT):
                        c = slice(j * P, (j + 1) * P)
                        ins = nc.vector.tensor_tensor(attT[h % 2][:, j, c], t0[:, c], t1[:, c], ALU.add)
                    ins.then_inc(att_masked, 1)
                    if h >= 1:
                        head_out(h - 1)
                head_out(GLA_HEADS - 1)
                inverse([(1, [(0, SEQ)], DV)] * 2, sumG, None, heads=2)
                silus.add()
                dve.wait_ge(silu_done, silus.now())
                for k in range(2):
                    v(nc.vector.scalar_tensor_tensor(unG[k][:, 0:SEQ], mix[:, 4 + k, :], col(f"gla_g{l}", k),
                                                     spread(ACC_BANKS, k * QT, SEQ), ALU.mult, ALU.mult))
                    v(nc.vector.tensor_tensor(mix[:, 4 + k, :], unG[k][:, 0:SEQ], silu_r[:, k, :], ALU.mult))

            def dsa(l):
                def maxima(i):
                    h, t = ITEMS_2[i]
                    nk, st = (t + 1) * P, stat[:, i % 2, :]
                    dve.wait_ge(s_ready, maps.now() + i + 1)
                    v(nc.vector.tensor_tensor_reduce(out=p2[i % 2][:, 0:nk], in0=ps[:, i % 4, 0:nk], in1=bias2[:, t, 0:nk],
                                                     scale=1.0, scalar=TAKEN, op0=ALU.add, op1=ALU.max,
                                                     accum_out=st[:, 6:7]))
                    nc.vector.tensor_scalar(st[:, 0:1], st[:, 6:7], -HD ** -0.5, None, ALU.mult).then_inc(s_max, 1)

                def normalise(i):
                    nk, st = (ITEMS_2[i][1] + 1) * P, stat[:, i % 2, :]
                    dve.wait_ge(p_ready, maps.now() + i + 1)
                    v(nc.vector.reciprocal(st[:, 4:5], st[:, 2:3]))
                    nc.vector.tensor_scalar(p2[i % 2][:, 0:nk], p2[i % 2][:, 0:nk], st[:, 4:5], None, ALU.mult)\
                        .then_inc(p_normed, 1)

                def output(i, bank):
                    h, t = ITEMS_2[i]
                    r = (h % 2) * HD
                    return nc.vector.tensor_copy(mix[r:r + HD, h // 2, t * P:(t + 1) * P], ps[0:HD, bank, 0:P])

                attend(len(ITEMS_2), maxima, normalise, output)
                maps.add(len(ITEMS_2))

            def mixed2(l):
                for k in range(DC):
                    low(mix[:, k, :], (mix_hl[:, 0, k, :], mix_hl[:, 1, k, :]))
                with Loop(dve, 2, (res, 4)) as i:
                    for m in range(4):
                        residual(evo2[m], (CTX, SEQ), i * 4 + m)

            for l in range(LAYERS):
                if l == 0:
                    start()
                mla(l)
                attn_a(l)
                diff(l)
                attn_b(l)
                mixed(l)
                ffn_both(l) if l == 0 else ffn(l, SEQ, CTX, False)
            normed_in_place(x_ready)
            for l in range(LAYERS):
                in2(l)
                gla(l)
                dsa(l)
                mixed2(l)
                ffn(l, SEQ, CTX, True)
            normed_in_place(final_ready)


def columns(v):
    return np.ascontiguousarray(v).reshape(-1, P).T


def swap_matrix(dims, q, per, offset=0):
    m = np.zeros((P, P), np.float32)
    for b in range(offset, P, per):
        for base in range(0, dims, 2 * q):
            for j in range(q):
                if b + base + q + j < P:
                    m[b + base + q + j, b + base + j] = -1.0
                    m[b + base + j, b + base + q + j] = 1.0
    return m


def axial_table(dims, per, offset):
    q = dims // 4
    freqs = (ROPE_BASE ** (-np.arange(q, dtype=np.float32) / q)).astype(np.float32)
    t = np.arange(SEQ)
    where = ((t // GRID_W).astype(np.float32), (t % GRID_W).astype(np.float32))
    tab = np.zeros((P, 2, SEQ), np.float32)
    tab[:, 0] = 1.0
    for b in range(offset, P, per):
        for d in range(dims):
            if b + d < P:
                ang = where[d // (2 * q)] * freqs[d % q]
                tab[b + d, 0], tab[b + d, 1] = np.cos(ang), np.sin(ang)
    return tab


def constants():
    c = {"ident": np.eye(P), "ones": np.ones((P, P)), "zero": np.zeros((P, 1))}
    i = np.arange(P)
    c["headsum"] = (i[:, None] // DV == i[None, :] // DV) * 1.0
    c["perm_a"] = swap_matrix(ROPE_A, ROPE_A // 4, P, NOPE)
    c["perm_b"] = swap_matrix(DH_B, DH_B // 4, DH_B)
    c["perm_2"] = swap_matrix(ROT, ROT // 2, HD)
    c["tril"] = (i[None, :] <= i[:, None]) * 1.0
    c["above"] = np.where(i[None, :] <= i[:, None], 0.0, NEG)
    j, q = i[:, None], i[None, :]
    masks = [(j // (2 * half) == q // (2 * half)) & (q % (2 * half) >= half) & (j % (2 * half) < half) for half in (64, 32)]
    masks.append((j // 32 == q // 32) & (j <= q))
    c["gla_mask"] = np.concatenate(masks, 1) * 1.0
    inv = (ROPE_THETA ** (-np.arange(0, ROT, 2, dtype=np.float32) / ROT)).astype(np.float32)
    f = np.zeros((P, 1), np.float32)
    for b in range(0, P, HD):
        f[b:b + ROT, 0] = np.tile(inv, 2)
    c["inv_freq"] = f
    return c


def pack_params(a):
    par = np.zeros((P, NCOLS), np.float32)

    def put(name, v):
        o, w = COLS[name]
        par[0:v.shape[0], o:o + w] = v

    twice = lambda v: np.repeat(columns(v), 2, axis=1)
    for l in range(LAYERS):
        put(f"b_ada{l}", columns(a["b_ada"][l]))
        put(f"g_mix{l}", twice(a["g_mix"][l]))
        put(f"g_ffn{l}", twice(a["g_ffn"][l]))
        put(f"conv_w{l}", columns(a["conv_w"][l]))
        put(f"conv_b{l}", columns(a["conv_b"][l]))
        put(f"g_q{l}", columns(a["g_q"][l]))
        put(f"g_kv{l}", columns(a["g_kv"][l]))
        put(f"g_sub{l}", columns(a["g_sub"][l]))
        put(f"lam{l}", np.stack([a[f"lam_{n}"][l] for n in ("q1", "q2", "k1", "k2")], 1))
        put(f"norm1{l}", columns(a["norm1_g_2"][l]))
        put(f"norm2{l}", columns(a["norm2_g_2"][l]))
        put(f"conv_w_2{l}", columns(a["conv_w_2"][l]))
        put(f"conv_b_2{l}", columns(a["conv_b_2"][l]))
        put(f"b_gate{l}", columns(a["b_gate_2"][l]))
        put(f"gla_g{l}", columns(a["gla_norm_g_2"][l]))
        put(f"pool_scale{l}", columns(a["pool_scale_2"][l]))
        put(f"w_gate{l}", a["w_gate_up_2"][l])
        wp = np.zeros((2, P, P), np.float32)
        for g in range(4):
            r = slice(64 * (g % 2), 64 * (g % 2) + 64)
            wp[g // 2, r, r] = a["w_pool_2"][l, g]
        put(f"w_pool{l}", wp.transpose(1, 0, 2).reshape(P, -1))
    put("g_final", columns(a["g_final"]))
    put("final_g", columns(a["final_norm_g_2"]))
    for name, v in constants().items():
        put(name, np.asarray(v, np.float32))
    return par


def weight_stream(a):
    stream = np.zeros((N_SLABS, P, SLAB_TILES, P), np.float32)
    at = [0]

    def slab(tiles):
        for j, t in enumerate(tiles):
            stream[at[0], :, j, 0:t.shape[1]] = t
        at[0] += 1

    def rows(w, cols):
        return [w[k * P:(k + 1) * P, cols] for k in range(w.shape[0] // P)]

    def span(c0, n=P):
        return slice(c0, c0 + n)

    def by_k(w, c0, n, slabs):
        per = DC // slabs
        for s in range(slabs):
            slab([w[k * P:(k + 1) * P, span(c0 + j * P)] for k in range(s * per, (s + 1) * per) for j in range(n // P)])

    def ffn(up, down):
        for m in range(FC):
            slab(rows(up, span(m * P)))
            slab(rows(up, span(F + m * P)))
        for m in range(DC):
            t = rows(down, span(m * P))
            for k in range(0, FC, SLAB_TILES):
                slab(t[k:k + SLAB_TILES])

    def ffn_halves(up, down):
        for half in range(2):
            for m in range(half * HALF, (half + 1) * HALF):
                slab(rows(up, span(m * P)))
                slab(rows(up, span(F + m * P)))
            part = down[half * HALF * P:(half + 1) * HALF * P]
            tiles = [t for m in range(DC) for t in rows(part, span(m * P))]
            for t in range(0, len(tiles), SLAB_TILES):
                slab(tiles[t:t + SLAB_TILES])

    for l in range(LAYERS):
        w = a["w_in"][l]
        for m in range((Q_LORA + KV_LORA) // P):
            slab(rows(w, span(m * P)))
        slab(rows(w, span(Q_LORA + KV_LORA - NOPE)))
        for h in range(0, H_A, 2):
            slab(rows(a["w_uq"][l], span(h * QK_A, QK_A)) + rows(a["w_uq"][l], span((h + 1) * QK_A, QK_A)))
        ukv = a["w_ukv"][l].reshape(KV_LORA, H_A, NOPE + V_A)
        kn = np.ascontiguousarray(ukv[:, :, 0:NOPE]).reshape(KV_LORA, -1)
        vv = np.ascontiguousarray(ukv[:, :, NOPE:]).reshape(KV_LORA, -1)
        slab([t for j in range(H_A // 2) for t in rows(kn, span(j * P))])
        slab([vv[k * P:(k + 1) * P, span(j * P)] for k in range(2) for j in range(4)])
        c0 = Q_LORA + KV_LORA + ROPE_A
        for m in range(2 * H_B):
            slab(rows(w, span(c0 + m * P)))
        by_k(w, c0 + 2 * H_B * P, H_B * P, 4)
        c0 += 3 * H_B * P
        for m in range(DC):
            slab(rows(w, span(c0 + m * P)))
            slab(rows(w, span(c0 + D + m * P)))
            slab(rows(a["w_br_a"][l], span(m * P)) + rows(a["w_br_b"][l], span(m * P)))
        for m in range(DC):
            slab(rows(a["w_out"][l], span(m * P)))
        if l == 0:
            ffn_halves(a["w_up"][l], a["w_down"][l])
        else:
            ffn(a["w_up"][l], a["w_down"][l])
    for l in range(LAYERS):
        w = a["w_in_2"][l]
        for m in range(2):
            slab(rows(w, span(1536 + m * P)))
        slab([np.concatenate([t, t], 1) for t in rows(w, span(1792, HD))])
        slab(rows(w, span(1856, IDX_HEADS)))
        for c0 in (1860, 1988, 2372, 2500, 2644, 2772):
            slab(rows(w, span(c0)))
        slab(rows(w, span(2628, GATE_RANK)))
        by_k(w, 1024, 512, 4)
        by_k(w, 2116, 256, 2)
        for m in range(8):
            slab(rows(w, span(m * P)))
        for m in range(DC):
            slab(rows(a["w_out_2"][l], span(m * P)))
        ffn(a["w_up_2"][l], a["w_down_2"][l])
    assert at[0] == USED_SLABS, (at[0], USED_SLABS)
    return stream.reshape(N_SLABS, P, SLAB)


def tokens_last(v):
    return np.ascontiguousarray(v.T.reshape(DC, P, -1).transpose(1, 0, 2))


def host_inputs(a):
    count = np.minimum(np.arange(SEQ)[None, :] + 1, np.array(POOL_WINDOWS)[:, None]).astype(np.float32)
    cnt = np.repeat(np.float32(1.0) / count, 64, axis=0).reshape(2, P, SEQ).transpose(1, 0, 2)
    return {
        "wstream": weight_stream(a),
        "ada_w": np.stack([a["w_ada"][l][:, m * P:(m + 1) * P].T for tiles in ADA_GROUPS for l, m in tiles]),
        "c_in": np.ascontiguousarray(np.broadcast_to(np.stack([a["c"][0], a["c_ctx"]]), (P, 2, D))),
        "params": pack_params(a),
        "x_in": tokens_last(np.concatenate([a["ctx"][0], a["x"][0]], 0)),
        "rope_tab": np.concatenate([axial_table(ROPE_A, P, NOPE), axial_table(DH_B, DH_B, 0)], 1),
        "pos_in": np.ascontiguousarray(np.broadcast_to(a["positions_2"], (P, SEQ))),
        "cnt_in": np.ascontiguousarray(cnt),
    }


def program(nc, arrays):
    args = [nc.dram_tensor(name, v.shape, mybir.dt.from_np(v.dtype), kind="ExternalInput").ap()
            for name, v in arrays.items()]
    out = nc.dram_tensor("out_0", (P, DC, SEQ), F32, kind="ExternalOutput").ap()
    build(nc, *args, out)


def kernel(**inputs):
    import concourse.bacc as bacc
    from concourse.bass_utils import run_bass_kernel_spmd

    nc = bacc.Bacc("TRN2", target_bir_lowering=False, num_devices=1)
    arrays = host_inputs({k: np.asarray(v) for k, v in inputs.items()})
    program(nc, arrays)
    r = run_bass_kernel_spmd(nc, [arrays], core_ids=[0])
    got = r.results[0]["out_0"]
    return np.ascontiguousarray(got.transpose(1, 0, 2).reshape(D, SEQ).T).reshape(1, SEQ, D)
```
